# Optimizing a Trainium2 kernel written in Bass

```python
import math
import jax, jax.numpy as jnp
from jax import lax
import numpy as np

D_MODEL = 2048
BATCH = 1
SEQ = 512
DEPTH = 1
DEC_BATCH = 8
DEC_SEQ = 8
PAST_LEN = 4096
PAGE_SIZE = 128

MIX_WIDTH = D_MODEL
GLA_WIDTH = MIX_WIDTH // 2
SSD_WIDTH = MIX_WIDTH - GLA_WIDTH
GLA_HEADS = 4
GLA_HEAD_V = GLA_WIDTH // GLA_HEADS
GLA_HEAD_K = GLA_HEAD_V // 2
GLA_KDIM = GLA_HEADS * GLA_HEAD_K
GLA_LOWRANK = 16
GLA_GATE_NORMALIZER = 16.0
SSD_HEADDIM = 64
SSD_HEADS = SSD_WIDTH // SSD_HEADDIM
SSD_STATE = 128
SSD_GROUPS = 2
SSD_HPG = SSD_HEADS // SSD_GROUPS
SSD_CONV = 4
SSD_CONV_CH = SSD_WIDTH + 2 * SSD_GROUPS * SSD_STATE
FFN_DIM = 5632
FFN_CONV = 3
CHUNK = 64
EPS = 1e-6

IN_SIZES = (GLA_KDIM, GLA_KDIM, GLA_WIDTH, GLA_WIDTH, GLA_LOWRANK,
            SSD_WIDTH, SSD_CONV_CH, SSD_HEADS)
IN_COLS = sum(IN_SIZES)

kernel_name = "hymba_gla_ssd_convffn_step"

def _rmsnorm(x, w):
    xf = x.astype(jnp.float32)
    y = xf * lax.rsqrt(jnp.mean(xf * xf, axis=-1, keepdims=True) + EPS)
    return (y * w.astype(jnp.float32)).astype(x.dtype)

def _causal_dwconv(x, buf, w, b):
    width = w.shape[0]
    L = x.shape[1]
    xp = jnp.concatenate([buf.astype(x.dtype), x], axis=1)
    out = b + sum(xp[:, j:j + L] * w[j] for j in range(width))
    return out, xp[:, xp.shape[1] - (width - 1):]

def _to_chunks(a, c):
    B, L = a.shape[:2]
    return jnp.moveaxis(a.reshape((B, L // c, c) + a.shape[2:]), 1, 0)

def _from_chunks(a):
    n, B, c = a.shape[:3]
    return jnp.moveaxis(a, 0, 1).reshape((B, n * c) + a.shape[3:])

def _gla_chunked(q, k, v, lg, s0):
    L = q.shape[1]
    c = math.gcd(L, CHUNK)
    causal = jnp.tril(jnp.ones((c, c), dtype=bool))[None, :, :, None, None]

    def step(S, inp):
        qc, kc, vc, gc = inp
        b = jnp.cumsum(gc, axis=1)
        o_inter = jnp.einsum('bthk,bhkv->bthv', qc * jnp.exp(b), S)
        diff = b[:, :, None] - b[:, None, :]
        dec = jnp.exp(jnp.where(causal, diff, -jnp.inf))
        att = jnp.einsum('bthk,btshk,bshk->bhts', qc, dec, kc)
        o_intra = jnp.einsum('bhts,bshv->bthv', att, vc)
        b_last = b[:, -1]
        k_dec = kc * jnp.exp(b_last[:, None] - b)
        S_new = jnp.exp(b_last)[..., None] * S + jnp.einsum('bshk,bshv->bhkv', k_dec, vc)
        return S_new, o_inter + o_intra

    S, o = lax.scan(step, s0, tuple(_to_chunks(a, c) for a in (q, k, v, lg)))
    return _from_chunks(o), S

def _ssd_chunked(x, dt, la, Bm, Cm, h0):
    L = x.shape[1]
    c = math.gcd(L, CHUNK)
    causal = jnp.tril(jnp.ones((c, c), dtype=bool))[None, :, :, None, None]

    def step(h, inp):
        xc, dtc, lac, bc, cc = inp
        cum = jnp.cumsum(lac, axis=1)
        y_inter = jnp.einsum('btgn,bghpn->btghp', cc, h) * jnp.exp(cum)[..., None]
        diff = cum[:, :, None] - cum[:, None, :]
        dec = jnp.exp(jnp.where(causal, diff, -jnp.inf))
        cb = jnp.einsum('btgn,bsgn->btsg', cc, bc)
        y_intra = jnp.einsum('btsg,btsgh,bsgh,bsghp->btghp', cb, dec, dtc, xc)
        last = cum[:, -1]
        wdec = jnp.exp(last[:, None] - cum) * dtc
        h_new = jnp.exp(last)[..., None, None] * h + jnp.einsum('bsgh,bsgn,bsghp->bghpn', wdec, bc, xc)
        return h_new, y_inter + y_intra

    h, y = lax.scan(step, h0, tuple(_to_chunks(a, c) for a in (x, dt, la, Bm, Cm)))
    return _from_chunks(y), h

def _mixer(xn, s_gla, s_ssd, s_conv, p):
    B, L, _ = xn.shape
    f32 = jnp.float32
    proj = xn @ p['w_in']
    split_pts = np.cumsum(IN_SIZES)[:-1].tolist()
    q, k, v, g, lr, z, xbc, dtr = jnp.split(proj, split_pts, axis=-1)

    q = q.reshape(B, L, GLA_HEADS, GLA_HEAD_K).astype(f32) * (GLA_HEAD_K ** -0.5)
    k = k.reshape(B, L, GLA_HEADS, GLA_HEAD_K).astype(f32)
    v = v.reshape(B, L, GLA_HEADS, GLA_HEAD_V).astype(f32)
    lg = jax.nn.log_sigmoid((lr @ p['gla_w_gate2'] + p['gla_b_gate']).astype(f32)) / GLA_GATE_NORMALIZER
    lg = lg.reshape(B, L, GLA_HEADS, GLA_HEAD_K)
    o, S = _gla_chunked(q, k, v, lg, s_gla.astype(f32))
    o = _rmsnorm(o, p['gla_norm']) * jax.nn.silu(g.reshape(B, L, GLA_HEADS, GLA_HEAD_V).astype(f32))
    o_gla = o.reshape(B, L, GLA_WIDTH)

    xbc, conv_new = _causal_dwconv(xbc, s_conv, p['ssd_conv_w'], p['ssd_conv_b'])
    xbc = jax.nn.silu(xbc)
    xs, Bm, Cm = jnp.split(xbc, [SSD_WIDTH, SSD_WIDTH + SSD_GROUPS * SSD_STATE], axis=-1)
    xs = xs.reshape(B, L, SSD_GROUPS, SSD_HPG, SSD_HEADDIM).astype(f32)
    Bm = Bm.reshape(B, L, SSD_GROUPS, SSD_STATE).astype(f32)
    Cm = Cm.reshape(B, L, SSD_GROUPS, SSD_STATE).astype(f32)
    dt = jax.nn.softplus(dtr.astype(f32) + p['ssd_dt_bias'].astype(f32)).reshape(B, L, SSD_GROUPS, SSD_HPG)
    A = -jnp.exp(p['ssd_A_log'].astype(f32)).reshape(SSD_GROUPS, SSD_HPG)
    h0 = s_ssd.astype(f32).reshape(B, SSD_GROUPS, SSD_HPG, SSD_HEADDIM, SSD_STATE)
    y, h = _ssd_chunked(xs, dt, dt * A, Bm, Cm, h0)
    y = y + p['ssd_D'].astype(f32).reshape(SSD_GROUPS, SSD_HPG)[..., None] * xs
    y = y.reshape(B, L, SSD_GROUPS, SSD_WIDTH // SSD_GROUPS) * jax.nn.silu(
        z.reshape(B, L, SSD_GROUPS, SSD_WIDTH // SSD_GROUPS).astype(f32))
    y = _rmsnorm(y, p['ssd_norm'].reshape(SSD_GROUPS, SSD_WIDTH // SSD_GROUPS)).reshape(B, L, SSD_WIDTH)

    mix = jnp.concatenate([o_gla, y], axis=-1).astype(xn.dtype) @ p['w_out']
    h = h.reshape(B, SSD_HEADS, SSD_HEADDIM, SSD_STATE)
    return mix, S.astype(xn.dtype), h.astype(xn.dtype), conv_new.astype(xn.dtype)

def _conv_ffn(xn, s_ffn, p):
    u = xn @ p['ffn_w_in']
    u, buf = _causal_dwconv(u, s_ffn, p['ffn_conv_w'], p['ffn_conv_b'])
    a, b = jnp.split(u, 2, axis=-1)
    return (jax.nn.silu(a) * b) @ p['ffn_w_out'], buf.astype(xn.dtype)

def _layer(x, s_gla, s_ssd, s_conv, s_ffn, p):
    xn = _rmsnorm(x, p['n_mix_pre'])
    mix, g_new, h_new, c_new = _mixer(xn, s_gla, s_ssd, s_conv, p)
    x = x + _rmsnorm(mix, p['n_mix_post'])
    xn = _rmsnorm(x, p['n_ffn_pre'])
    f, f_new = _conv_ffn(xn, s_ffn, p)
    x = x + _rmsnorm(f, p['n_ffn_post'])
    return x, g_new, h_new, c_new, f_new

def setup_inputs(seed: int = 0) -> dict:
    key = jax.random.key(seed)
    ks = jax.random.split(key, 26)
    nrm = jax.random.normal
    f32 = jnp.float32
    dt = jnp.exp(jax.random.uniform(ks[16], (DEPTH, SSD_HEADS), f32,
                                    minval=math.log(1e-3), maxval=math.log(1e-1)))
    return {
        'x_prompt': nrm(ks[0], (BATCH, SEQ, D_MODEL), f32),
        'x_sample': nrm(ks[1], (DEC_BATCH, DEC_SEQ, D_MODEL), f32),
        'state_gla': 0.5 * nrm(ks[2], (DEPTH, DEC_BATCH, GLA_HEADS, GLA_HEAD_K, GLA_HEAD_V), f32),
        'state_ssd': 0.5 * nrm(ks[3], (DEPTH, DEC_BATCH, SSD_HEADS, SSD_HEADDIM, SSD_STATE), f32),
        'state_ssd_conv': nrm(ks[4], (DEPTH, DEC_BATCH, SSD_CONV - 1, SSD_CONV_CH), f32),
        'state_ffn_conv': nrm(ks[5], (DEPTH, DEC_BATCH, FFN_CONV - 1, 2 * FFN_DIM), f32),
        'norm_mix_pre': 1.0 + 0.02 * nrm(ks[6], (DEPTH, D_MODEL), f32),
        'norm_mix_post': 1.0 + 0.02 * nrm(ks[7], (DEPTH, D_MODEL), f32),
        'norm_ffn_pre': 1.0 + 0.02 * nrm(ks[8], (DEPTH, D_MODEL), f32),
        'norm_ffn_post': 1.0 + 0.02 * nrm(ks[9], (DEPTH, D_MODEL), f32),
        'w_in': nrm(ks[10], (DEPTH, D_MODEL, IN_COLS), f32) * D_MODEL ** -0.5,
        'gla_w_gate2': nrm(ks[11], (DEPTH, GLA_LOWRANK, GLA_KDIM), f32) * GLA_LOWRANK ** -0.5,
        'gla_b_gate': 0.1 * nrm(ks[12], (DEPTH, GLA_KDIM), f32),
        'gla_norm': 1.0 + 0.02 * nrm(ks[13], (DEPTH, GLA_HEAD_V), f32),
        'ssd_conv_w': nrm(ks[14], (DEPTH, SSD_CONV, SSD_CONV_CH), f32) * SSD_CONV ** -0.5,
        'ssd_conv_b': 0.01 * nrm(ks[15], (DEPTH, SSD_CONV_CH), f32),
        'ssd_dt_bias': dt + jnp.log(-jnp.expm1(-dt)),
        'ssd_A_log': jnp.log(jax.random.uniform(ks[17], (DEPTH, SSD_HEADS), f32, minval=1.0, maxval=16.0)),
        'ssd_D': 1.0 + 0.1 * nrm(ks[18], (DEPTH, SSD_HEADS), f32),
        'ssd_norm': 1.0 + 0.02 * nrm(ks[19], (DEPTH, SSD_WIDTH), f32),
        'w_out': nrm(ks[20], (DEPTH, MIX_WIDTH, D_MODEL), f32) * MIX_WIDTH ** -0.5,
        'ffn_w_in': nrm(ks[21], (DEPTH, D_MODEL, 2 * FFN_DIM), f32) * D_MODEL ** -0.5,
        'ffn_conv_w': nrm(ks[22], (DEPTH, FFN_CONV, 2 * FFN_DIM), f32) * FFN_CONV ** -0.5,
        'ffn_conv_b': 0.01 * nrm(ks[23], (DEPTH, 2 * FFN_DIM), f32),
        'ffn_w_out': nrm(ks[24], (DEPTH, FFN_DIM, D_MODEL), f32) * FFN_DIM ** -0.5,
    }

def reference(x_prompt, x_sample, state_gla, state_ssd, state_ssd_conv, state_ffn_conv,
              norm_mix_pre, norm_mix_post, norm_ffn_pre, norm_ffn_post, w_in,
              gla_w_gate2, gla_b_gate, gla_norm, ssd_conv_w, ssd_conv_b, ssd_dt_bias,
              ssd_A_log, ssd_D, ssd_norm, w_out, ffn_w_in, ffn_conv_w, ffn_conv_b, ffn_w_out):
    dt_ = x_prompt.dtype
    xp, xs = x_prompt, x_sample
    gp, hp, cp, fp = [], [], [], []
    gs, hs, cs, fs = [], [], [], []
    for l in range(DEPTH):
        p = dict(n_mix_pre=norm_mix_pre[l], n_mix_post=norm_mix_post[l],
                 n_ffn_pre=norm_ffn_pre[l], n_ffn_post=norm_ffn_post[l], w_in=w_in[l],
                 gla_w_gate2=gla_w_gate2[l], gla_b_gate=gla_b_gate[l], gla_norm=gla_norm[l],
                 ssd_conv_w=ssd_conv_w[l], ssd_conv_b=ssd_conv_b[l], ssd_dt_bias=ssd_dt_bias[l],
                 ssd_A_log=ssd_A_log[l], ssd_D=ssd_D[l], ssd_norm=ssd_norm[l], w_out=w_out[l],
                 ffn_w_in=ffn_w_in[l], ffn_conv_w=ffn_conv_w[l], ffn_conv_b=ffn_conv_b[l],
                 ffn_w_out=ffn_w_out[l])
        B = xp.shape[0]
        xp, g1, h1, c1, f1 = _layer(
            xp,
            jnp.zeros((B, GLA_HEADS, GLA_HEAD_K, GLA_HEAD_V), dt_),
            jnp.zeros((B, SSD_HEADS, SSD_HEADDIM, SSD_STATE), dt_),
            jnp.zeros((B, SSD_CONV - 1, SSD_CONV_CH), dt_),
            jnp.zeros((B, FFN_CONV - 1, 2 * FFN_DIM), dt_),
            p)
        xs, g2, h2, c2, f2 = _layer(xs, state_gla[l], state_ssd[l], state_ssd_conv[l],
                                    state_ffn_conv[l], p)
        gp.append(g1); hp.append(h1); cp.append(c1); fp.append(f1)
        gs.append(g2); hs.append(h2); cs.append(c2); fs.append(f2)
    return (xp, xs,
            jnp.stack(gp), jnp.stack(hp), jnp.stack(cp), jnp.stack(fp),
            jnp.stack(gs), jnp.stack(hs), jnp.stack(cs), jnp.stack(fs))


_drawn_inputs = setup_inputs


def setup_inputs(seed=0):
    import zlib

    import numpy as np

    out = dict(_drawn_inputs(seed))
    spreads = {}
    factors = {'norm_mix_post': 3.426,
     'norm_ffn_pre': 2.787,
     'norm_ffn_post': 4.818,
     'gla_norm': 6.457,
     'ssd_conv_b': 3.058,
     'ssd_norm': 3.988,
     'ffn_conv_b': 6.87}
    for name, (base, spread) in spreads.items():
        noise = np.random.default_rng([zlib.crc32(name.encode()), seed]).standard_normal(out[name].shape)
        drawn = base * np.exp(spread * noise) if base else spread * noise
        out[name] = __import__('jax').numpy.asarray(drawn.astype(out[name].dtype))
    for name, factor in factors.items():
        out[name] = (out[name] * factor).astype(out[name].dtype)
    return out
```

```python
from contextlib import ExitStack

import numpy as np

import concourse.bass as bass
from concourse import mybir

F32 = mybir.dt.float32
F32R = mybir.dt.float32r
U8 = mybir.dt.uint8
ALU = mybir.AluOpType
ACT = mybir.ActivationFunctionType

P = 128
D = 2048
SEQ, BATCHES, DEC = 512, 8, 8
SMP = BATCHES * DEC
T = SEQ + SMP
KT = D // P
GH, GK, GV = 4, 128, 256
RANK = 16
SH, SD, SN, SG = 16, 64, 128, 2
SC = 4
F = 5632
FT = F // P
FC = 3
EPS = 1e-6
GATE_NORM = 16.0
CH = 128
NC = SEQ // CH
HALF = T // 2
LEVELS = [CH >> (i + 1) for i in range(7)]

PAIR_TILES, PAIR_UNITS = 2, 4
IN_PAIRS = 22
OUT_PAIRS = KT // 2
OUT_UNIT0 = 2 + IN_PAIRS * PAIR_UNITS
OUT_TILE0 = 1 + IN_PAIRS * PAIR_TILES
FFN_UNIT0 = OUT_UNIT0 + OUT_PAIRS * PAIR_UNITS
FFN_TILE0 = OUT_TILE0 + OUT_PAIRS * PAIR_TILES
BLOCKS = FT // 2
UNITS = FFN_UNIT0 + 12 * BLOCKS
RING = 4

V_PAIR0, SPILL_PAIR0 = 4, 8
SPILLED = 28
XBC_TILES, G_SPILL, Z_SPILL = 12, 12, 20

COL = {}
_n = 0
for _name, _w in (("mix_pre", 16), ("mix_post", 16), ("ffn_pre", 16), ("ffn_post", 16), ("gate_b", 4),
                  ("gla_norm", 2), ("conv_w", 48), ("conv_b", 12), ("ssd_D", 8), ("ssd_norm", 8),
                  ("dt_bias", 1), ("A_log", 1), ("eps", 1), ("batch", 8)):
    COL[_name] = _n
    _n += _w
NVEC = _n
MASK_TRI, MASK_TRI_S = 8, 9

PADW = SC - 1 + SEQ + BATCHES * (SC - 1 + DEC)
CONVW = PADW - (SC - 1)
FPADW = FC - 1 + SEQ + BATCHES * (FC - 1 + DEC)
FCONVW = FPADW - (FC - 1)


SAMPLE_STEPS = (0, 5, 6, 7)


def att_base(s):
    return GH * s + sum(t < s for t in SAMPLE_STEPS)


def build(nc, xT, weights, vecs, ident_d, masks_d, psel_d, gate2, sconv_in, fconv_in, fvec_d, gla_in,
          ssdT_in, ssd_in, yT, gla_p, ssd_p, sconv_out, fconv_out, gla_s, ssd_s):
    spill = nc.dram_tensor("spill", [SPILLED, P, T], F32, kind="Internal").ap()
    h_spill = nc.dram_tensor("h_spill", [KT, P, T], F32, kind="Internal").ap()
    with ExitStack() as ctx:
        def sb(name, shape, dt=F32):
            return ctx.enter_context(nc.sbuf_tensor(name, shape, dt))

        def sem(name):
            return ctx.enter_context(nc.semaphore(name))

        raw = sb("raw", [P, 2, 8, P])
        w_hi = sb("w_hi", [P, RING, 8, P], F32R)
        w_lo = sb("w_lo", [P, RING, 8, P], F32R)
        x_hi = sb("x_hi", [P, KT, T], F32R)
        x_lo = sb("x_lo", [P, KT, T], F32R)
        vec = sb("vec", [P, NVEC])
        ident = sb("ident", [P, P])
        ones = sb("ones", [P, P])
        masks = sb("masks", [P, 10, P], U8)
        reset = sb("reset", [P, T])
        rstd = sb("rstd", [P, T])
        misc = sb("misc", [P, T])
        decay = sb("decay", [P, 64])
        tok = sb("tok", [P, 5, 64])
        arena = sb("arena", [P, 16768])
        with nc.sbuf_tensor("tail", [P, 4736], F32) as tail:
            pass
        g_hi = sb("g_hi", [P, 2, 2, T], F32R)
        g_lo = sb("g_lo", [P, 2, 2, T], F32R)
        psum_proj = ctx.enter_context(nc.psum_tensor("psum_proj", [P, 4, 512], F32))
        work = ctx.enter_context(nc.psum_tensor("psum_work", [P, 4, 512], F32))

        def V(name, j=0, rows=P):
            return vec[0:rows, COL[name] + j:COL[name] + j + 1]

        def A(off, n, rows=P):
            return arena[0:rows, off:off + n]

        def TL(off, n, rows=P):
            return tail[0:rows, off:off + n]

        gdecay = decay[:, 0:48].rearrange("p (h c) -> p h c", h=GH)
        GQ, GKK, GB, GE = A(0, 2304), A(2304, 2304), A(4608, 2304), A(6912, 2304)
        GE2 = TL(0, 2304)
        xin = [A(6912, 2304), TL(0, 2304)]
        v_tok = A(9216, 5120).rearrange("p (t v) -> p t v", t=5)
        w_gate2 = A(9216, 512)
        masks_f = A(9728, 10 * P).rearrange("p (n t) -> p n t", n=10)
        att = A(14336, 2048).rearrange("p (n t) -> p n t", n=16)
        att_s = A(16384, 256, SMP).rearrange("p (h t) -> p h t", h=GH)
        kd_tok = TL(0, 2560).rearrange("p (t k) -> p t k", t=5)
        stage = TL(2560, 1152).rearrange("p (j t) -> p j t", j=2)
        S = TL(3712, 1024).rearrange("p (h v) -> p h v", h=GH)
        oT = A(2304, 4608).rearrange("p (n t) -> p n t", n=8)
        gsum2 = A(6912 + 2 * T, T)
        s0ring = A(6912, 2048).rearrange("p (r h v) -> p r h v", r=2, h=GH)
        kd_m = A(14336, 1024, SMP).rearrange("p (r h k) -> p r h k", r=2, h=GH)
        gT = A(9216, 4608).rearrange("p (n t) -> p n t", n=8)
        XC = A(0, 6912).rearrange("p (n t) -> p n t", n=12)
        xdt = A(6912, 5120).rearrange("p (t v) -> p t v", t=5)
        dt_tmp = [A(6912 + 576 * i, 576, SH) for i in range(4)]
        B_tok = A(12032, 1280).rearrange("p (t g n) -> p t g n", t=5, g=SG)
        W = A(13312, 2048).rearrange("p (h t) -> p h t", h=SH)
        conv_t = [A(13312 + PADW * i, PADW) for i in range(2)]
        hT = A(15360, 1024)
        cbm = A(16384, 256).rearrange("p (g t) -> p g t", g=SG)
        xw = TL(0, 1024)
        pad = [TL(1024 + PADW * i, PADW) for i in range(2)]
        psel = TL(2230, 1024, SH)
        cumT = TL(3254, 576, SH)
        ecum = TL(1024, 512)
        yt = TL(3830, 512)
        sconv_o = TL(4342, 324).rearrange("p (n c) -> p n c", n=12)
        lastrow = TL(4666, 64, SH)
        dtT = misc[0:SH, :]
        hTs = A(6912, 2048).rearrange("p (r x) -> p r x", r=2)
        hns = A(8960, 2048).rearrange("p (r j n) -> p r j n", r=2, j=8)
        Bm = A(13312, 2048, SMP).rearrange("p (b g n) -> p b g n", b=BATCHES, g=SG)
        zT = A(6912, 4608).rearrange("p (n t) -> p n t", n=8)
        ysq = A(13312, 2304).rearrange("p (n t) -> p n t", n=4)
        mixT = A(0, 9216).rearrange("p (n t) -> p n t", n=KT)
        acc = mixT
        sq = [TL(2560 + 576 * i, 576) for i in range(2)]
        sqsum = TL(3712, 576)

        def xres(kt):
            return A(9216 + 576 * kt, 576) if kt < 13 else TL(576 * (kt - 13), 576)

        fpad = [A(9216 + FPADW * i, FPADW) for i in range(2)]
        ftap = [A(10404 + FPADW * i, FPADW) for i in range(2)]
        fgate = A(11592, 576)
        fstate = A(12168, 1408).rearrange("p (b c) -> p b c", b=BLOCKS)
        fout = A(13576, 1584).rearrange("p (b c) -> p b c", b=BLOCKS)
        fvec = A(15160, 352).rearrange("p (b c) -> p b c", b=BLOCKS)
        fc = [A(15512 + 16 * i, 16) for i in range(2)]
        fsq = [A(15544, 576), A(16120, 576)]

        const_in = sem("const_in")
        gate2_in = sem("gate2_in")
        x_in = [sem("x_in0"), sem("x_in1")]
        raw_in = [sem("raw_in0"), sem("raw_in1")]
        hi_ready, lo_ready = sem("hi_ready"), sem("lo_ready")
        units_done = sem("units_done")
        taken = sem("taken")
        setup = sem("setup")
        own_step = sem("own_step")
        small_mm, small_out, e_mm, sq_free, hsq_mm, ysq_mm = (sem(n) for n in (
            "small_mm", "small_out", "e_mm", "sq_free", "hsq_mm", "ysq_mm"))
        f_st, fo_st, f_tap1, down_mm = (sem(n) for n in ("f_st", "fo_st", "f_tap1", "down_mm"))
        x_hi_w, x_split = sem("x_hi_w"), sem("x_split")
        sq_ready, sq_used = sem("sq_ready"), sem("sq_used")
        root_ready = sem("root_ready")
        rstd_ready = sem("rstd_ready")
        gate_mm, gate_out, gate_sub, gate_exp, gate_ln = (sem(n) for n in ("gate_mm", "gate_out", "gate_sub", "gate_exp", "gate_ln"))
        b_ready = sem("b_ready")
        v_tr, v_out = sem("v_tr"), sem("v_out")
        spilled = [sem("spilled0"), sem("spilled1")]
        sub_ready, exp_ready, pq_ready, att_mm, att_out = (sem(n) for n in ("sub_ready", "exp_ready", "pq_ready", "att_mm", "att_out"))
        kdT_ready, kd_tr, kd_out, qd_ready = (sem(n) for n in ("kdT_ready", "kd_tr", "kd_out", "qd_ready"))
        o_mm, o_out, S_mm, S_ready = (sem(n) for n in ("o_mm", "o_out", "S_mm", "S_ready"))
        s0_in = [sem("s0_in0"), sem("s0_in1")]
        s0_out = [sem("s0_out0"), sem("s0_out1")]
        kdm_ready, os_mm, os_out, s1_mm, s1_ready = (sem(n) for n in ("kdm_ready", "os_mm", "os_out", "s1_mm", "s1_ready"))
        gla_p_out = sem("gla_p_out")
        g_in, gsq, gsum, gss, groot, grs, gsilu, gy, ghi, mix_in = (sem(n) for n in (
            "g_in", "gsq", "gsum", "gss", "groot", "grs", "gsilu", "gy", "ghi", "mix_in"))
        pad_in = [sem("pad_in0"), sem("pad_in1")]
        pad_zero, tap0, taps, conv_out, sco = (sem(n) for n in ("pad_zero", "tap0", "taps", "conv_out", "sco"))
        psel_in, dts, dte, dt_ready, dttr, dtt_out = (sem(n) for n in ("psel_in", "dts", "dte", "dt_ready", "dttr", "dtt_out"))
        xtr, xdt_out, b_out = sem("xtr"), sem("xdt_out"), sem("b_out")
        bc_mm, D_ready, W_exp, W_ready, y_mm, e_exp, y_out = (sem(n) for n in (
            "bc_mm", "D_ready", "W_exp", "W_ready", "y_mm", "e_exp", "y_out"))
        wd_exp, xw_ready, h_mm, h_ready = (sem(n) for n in (
            "wd_exp", "xw_ready", "h_mm", "h_ready"))
        ssd_p_out = sem("ssd_p_out")
        hs_in = [sem("hs_in0"), sem("hs_in1")]
        hs_out = [sem("hs_out0"), sem("hs_out1")]
        sm_ready, hs_mm, hs_ready = sem("sm_ready"), sem("hs_mm"), sem("hs_ready")
        z_in, zsilu, yz, ysq_r, ysum, yroot, ymix, yhi = (sem(n) for n in (
            "z_in", "zsilu", "yz", "ysq_r", "ysum", "yroot", "ymix", "yhi"))
        sconv_st = sem("sconv_st")
        xr_in = [sem("xr_in%d" % i) for i in range(4)]
        msq, msum_mm, mroot = (sem(n) for n in ("msq", "msum_mm", "mroot"))
        h_w, hsq, h_hi, h_split, h_st = (sem(n) for n in ("h_w", "hsq", "h_hi", "h_split", "h_st"))
        ffn_in, acc_zero, fpad_zero = sem("ffn_in"), sem("acc_zero"), sem("fpad_zero")
        fc_ready, f_tap0, f_padout, f_taps, f_silu, f_prod, f_hi, act_ready = (sem(n) for n in (
            "fc_ready", "f_tap0", "f_padout", "f_taps", "f_silu", "f_prod", "f_hi", "act_ready"))
        ysq2, h_back, y_w, y_st = (sem(n) for n in (
            "ysq2", "h_back", "y_w", "y_st"))

        block = ctx.enter_context(nc.Block())

        def halves(ap):
            return ap.rearrange("p (n t) -> p n t", n=2)

        def proj(ring):
            return psum_proj[:, 2 * ring:2 * ring + 2, 0:HALF]

        def bcast(ap, shape):
            return ap.broadcast_to(shape)

        @block.sync
        def _(sp):
            def x_chunk(c):
                sp.dma_start(xin[c % 2], xT[c]).then_inc(x_in[c % 2], 16)

            x_chunk(0)
            sp.dma_start(raw[:, 0], weights[0]).then_inc(raw_in[0], 16)
            x_chunk(1)
            sp.dma_start(raw[:, 1], weights[1]).then_inc(raw_in[1], 16)
            for c in (2, 3):
                sp.wait_ge(x_split, 4 * (c - 1))
                sp.wait_ge(sq_ready, 4 * (c - 1))
                x_chunk(c)
            with sp.Fori(1, UNITS // 2) as i:
                for j in range(2):
                    sp.wait_ge(lo_ready, 2 * i + j - 1)
                    sp.dma_start(raw[:, j], weights[bass.ds(2 * i + j, 1)].rearrange("o p a b -> (o p) a b"))\
                        .then_inc(raw_in[j], 16)

        @block.gpsimd
        def _(pool):
            def weight_lo(unit, slot, r):
                pool.wait_ge(hi_ready, unit + 1)
                nc.gpsimd.tensor_tensor(w_lo[:, slot], raw[:, r], w_hi[:, slot].bitcast(F32),
                                        ALU.subtract).then_inc(lo_ready, 1)

            weight_lo(0, 0, 0)
            weight_lo(1, 1, 1)
            with pool.Fori(0, (UNITS - 2) // 4) as i:
                for j in range(4):
                    weight_lo(4 * i + 2 + j, (2 + j) % 4, j % 2)

        @block.scalar
        def _(act):
            def weight_hi(unit, half_unit, slot, r, wait=True):
                act.wait_ge(raw_in[r], 16 * half_unit + 16)
                if wait:
                    act.wait_ge(units_done, unit - 3)
                nc.scalar.activation(w_hi[:, slot], raw[:, r], ACT.Copy).then_inc(hi_ready, 1)

            def two_hi(unit, half_unit, slot):
                weight_hi(unit, half_unit, slot, 0)
                weight_hi(unit + 1, half_unit, slot + 1, 1)

            def root(out, psum, scale, done):
                nc.scalar.activation(halves(out), psum, ACT.Sqrt, bias=V("eps"), scale=scale).then_inc(done, 1)

            act.dma_start(vec[:], vecs).then_inc(const_in, 16)
            act.dma_start(ident[:], ident_d).then_inc(const_in, 16)
            act.dma_start(masks_f, masks_d).then_inc(const_in, 16)
            act.dma_start(w_gate2[32:32 + RANK, :], gate2).then_inc(gate2_in, 16)
            weight_hi(0, 0, 0, 0, wait=False)
            weight_hi(1, 0, 1, 1, wait=False)
            for kt in range(KT):
                act.wait_ge(x_in[kt // 4 % 2], 16 * (kt // 8 + 1))
                if kt >= 2:
                    act.wait_ge(sq_used, kt - 1)
                nc.scalar.activation(stage[:, kt % 2], xin[kt // 4 % 2][:, kt % 4 * T:(kt % 4 + 1) * T],
                                     ACT.Square).then_inc(sq_ready, 1)
            weight_hi(2, 1, 2, 0, wait=False)
            weight_hi(3, 1, 3, 1, wait=False)
            act.wait_ge(sq_used, KT)
            act.wait_ge(const_in, 48)
            root(rstd[:], work[:, 0:2, 0:HALF], 1.0 / D, root_ready)
            weight_hi(4, 2, 0, 0)
            weight_hi(5, 2, 1, 1)
            with act.Fori(0, V_PAIR0) as i:
                two_hi(4 * i + 6, 2 * i + 3, 2)
                two_hi(4 * i + 8, 2 * i + 4, 0)
            for h in range(GH):
                act.wait_ge(gate_mm, h + 1)
                nc.scalar.activation(halves(GE[:, h * T:(h + 1) * T]), work[:, 2 * (h % 2):2 * (h % 2) + 2, 0:HALF],
                                     ACT.Identity, bias=V("gate_b", h)).then_inc(gate_out, 1)
            act.wait_ge(gate_sub, 1)
            nc.scalar.activation(GE2, GE2, ACT.Exp).then_inc(gate_exp, 1)
            act.wait_ge(gate_exp, 1)
            nc.scalar.activation(GE2, GE2, ACT.Ln, bias=1.0).then_inc(gate_ln, 1)
            with act.Fori(0, 4) as i:
                two_hi(4 * i + 4 * V_PAIR0 + 6, 2 * i + 2 * V_PAIR0 + 3, 2)
                two_hi(4 * i + 4 * V_PAIR0 + 8, 2 * i + 2 * V_PAIR0 + 4, 0)
                for j in range(2):
                    act.wait_ge(v_tr, 2 * i + j + 1)
                    nc.scalar.activation(v_tok[:, 0:4, bass.ds((2 * i + j) * P, P)],
                                         work[:, j, :].rearrange("p (a b) -> p a b", a=4), ACT.Copy)
                    nc.scalar.activation(v_tok[0:SMP, 4, bass.ds((2 * i + j) * P, P)],
                                         work[0:SMP, 2 + j, 0:P], ACT.Copy).then_inc(v_out, 1)

            def spill_tile(n, j, count):
                act.wait_ge(taken, count + 2)
                act.dma_start(spill[bass.ds(n, 1)].rearrange("o p t -> (o p) t"), stage[:, j])\
                    .then_inc(spilled[j], 16)

            for s in range(8):
                if s >= 1:
                    m = LEVELS[s - 1]
                    buf = GE if s % 2 else GE2
                    view = buf if m <= 4 else buf.rearrange("p (h t) -> p h t", h=GH)[:, :, 0:SEQ]
                    act.wait_ge(sub_ready, s)
                    nc.scalar.activation(view, view, ACT.Exp, scale=1.0 / GATE_NORM).then_inc(exp_ready, 1)
                p = SPILL_PAIR0 + s
                two_hi(4 * p + 6, 2 * p + 3, 2)
                spill_tile(2 * s, 0, 2 * p + 2)
                two_hi(4 * p + 8, 2 * p + 4, 0)
                spill_tile(2 * s + 1, 1, 2 * p + 3)
            with act.Fori(8, 14) as i:
                two_hi(4 * i + 4 * SPILL_PAIR0 + 6, 2 * i + 2 * SPILL_PAIR0 + 3, 2)
                spill_tile(2 * i, 0, 2 * i + 2 * SPILL_PAIR0 + 2)
                two_hi(4 * i + 4 * SPILL_PAIR0 + 8, 2 * i + 2 * SPILL_PAIR0 + 4, 0)
                spill_tile(2 * i + 1, 1, 2 * i + 2 * SPILL_PAIR0 + 3)

            act.wait_ge(sub_ready, 8)
            nc.scalar.activation(GE, GE, ACT.Exp, scale=1.0 / GATE_NORM).then_inc(exp_ready, 1)
            nc.scalar.activation(GE2, GB, ACT.Exp, scale=1.0 / GATE_NORM).then_inc(exp_ready, 1)
            act.wait_ge(qd_ready, 1)
            for tt in range(5):
                n = P if tt < 4 else SMP
                act.wait_ge(kd_tr, tt + 1)
                nc.scalar.activation(kd_tok[0:n, tt, :], work[0:n, tt % 4, :], ACT.Copy).then_inc(kd_out, 1)
            for b in range(2):
                act.dma_start(s0ring[:, b], gla_in[:, b * GH:(b + 1) * GH, :]).then_inc(s0_in[b], 16)
            for c in range(NC):
                act.wait_ge(o_mm, c + 1)
                nc.scalar.activation(oT[:, :, c * CH:(c + 1) * CH],
                                     work[:, 0:2, :].rearrange("p a (b t) -> p (a b) t", b=4), ACT.Copy)\
                    .then_inc(o_out, 1)
            act.wait_ge(S_ready, NC)
            act.dma_start(gla_p, S).then_inc(gla_p_out, 16)
            for b in range(BATCHES):
                act.wait_ge(s1_ready, b + 1)
                act.dma_start(gla_s[:, b * GH:(b + 1) * GH, :], s0ring[:, b % 2]).then_inc(s0_out[b % 2], 16)
                if b + 2 < BATCHES:
                    act.wait_ge(s0_out[b % 2], 16 * (b // 2 + 1))
                    act.dma_start(s0ring[:, b % 2], gla_in[:, (b + 2) * GH:(b + 3) * GH, :])\
                        .then_inc(s0_in[b % 2], 16)
            act.wait_ge(os_mm, 1)
            nc.scalar.activation(oT[:, :, SEQ:T], work[:, 0, :].rearrange("p (n t) -> p n t", n=8), ACT.Copy)\
                .then_inc(os_out, 1)
            for j in range(2):
                act.wait_ge(spilled[j], 16 * SPILLED // 2)
            act.dma_start(gT, spill[G_SPILL:G_SPILL + 8].rearrange("n p t -> p n t")).then_inc(g_in, 16)
            act.wait_ge(os_out, 1)
            for j in range(2):
                act.wait_ge(s0_out[j], 16 * BATCHES // 2)
            for h in range(GH):
                if h >= 1:
                    act.wait_ge(gss, h)
                nc.scalar.activation(GE[:, 0:2 * T].rearrange("p (n t) -> p n t", n=2), oT[:, 2 * h:2 * h + 2, :],
                                     ACT.Square).then_inc(gsq, 1)
                act.wait_ge(gsum, h + 1)
                root(GQ[:, h * T:(h + 1) * T], work[:, 0:2, 0:HALF], 1.0 / GV, groot)
            act.wait_ge(g_in, 16)
            for h in range(GH):
                nc.scalar.activation(gT[:, 2 * h:2 * h + 2, :], gT[:, 2 * h:2 * h + 2, :], ACT.Silu)\
                    .then_inc(gsilu, 1)
            for h in range(GH):
                act.wait_ge(gy, h + 1)
                nc.scalar.activation(x_hi[:, 2 * h:2 * h + 2, :], oT[:, 2 * h:2 * h + 2, :], ACT.Copy)\
                    .then_inc(ghi, 1)

            act.dma_start(psel, psel_d).then_inc(psel_in, 16)
            act.wait_ge(dts, 1)
            nc.scalar.activation(V("A_log", rows=SH), V("A_log", rows=SH), ACT.Exp)
            nc.scalar.activation(dt_tmp[0], dt_tmp[0], ACT.Exp).then_inc(dte, 1)

            def pad_load(n):
                q = pad[n % 2]
                act.dma_start(q[:, SC - 1:SC - 1 + SEQ], spill[n, :, 0:SEQ]).then_inc(pad_in[n % 2], 16)
                s = q[:, SC - 1 + SEQ:PADW].rearrange("p (b t) -> p b t", b=BATCHES)
                act.dma_start(s[:, :, SC - 1:], spill[n, :, SEQ:T].rearrange("p (b t) -> p b t", b=BATCHES))\
                    .then_inc(pad_in[n % 2], 16)
                act.dma_start(s[:, :, 0:SC - 1], sconv_in[:, n]).then_inc(pad_in[n % 2], 16)

            act.wait_ge(mix_in, 4)
            act.wait_ge(gla_p_out, 16)
            pad_load(0)
            pad_load(1)
            for n in range(XBC_TILES):
                q = pad[n % 2]
                act.wait_ge(pad_in[n % 2], 48 * (n // 2 + 1))
                act.wait_ge(pad_zero, 1)
                nc.scalar.activation(conv_t[n % 2][:, 0:CONVW], q[:, 0:CONVW], ACT.Identity,
                                     bias=V("conv_b", n), scale=V("conv_w", 4 * n)).then_inc(tap0, 1)
                nc.scalar.activation(sconv_o[:, n, 0:SC - 1], q[:, SEQ:SEQ + SC - 1], ACT.Copy)
                nc.scalar.activation(
                    sconv_o[:, n, SC - 1:].rearrange("p (b c) -> p b c", b=BATCHES),
                    q[:, SC - 1 + SEQ:].rearrange("p (b t) -> p b t", b=BATCHES)[:, :, DEC:], ACT.Copy).then_inc(sco, 1)
                act.wait_ge(taps, n + 1)
                nc.scalar.activation(XC[:, n, 0:SEQ], conv_t[n % 2][:, 0:SEQ], ACT.Silu)
                nc.scalar.activation(
                    XC[:, n, SEQ:].rearrange("p (b t) -> p b t", b=BATCHES),
                    conv_t[n % 2][:, SEQ + SC - 1:].rearrange("p (b t) -> p b t", b=BATCHES)[:, :, 0:DEC], ACT.Silu)\
                    .then_inc(conv_out, 1)
                if n + 2 < XBC_TILES:
                    act.wait_ge(sco, n + 1)
                    pad_load(n + 2)
            act.wait_ge(sco, XBC_TILES)
            act.dma_start(sconv_out, sconv_o).then_inc(sconv_st, 16)
            for tt in range(5):
                n = P if tt < 4 else SMP
                act.wait_ge(xtr, tt + 1)
                nc.scalar.activation(B_tok[0:n, tt].rearrange("p g n -> p (g n)"), work[0:n, 2, 0:SG * SN],
                                     ACT.Copy).then_inc(b_out, 1)
            for c in range(NC):
                act.wait_ge(small_out, c + 1)
                nc.scalar.activation(tok[:, c, 32:64], tok[:, c, 32:64], ACT.Exp).then_inc(wd_exp, 1)
                for g in range(SG):
                    k = SG * c + g
                    act.wait_ge(D_ready, k + 1)
                    nc.scalar.activation(W[:, 8 * g:8 * g + 8, :], W[:, 8 * g:8 * g + 8, :], ACT.Exp, scale=-1.0)\
                        .then_inc(W_exp, 1)
                    act.wait_ge(e_mm, k + 1)
                    if k >= 1:
                        act.wait_ge(y_out, k)
                    nc.scalar.activation(ecum, work[:, 3, :], ACT.Exp).then_inc(e_exp, 1)
            act.wait_ge(h_ready, SG * NC)
            act.dma_start(ssd_p, hT).then_inc(ssd_p_out, 16)
            for b in range(2):
                act.dma_start(hTs[:, b], ssdT_in[:, b]).then_inc(hs_in[b], 16)
                act.dma_start(hns[:, b], ssd_in[:, b]).then_inc(hs_in[b], 16)
            act.wait_ge(small_out, NC + 1)
            nc.scalar.activation(decay[:], work[:, 2, 272:336], ACT.Exp)
            nc.scalar.activation(tok[0:SMP, NC, 32:48], tok[0:SMP, NC, 32:48], ACT.Exp).then_inc(wd_exp, 1)
            act.wait_ge(D_ready, SG * NC + 1)
            nc.scalar.activation(W[0:SMP, :, 0:SMP], W[0:SMP, :, 0:SMP], ACT.Exp, scale=-1.0).then_inc(W_exp, 1)
            act.wait_ge(e_mm, SG * NC + 1)
            act.wait_ge(y_out, SG * NC)
            nc.scalar.activation(ecum, work[:, 3, :], ACT.Exp).then_inc(e_exp, 1)
            for b in range(BATCHES):
                act.wait_ge(hs_ready, b + 1)
                act.dma_start(ssd_s[:, b], hns[:, b % 2]).then_inc(hs_out[b % 2], 16)
                if b + 2 < BATCHES:
                    act.wait_ge(hs_mm, b + 1)
                    act.dma_start(hTs[:, b % 2], ssdT_in[:, b + 2]).then_inc(hs_in[b % 2], 16)
                    act.wait_ge(hs_out[b % 2], 16 * (b // 2 + 1))
                    act.dma_start(hns[:, b % 2], ssd_in[:, b + 2]).then_inc(hs_in[b % 2], 16)
            for j in range(2):
                act.wait_ge(hs_out[j], 16 * BATCHES // 2)
            act.wait_ge(y_out, SG * NC + 1)
            act.dma_start(zT, spill[Z_SPILL:Z_SPILL + 8].rearrange("n p t -> p n t")).then_inc(z_in, 16)
            act.wait_ge(z_in, 16)
            nc.scalar.activation(zT, zT, ACT.Silu).then_inc(zsilu, 1)
            act.wait_ge(yz, 1)
            act.wait_ge(ssd_p_out, 16)
            for g in range(SG):
                if g >= 1:
                    act.wait_ge(ysum, g)
                nc.scalar.activation(ysq, XC[:, 4 * g:4 * g + 4, :], ACT.Square).then_inc(ysq_r, 1)
            for g in range(SG):
                act.wait_ge(ysum, g + 1)
                root(zT[:, g], work[:, 2 * g:2 * g + 2, 0:HALF], 1.0 / (SH * SD // SG), yroot)
            for j in range(8):
                act.wait_ge(ymix, j + 1)
                nc.scalar.activation(x_hi[:, 8 + j], XC[:, j], ACT.Copy).then_inc(yhi, 1)

            act.wait_ge(mix_in, 12)
            for c in range(3):
                act.dma_start(A(9216 + 2304 * c, 2304), xT[c]).then_inc(xr_in[c], 16)
            act.dma_start(A(9216 + 3 * 2304, T), xT[3, :, 0:T]).then_inc(xr_in[3], 16)
            act.dma_start(TL(0, 3 * T), xT[3, :, T:4 * T]).then_inc(xr_in[3], 16)
            with act.Fori(0, OUT_PAIRS) as i:
                two_hi(4 * i + OUT_UNIT0 + 4, 2 * i + OUT_UNIT0 // 2 + 2, 2)
                two_hi(4 * i + OUT_UNIT0 + 6, 2 * i + OUT_UNIT0 // 2 + 3, 0)
                for j in range(2):
                    act.wait_ge(taken, 2 * i + j + OUT_TILE0 + 3)
                    act.wait_ge(sq_free, 2 * i + j + 1)
                    nc.scalar.activation(sq[j], mixT[:, bass.ds(2 * i + j, 1), :].rearrange("p o t -> p (o t)"),
                                         ACT.Square).then_inc(msq, 1)
            act.wait_ge(msum_mm, 1)
            root(rstd[:], work[:, 0:2, 0:HALF], 1.0 / D, mroot)
            for kt in range(KT):
                act.wait_ge(h_w, kt + 1)
                if kt >= 2:
                    act.wait_ge(hsq_mm, kt - 1)
                nc.scalar.activation(sq[kt % 2], mixT[:, kt], ACT.Square).then_inc(hsq, 1)
                nc.scalar.activation(x_hi[:, kt], mixT[:, kt], ACT.Copy, scale=V("ffn_pre", kt)).then_inc(h_hi, 1)
            act.dma_start(h_spill.rearrange("n p t -> p n t"), mixT).then_inc(h_st, 16)
            act.wait_ge(h_split, KT)
            act.dma_start(fstate, fconv_in).then_inc(ffn_in, 16)
            act.dma_start(fvec, fvec_d).then_inc(ffn_in, 16)
            act.wait_ge(hsq_mm, KT)
            root(rstd[:], work[:, 0:2, 0:HALF], 1.0 / D, mroot)

            def ffn_up(blk, q, unit, half_unit, first=False):
                act.wait_ge(ffn_in, 32)
                if not first:
                    act.wait_ge(f_taps, 4 * blk - 3)
                nc.scalar.activation(fc[q], fvec[:, bass.ds(blk, 1), :].rearrange("p o c -> p (o c)"), ACT.Copy)\
                    .then_inc(fc_ready, 1)
                for j in range(4):
                    t, pair = 4 * blk + j, 2 * blk + j // 2
                    pd = fpad[j % 2]
                    smp = pd[:, FC - 1 + SEQ:].rearrange("p (b t) -> p b t", b=BATCHES)
                    if not (first and j < 2):
                        act.wait_ge(f_taps, t - 1)
                    nc.scalar.activation(
                        smp[:, :, 0:FC - 1],
                        fstate[:, bass.ds(blk, 1), 16 * j:16 * j + 16].rearrange("p o (b t) -> p (o b) t", b=BATCHES),
                        ACT.Copy).then_inc(f_st, 1)
                    act.wait_ge(taken, 20 * blk + j + (FFN_TILE0 + 3 if first else FFN_TILE0 + 3 - 16))
                    act.wait_ge(fc_ready, blk + 1)
                    act.wait_ge(f_st, t + 1)
                    if j % 2 and not (first and j == 1):
                        act.wait_ge(f_prod, pair)
                    act.wait_ge(fpad_zero, 1)
                    nc.scalar.activation(ftap[j % 2][:, 0:FCONVW], pd[:, 0:FCONVW], ACT.Identity,
                                         bias=fc[q][:, 4 * j + 3:4 * j + 4], scale=fc[q][:, 4 * j:4 * j + 1])\
                        .then_inc(f_tap0, 1)
                    nc.scalar.activation(fout[:, bass.ds(blk, 1), 18 * j:18 * j + 2].rearrange("p o c -> p (o c)"),
                                         pd[:, SEQ:SEQ + FC - 1], ACT.Copy)
                    nc.scalar.activation(
                        fout[:, bass.ds(blk, 1), 18 * j + 2:18 * j + 18].rearrange("p o (b t) -> p (o b) t", b=BATCHES),
                        smp[:, :, DEC:], ACT.Copy).then_inc(f_padout, 1)
                    two_hi(unit + 2 * j, half_unit + j, (2 + 2 * j) % 4)
                    if j % 2:
                        a = ftap[0]
                        act.wait_ge(f_taps, t)
                        if not (first and j == 1):
                            act.wait_ge(act_ready, pair)
                        nc.scalar.activation(fgate[:, 0:SEQ], a[:, 0:SEQ], ACT.Silu)
                        nc.scalar.activation(
                            fgate[:, SEQ:T].rearrange("p (b t) -> p b t", b=BATCHES),
                            a[:, SEQ + FC - 1:].rearrange("p (b t) -> p b t", b=BATCHES)[:, :, 0:DEC], ACT.Silu)\
                            .then_inc(f_silu, 1)
                        act.wait_ge(f_prod, pair + 1)
                        nc.scalar.activation(g_hi[:, q, j // 2], fgate, ACT.Copy).then_inc(f_hi, 1)

            def ffn_down(unit, half_unit):
                two_hi(unit, half_unit, 2)
                two_hi(unit + 2, half_unit + 1, 0)

            act.wait_ge(sconv_st, 16)
            U = FFN_UNIT0 + 4
            ffn_up(0, 0, U, U // 2, first=True)
            with act.Fori(0, (BLOCKS - 2) // 2) as i:
                for q in (1, 0):
                    blk = 2 * i + (1 if q else 2)
                    u = 24 * i + U + 8 + (0 if q else 12)
                    hu = 12 * i + (U + 8) // 2 + (0 if q else 6)
                    ffn_up(blk, q, u, hu)
                    ffn_down(u + 8, hu + 4)
            u = U + 8 + 12 * (BLOCKS - 2)
            ffn_up(BLOCKS - 1, 1, u, u // 2)
            ffn_down(u + 8, u // 2 + 4)
            act.wait_ge(f_padout, 4 * BLOCKS)
            act.dma_start(fconv_out, fout).then_inc(fo_st, 16)
            act.dma_start(x_hi[:].bitcast(F32), h_spill.rearrange("n p t -> p n t")).then_inc(h_back, 16)
            act.wait_ge(taken, FFN_TILE0 + 20 * BLOCKS + 2)
            for kt in range(KT):
                if kt >= 2:
                    act.wait_ge(ysq_mm, kt - 1)
                nc.scalar.activation(fsq[kt % 2], acc[:, kt], ACT.Square).then_inc(ysq2, 1)
            act.wait_ge(ysq_mm, KT)
            root(rstd[:], work[:, 0:2, 0:HALF], 1.0 / D, mroot)
            for n in range(4):
                act.wait_ge(y_w, 4 * (n + 1))
                act.dma_start(yT[n], acc[:, 4 * n:4 * n + 4, :]).then_inc(y_st, 16)
            act.wait_ge(y_st, 64)
            act.wait_ge(fo_st, 16)
            act.wait_ge(sconv_st, 16)
            act.wait_ge(ssd_p_out, 16)
            act.wait_ge(gla_p_out, 16)
            for j in range(2):
                act.wait_ge(s0_out[j], 16 * BATCHES // 2)
                act.wait_ge(hs_out[j], 16 * BATCHES // 2)

        @block.tensor
        def _(pe):
            def products(slot, k, ring, split, first, last, hi, lo):
                cuts = ((0, 0, split), (1, split, T))
                for n, a, b in cuts:
                    for part in (0, 1):
                        nc.tensor.matmul(psum_proj[:, 2 * ring + n, 0:b - a], w_hi[:, slot, k], (hi, lo)[part][:, a:b],
                                         start=first and part == 0, stop=False)
                for n, a, b in cuts:
                    mm = nc.tensor.matmul(psum_proj[:, 2 * ring + n, 0:b - a], w_lo[:, slot, k], hi[:, a:b],
                                          start=False, stop=last)
                return mm

            def project(tile, unit, slot, ring, split=HALF, before=None):
                pe.wait_ge(taken, tile + 1)
                for half in range(2):
                    pe.wait_ge(lo_ready, unit + half + 1)
                    for k in range(8):
                        kt = 8 * half + k
                        if before:
                            before(kt)
                        mm = products(slot + half, k, ring, split, kt == 0, kt == KT - 1, x_hi[:, kt], x_lo[:, kt])
                        if k == 7:
                            mm.then_inc(units_done, 1)

            def pair(p):
                project(2 * p + 1, 4 * p + 2, 2, 1)
                project(2 * p + 2, 4 * p + 4, 0, 0)

            def sum_tokens(sources, bank, done, start=True, stop=True):
                for n in range(2):
                    for i, s in enumerate(sources):
                        mm = nc.tensor.matmul(work[:, bank + n, 0:HALF], ones[:], s[:, n * HALF:(n + 1) * HALF],
                                              start=start and i == 0, stop=stop and i == len(sources) - 1)
                mm.then_inc(done, 1)

            pe.wait_ge(setup, 1)
            for kt in range(KT):
                pe.wait_ge(sq_ready, kt + 1)
                sum_tokens([stage[:, kt % 2]], 0, sq_used, kt == 0, kt == KT - 1)
            project(0, 0, 0, 0, before=lambda kt: pe.wait_ge(x_split, kt + 1))
            with pe.Fori(0, V_PAIR0) as i:
                pair(i)
            pe.wait_ge(gate2_in, 16)
            pe.wait_ge(root_ready, 1)
            for h in range(GH):
                if h >= 2:
                    pe.wait_ge(gate_out, h - 1)
                for n in range(2):
                    mm = nc.tensor.matmul(work[:, 2 * (h % 2) + n, 0:HALF], w_gate2[32:32 + RANK, h * GK:(h + 1) * GK],
                                          misc[32:32 + RANK, n * HALF:(n + 1) * HALF], start=True, stop=True)
                mm.then_inc(gate_mm, 1)
            with pe.Fori(0, 4) as i:
                pair(i + V_PAIR0)
                pe.wait_ge(gate_out, GH)
                for j in range(2):
                    pe.wait_ge(taken, 2 * i + 2 * V_PAIR0 + j + 4)
                    pe.wait_ge(v_out, 2 * i + j + 1)
                    for tt in range(4):
                        nc.tensor.transpose(work[:, j, tt * P:(tt + 1) * P], stage[:, j, tt * P:(tt + 1) * P], ident[:])
                    nc.tensor.transpose(work[0:SMP, 2 + j, 0:P], stage[:, j, SEQ:T], ident[:]).then_inc(v_tr, 1)

            def att_step(s, q, k, samples=None):
                pe.wait_ge(pq_ready, s)
                for h in range(GH):
                    for c in range(NC):
                        at = h * T + c * CH
                        mm = nc.tensor.matmul(work[:, h, c * CH:(c + 1) * CH], k[:, at:at + CH], q[:, at:at + CH],
                                              start=True, stop=True)
                    mm.then_inc(att_mm, 1)
                if samples is not None:
                    pe.wait_ge(att_out, samples)
                    for h in range(GH):
                        at = h * T + SEQ
                        mm = nc.tensor.matmul(work[0:SMP, 0, h * SMP:(h + 1) * SMP], k[:, at:at + SMP],
                                              q[:, at:at + SMP], start=True, stop=True)
                    mm.then_inc(att_mm, 1)

            pair(SPILL_PAIR0)
            pe.wait_ge(v_out, 10)
            att_step(1, GQ, GKK, samples=1)
            with pe.Fori(0, 2) as i:
                pair(2 * i + SPILL_PAIR0 + 1)
                att_step(2 * i + 2, GE, GE)
                pair(2 * i + SPILL_PAIR0 + 2)
                att_step(2 * i + 3, GE2, GE2)
            for s in (5, 6, 7):
                pair(SPILL_PAIR0 + s)
                att_step(s + 1, GE if s % 2 else GE2, GE if s % 2 else GE2, samples=att_base(s) + 1)
            with pe.Fori(SPILL_PAIR0 + 8, IN_PAIRS) as i:
                pair(i)

            pe.wait_ge(kdT_ready, 1)
            pe.wait_ge(att_out, att_base(8))
            for tt in range(5):
                n = P if tt < 4 else SMP
                if tt == 4:
                    pe.wait_ge(kd_out, 1)
                for h in range(GH):
                    at = h * T + tt * P
                    mm = nc.tensor.transpose(work[0:n, tt % 4, h * GK:(h + 1) * GK], GE[:, at:at + n], ident[:])
                mm.then_inc(kd_tr, 1)
            pe.wait_ge(kd_out, 5)
            pe.wait_ge(qd_ready, 1)
            for c in range(NC):
                if c >= 1:
                    pe.wait_ge(o_out, c)
                    pe.wait_ge(S_ready, c)
                for n in range(8):
                    h, vh = n // 2, n % 2
                    region = work[:, n // 4, n % 4 * CH:(n % 4 + 1) * CH]
                    mm = nc.tensor.matmul(region, v_tok[:, c, n * P:(n + 1) * P], att[:, h * NC + c, :],
                                          start=True, stop=c == 0)
                    if c >= 1:
                        at = h * T + c * CH
                        mm = nc.tensor.matmul(region, S[:, h, vh * P:(vh + 1) * P], GQ[:, at:at + CH],
                                              start=False, stop=True)
                mm.then_inc(o_mm, 1)
                for h in range(GH):
                    mm = nc.tensor.matmul(work[:, 2 + h // 2, h % 2 * GV:(h % 2 + 1) * GV],
                                          kd_tok[:, c, h * GK:(h + 1) * GK], v_tok[:, c, h * GV:(h + 1) * GV],
                                          start=True, stop=True)
                mm.then_inc(S_mm, 1)
            pe.wait_ge(o_out, NC)
            for n in range(8):
                nc.tensor.matmul(work[:, 0, n * SMP:(n + 1) * SMP], v_tok[0:SMP, 4, n * P:(n + 1) * P],
                                 att_s[:, n // 2, :], start=n == 0, stop=False, skip_group_check=True)
            for b in range(BATCHES):
                pe.wait_ge(s0_in[b % 2], 16 * (b // 2 + 1))
                for n in range(8):
                    h, vh = n // 2, n % 2
                    at = h * T + SEQ + b * DEC
                    mm = nc.tensor.matmul(work[:, 0, n * SMP + b * DEC:n * SMP + (b + 1) * DEC],
                                          s0ring[:, b % 2, h, vh * P:(vh + 1) * P], GQ[:, at:at + DEC],
                                          start=False, stop=b == BATCHES - 1 and n == 7, skip_group_check=True)
                if b == BATCHES - 1:
                    mm.then_inc(os_mm, 1)
                pe.wait_ge(kdm_ready, b + 1)
                if b == 0:
                    pe.wait_ge(S_ready, NC)
                else:
                    pe.wait_ge(s1_ready, b)
                for h in range(GH):
                    mm = nc.tensor.matmul(work[:, 2 + h // 2, h % 2 * GV:(h % 2 + 1) * GV],
                                          kd_m[:, b % 2, h, :], v_tok[0:SMP, 4, h * GV:(h + 1) * GV],
                                          start=True, stop=True)
                mm.then_inc(s1_mm, 1)
            pe.wait_ge(os_out, 1)
            for h in range(GH):
                pe.wait_ge(gss, h + 1)
                if h >= 1:
                    pe.wait_ge(groot, h)
                sum_tokens([gsum2], 0, gsum)

            pe.wait_ge(dt_ready, 1)
            pe.wait_ge(s1_ready, BATCHES)
            for tt in range(5):
                n = P if tt < 4 else SMP
                for i, src in enumerate((dtT, cumT)):
                    mm = nc.tensor.transpose(work[0:n, 3, 32 * tt + SH * i:32 * tt + SH * (i + 1)],
                                             src[:, tt * P:tt * P + n], ident[0:SH, 0:SH])
            mm.then_inc(dttr, 1)
            pe.wait_ge(conv_out, XBC_TILES)
            pe.wait_ge(groot, GH)
            for tt in range(5):
                n = P if tt < 4 else SMP
                if tt >= 1:
                    pe.wait_ge(xdt_out, tt)
                    pe.wait_ge(b_out, tt)
                for j in range(10):
                    mm = nc.tensor.transpose(work[0:n, j // 4, j % 4 * P:(j % 4 + 1) * P],
                                             XC[:, j, tt * P:tt * P + n], ident[:])
                mm.then_inc(xtr, 1)
            pe.wait_ge(xdt_out, 5)
            pe.wait_ge(b_out, 5)
            pe.wait_ge(dtt_out, 1)
            pe.wait_ge(psel_in, 16)
            pe.wait_ge(dt_ready, 2)
            for c in range(NC):
                a, z = c * CH, (c + 1) * CH
                if c >= 1:
                    pe.wait_ge(y_out, SG * c)
                for g in range(SG):
                    nc.tensor.matmul(work[:, 2, g * CH:(g + 1) * CH], XC[:, 8 + g, a:z], XC[:, 10 + g, a:z],
                                     start=True, stop=True)
                nc.tensor.matmul(work[:, 2, 256:256 + SH], cumT[:, z - 1:z].broadcast_to([SH, P]), ident[0:SH, 0:SH],
                                 start=True, stop=True).then_inc(small_mm, 1)
                for g in range(SG):
                    k = SG * c + g
                    if k >= 1:
                        pe.wait_ge(h_ready, k)
                    for i in range(8):
                        h = 8 * g + i
                        mm = nc.tensor.matmul(work[:, i // 4, i % 4 * CH:(i % 4 + 1) * CH],
                                              ident[0:SH, h:h + 1].broadcast_to([SH, P]), cumT[:, a:z],
                                              start=True, stop=True)
                    mm.then_inc(bc_mm, 1)
                    if k >= 1:
                        pe.wait_ge(y_out, k)
                    for i in range(4):
                        j = 4 * g + i
                        mm = nc.tensor.matmul(work[:, 3, i * CH:(i + 1) * CH], psel[:, j * P:(j + 1) * P], cumT[:, a:z],
                                              start=True, stop=True)
                    mm.then_inc(e_mm, 1)
                    pe.wait_ge(small_out, c + 1)
                    for i in range(4):
                        j = 4 * g + i
                        nc.tensor.matmul(work[:, 2, i * CH:(i + 1) * CH], hT[:, j * P:(j + 1) * P], XC[:, 10 + g, a:z],
                                         start=True, stop=True)
                    pe.wait_ge(e_exp, k + 1)
                    pe.wait_ge(W_ready, k + 1)
                    for i in range(8):
                        h = 8 * g + i
                        mm = nc.tensor.matmul(work[i % 2 * SD:(i % 2 + 1) * SD, 3, i // 2 * CH:(i // 2 + 1) * CH],
                                              xdt[:, c, h * SD:(h + 1) * SD], W[:, h, :], start=True, stop=True)
                    mm.then_inc(y_mm, 1)
                    pe.wait_ge(xw_ready, c + 1)
                    nc.tensor.matmul(work[:, g, :], B_tok[:, c, g, :], xw[:, g * 512:(g + 1) * 512],
                                     start=True, stop=True).then_inc(h_mm, 1)
            pe.wait_ge(y_out, SG * NC)
            for g in range(SG):
                nc.tensor.matmul(work[0:SMP, 2, g * SMP:(g + 1) * SMP], XC[:, 8 + g, SEQ:T], XC[:, 10 + g, SEQ:T],
                                 start=True, stop=True)
            nc.tensor.matmul(work[0:SMP, 2, 256:256 + SH], lastrow, ident[0:SH, 0:SH], start=True, stop=True)
            for j in range(8):
                mm = nc.tensor.matmul(work[:, 2, 272 + j * BATCHES:272 + (j + 1) * BATCHES], psel[:, j * P:(j + 1) * P],
                                      cumT[:, SEQ + DEC - 1:T:DEC], start=True, stop=True)
            mm.then_inc(small_mm, 1)
            pe.wait_ge(h_ready, SG * NC)
            for h in range(SH):
                mm = nc.tensor.matmul(work[0:SMP, h // 8, h % 8 * SMP:(h % 8 + 1) * SMP],
                                      ident[0:SH, h:h + 1].broadcast_to([SH, SMP]), cumT[:, SEQ:T], start=True, stop=True)
            mm.then_inc(bc_mm, 1)
            for j in range(8):
                mm = nc.tensor.matmul(work[:, 3, j * SMP:(j + 1) * SMP], psel[:, j * P:(j + 1) * P], cumT[:, SEQ:T],
                                      start=True, stop=True)
            mm.then_inc(e_mm, 1)
            pe.wait_ge(e_exp, SG * NC + 1)
            pe.wait_ge(W_ready, SG * NC + 1)
            for h in range(SH):
                mm = nc.tensor.matmul(work[h % 2 * SD:(h % 2 + 1) * SD, 3, h // 2 * SMP:(h // 2 + 1) * SMP],
                                      xdt[0:SMP, 4, h * SD:(h + 1) * SD], W[0:SMP, h, 0:SMP], start=True, stop=True)
            mm.then_inc(y_mm, 1)
            pe.wait_ge(wd_exp, NC + 1)
            pe.wait_ge(small_out, NC + 1)
            pe.wait_ge(sm_ready, 1)
            for b in range(BATCHES):
                pe.wait_ge(hs_in[b % 2], 32 * (b // 2 + 1))
                for j in range(8):
                    at = j * SMP + b * DEC
                    nc.tensor.matmul(work[:, 2, at:at + DEC], hTs[:, b % 2, j * P:(j + 1) * P],
                                     XC[:, 10 + j // 4, SEQ + b * DEC:SEQ + (b + 1) * DEC], start=True, stop=True)
                if b >= 1:
                    pe.wait_ge(hs_ready, b)
                for j in range(8):
                    mm = nc.tensor.matmul(work[:, j // 4, j % 4 * SN:(j % 4 + 1) * SN], xw[0:SMP, j * P:(j + 1) * P],
                                          Bm[:, b, j // 4, :], start=True, stop=True)
                mm.then_inc(hs_mm, 1)
            pe.wait_ge(y_out, SG * NC + 1)
            pe.wait_ge(hs_ready, BATCHES)
            for g in range(SG):
                pe.wait_ge(ysq_r, g + 1)
                sum_tokens([ysq[:, i] for i in range(4)], 2 * g, ysum)

            pe.wait_ge(mix_in, 12)
            with pe.Fori(IN_PAIRS, IN_PAIRS + OUT_PAIRS) as i:
                pair(i)
            pe.wait_ge(sq_free, KT + 2)
            sum_tokens([sqsum], 0, msum_mm)
            pe.wait_ge(mroot, 1)

            def h_arrives(kt):
                pe.wait_ge(hsq, kt + 1)
                sum_tokens([sq[kt % 2]], 0, hsq_mm, kt == 0, kt == KT - 1)
                pe.wait_ge(h_split, kt + 1)

            def up(tile, unit, before=None):
                for j in range(4):
                    project(tile + j, unit + 2 * j, (2 + 2 * j) % 4, (1 + j) % 2, split=256, before=before if j == 0 else None)

            def down(blk, q, tile, unit):
                pe.wait_ge(act_ready, 2 * blk + 2)
                for d in range(KT):
                    if d % 4 == 0:
                        pe.wait_ge(lo_ready, unit + d // 4 + 1)
                    pe.wait_ge(taken, tile + d + 1)
                    for k in range(2):
                        mm = products((2 + d // 4) % 4, d % 4 * 2 + k, (1 + d) % 2, HALF, k == 0, k == 1,
                                      g_hi[:, q, k], g_lo[:, q, k])
                    mm.then_inc(units_done if d % 4 == 3 else down_mm, 1)

            up(FFN_TILE0, FFN_UNIT0, before=h_arrives)
            with pe.Fori(0, (BLOCKS - 2) // 2) as i:
                for q in (1, 0):
                    b = 1 if q else 2
                    tile, unit = FFN_TILE0 - 16 + 20 * b, FFN_UNIT0 - 4 + 12 * b
                    up(40 * i + tile, 24 * i + unit)
                    down(2 * i + b - 1, 1 - q, 40 * i + tile + 4, 24 * i + unit + 8)
            tile, unit = FFN_TILE0 - 16 + 20 * (BLOCKS - 1), FFN_UNIT0 - 4 + 12 * (BLOCKS - 1)
            up(tile, unit)
            down(BLOCKS - 2, 0, tile + 4, unit + 8)
            down(BLOCKS - 1, 1, tile + 20, unit + 12)
            for kt in range(KT):
                pe.wait_ge(ysq2, kt + 1)
                sum_tokens([fsq[kt % 2]], 0, ysq_mm, kt == 0, kt == KT - 1)

        @block.vector
        def _(ve):
            steps = [0]

            def own(instruction):
                instruction.then_inc(own_step, 1)
                steps[0] += 1

            def settle():
                ve.wait_ge(own_step, steps[0])

            tt_op, ts_op, stt = nc.vector.tensor_tensor, nc.vector.tensor_scalar, nc.vector.scalar_tensor_tensor

            nc.vector.memset(ones[:], 1.0).then_inc(setup, 1)
            nc.vector.memset(att, 0.0).then_inc(taken, 2)
            nc.vector.memset(att_s, 0.0).then_inc(v_out, 2)
            own(nc.vector.memset(reset[:], 1.0))
            settle()
            nc.vector.memset(reset[:, 0:SEQ:CH], 0.0).then_inc(pq_ready, 1)
            own(nc.vector.memset(reset[:, SEQ:T:DEC], 0.0))
            ve.wait_ge(const_in, 48)
            own(nc.vector.tensor_copy(masks[:], masks_f))
            for kt in range(KT):
                x = xin[kt // 4 % 2][:, kt % 4 * T:(kt % 4 + 1) * T]
                ve.wait_ge(x_in[kt // 4 % 2], 16 * (kt // 8 + 1))
                ts_op(x_hi[:, kt], x, V("mix_pre", kt), None, ALU.mult).then_inc(x_hi_w, 1)
                ve.wait_ge(x_hi_w, kt + 1)
                stt(x_lo[:, kt], x, V("mix_pre", kt), x_hi[:, kt].bitcast(F32), ALU.mult, ALU.subtract)\
                    .then_inc(x_split, 1)
            ve.wait_ge(root_ready, 1)
            nc.vector.reciprocal(rstd[:], rstd[:]).then_inc(rstd_ready, 1)
            ve.wait_ge(rstd_ready, 1)

            def take(tile, out):
                ve.wait_ge(units_done, 2 * tile + 2)
                tt_op(halves(out), proj(ring_of(tile)), halves(rstd[:]), ALU.mult).then_inc(taken, 1)

            def ring_of(tile):
                return tile % 2

            take(0, misc[:])
            for tile in range(1, 1 + 2 * V_PAIR0):
                h = (tile - 1) % GH
                if tile <= GH:
                    ve.wait_ge(units_done, 2 * tile + 2)
                    stt(halves(GQ[:, h * T:(h + 1) * T]), proj(tile % 2), GK ** -0.5, halves(rstd[:]), ALU.mult, ALU.mult)\
                        .then_inc(taken, 1)
                else:
                    take(tile, GKK[:, h * T:(h + 1) * T])
            ve.wait_ge(gate_out, GH)
            own(ts_op(GB, GE, 0.0, None, ALU.min))
            settle()
            stt(GE2, GB, 2.0, GE, ALU.mult, ALU.subtract).then_inc(gate_sub, 1)
            ve.wait_ge(gate_ln, 1)
            own(tt_op(GE, GB, GE2, ALU.subtract))
            settle()
            for h in range(GH):
                i = nc.vector.tensor_tensor_scan(GB[:, h * T:(h + 1) * T], reset[:], GE[:, h * T:(h + 1) * T],
                                                 0.0, ALU.mult, ALU.add)
            i.then_inc(b_ready, 1)
            tile0 = 1 + 2 * V_PAIR0
            for n in range(8):
                if n >= 2:
                    ve.wait_ge(v_tr, n - 1)
                take(tile0 + n, stage[:, n % 2])
            ve.wait_ge(b_ready, 1)

            def chunk_view(buf, m):
                if m <= DEC // 2:
                    v = buf.rearrange("p (n u m) -> p n u m", u=2, m=m)
                    return v[:, :, 0], v[:, :, 1]
                v = buf.rearrange("p (h t) -> p h t", h=GH)[:, :, 0:SEQ].rearrange("p h (n u m) -> p h n u m", u=2, m=m)
                return v[:, :, :, 0], v[:, :, :, 1]

            def take_att(s):
                for h in range(GH):
                    ve.wait_ge(att_mm, att_base(s) + h + 1)
                    nc.vector.copy_predicated(att[:, h * NC:(h + 1) * NC, :], masks[:, s:s + 1, :].broadcast_to([P, NC, P]),
                                              work[:, h, :].rearrange("p (c t) -> p c t", c=NC)).then_inc(att_out, 1)
                if s in SAMPLE_STEPS:
                    ve.wait_ge(att_mm, att_base(s + 1))
                    nc.vector.copy_predicated(att_s, masks[0:SMP, s:s + 1, 0:SMP].broadcast_to([SMP, GH, SMP]),
                                              work[0:SMP, 0, 0:GH * SMP].rearrange("p (h t) -> p h t", h=GH))\
                        .then_inc(att_out, 1)

            def operands(s):
                m = LEVELS[s - 1]
                buf = GE if s % 2 else GE2
                (k_out, q_out), (k_b, q_b) = chunk_view(buf, m), chunk_view(GB, m)
                ref = k_b[..., m - 1:m].broadcast_to(list(k_b.shape))
                if s >= 3:
                    ve.wait_ge(att_mm, att_base(s - 1))
                tt_op(k_out, ref, k_b, ALU.subtract)
                tt_op(q_out, q_b, ref, ALU.subtract).then_inc(sub_ready, 1)
                ve.wait_ge(exp_ready, s)
                tt_op(k_out, k_out, chunk_view(GKK, m)[0], ALU.mult)
                tt_op(q_out, q_out, chunk_view(GQ, m)[1], ALU.mult).then_inc(pq_ready, 1)

            ve.wait_ge(v_tr, 8)
            for s in range(8):
                if s >= 1:
                    take_att(s - 1)
                    operands(s)
                for j in range(2):
                    n = 2 * s + j
                    if s >= 1:
                        ve.wait_ge(spilled[j], 16 * s)
                    take(1 + 2 * SPILL_PAIR0 + n, stage[:, j])
            take_att(7)
            with ve.Fori(8, SPILLED // 2) as i:
                for j in range(2):
                    ve.wait_ge(spilled[j], 16 * i)
                    ve.wait_ge(units_done, 4 * i + 2 * j + 4 * SPILL_PAIR0 + 4)
                    tt_op(halves(stage[:, j]), proj((1 + j) % 2), halves(rstd[:]), ALU.mult).then_inc(taken, 1)

            ve.wait_ge(att_mm, att_base(8))
            for lo, hi, n in ((0, SEQ, CH), (SEQ, T, DEC)):
                def v(buf):
                    return buf.rearrange("p (h t) -> p h t", h=GH)[:, :, lo:hi].rearrange("p h (c t) -> p h c t", t=n)
                b = v(GB)
                i = tt_op(v(GE), b[..., n - 1:n].broadcast_to(list(b.shape)), b, ALU.subtract)
            i.then_inc(sub_ready, 1)
            ve.wait_ge(exp_ready, 8)
            tt_op(GE, GE, GKK, ALU.mult).then_inc(kdT_ready, 1)
            ve.wait_ge(exp_ready, 9)
            e = GE2.rearrange("p (h t) -> p h t", h=GH)
            tt_op(GQ, GQ, GE2, ALU.mult)
            nc.vector.tensor_copy(gdecay[:, :, 0:NC], e[:, :, CH - 1:SEQ:CH])
            nc.vector.tensor_copy(gdecay[:, :, NC:NC + BATCHES], e[:, :, SEQ + DEC - 1:T:DEC]).then_inc(qd_ready, 1)
            ve.wait_ge(qd_ready, 1)
            for c in range(NC):
                ve.wait_ge(S_mm, c + 1)
                if c >= 1:
                    ve.wait_ge(S_ready, c)
                for h in range(GH):
                    inc = work[:, 2 + h // 2, h % 2 * GV:(h % 2 + 1) * GV]
                    if c == 0:
                        i = nc.vector.tensor_copy(S[:, h, :], inc)
                    else:
                        i = stt(S[:, h, :], S[:, h, :], gdecay[:, h, c:c + 1], inc, ALU.mult, ALU.add)
                i.then_inc(S_ready, 1)
            ve.wait_ge(o_mm, NC)

            def masked_keys(b):
                if b >= 2:
                    ve.wait_ge(s1_mm, b - 1)
                ts_op(kd_m[:, b % 2].rearrange("p h k -> p (h k)"), kd_tok[0:SMP, 4, :], V("batch", b, SMP), None, ALU.mult)\
                    .then_inc(kdm_ready, 1)

            masked_keys(0)
            masked_keys(1)
            for b in range(BATCHES):
                ve.wait_ge(s1_mm, b + 1)
                ve.wait_ge(s0_in[b % 2], 16 * (b // 2 + 1))
                for h in range(GH):
                    s = s0ring[:, b % 2, h, :]
                    i = stt(s, s, gdecay[:, h, NC + b:NC + b + 1], work[:, 2 + h // 2, h % 2 * GV:(h % 2 + 1) * GV],
                            ALU.mult, ALU.add)
                i.then_inc(s1_ready, 1)
                if b + 2 < BATCHES:
                    masked_keys(b + 2)
            for h in range(GH):
                ve.wait_ge(gsq, h + 1)
                if h >= 1:
                    ve.wait_ge(gsum, h)
                tt_op(gsum2, GE[:, 0:T], GE[:, T:2 * T], ALU.add).then_inc(gss, 1)
            for h in range(GH):
                ve.wait_ge(groot, h + 1)
                r = GQ[:, h * T:(h + 1) * T]
                nc.vector.reciprocal(r, r).then_inc(grs, 1)
            for h in range(GH):
                ve.wait_ge(grs, h + 1)
                r = GQ[:, h * T:(h + 1) * T]
                for vh in range(2):
                    o = oT[:, 2 * h + vh]
                    i = stt(o, o, V("gla_norm", vh), r, ALU.mult, ALU.mult)
                own(i)
                settle()
                ve.wait_ge(gsilu, h + 1)
                o = oT[:, 2 * h:2 * h + 2]
                tt_op(o, o, gT[:, 2 * h:2 * h + 2], ALU.mult).then_inc(gy, 1)
            for h in range(GH):
                ve.wait_ge(ghi, h + 1)
                tt_op(x_lo[:, 2 * h:2 * h + 2], oT[:, 2 * h:2 * h + 2], x_hi[:, 2 * h:2 * h + 2].bitcast(F32), ALU.subtract)\
                    .then_inc(mix_in, 1)

            for j in range(2):
                ve.wait_ge(s0_out[j], 16 * BATCHES // 2)
            ve.wait_ge(gla_p_out, 16)
            ve.wait_ge(gsum, GH)
            own(ts_op(dtT, dtT, V("dt_bias", rows=SH), None, ALU.add))
            nc.vector.memset(pad[0][:, 0:SC - 1], 0.0)
            nc.vector.memset(pad[1][:, 0:SC - 1], 0.0).then_inc(pad_zero, 1)
            nc.vector.memset(hT, 0.0)
            own(nc.vector.memset(cbm, 0.0))
            settle()
            e, z, z2, acc_t = dt_tmp
            own(ts_op(z, dtT, 0.0, None, ALU.min))
            settle()
            stt(e, z, 2.0, dtT, ALU.mult, ALU.subtract).then_inc(dts, 1)
            ve.wait_ge(dte, 1)
            own(ts_op(z, e, 2.0, None, ALU.add))
            settle()
            own(nc.vector.reciprocal(z, z))
            settle()
            own(tt_op(z, z, e, ALU.mult))
            settle()
            own(tt_op(z2, z, z, ALU.mult))
            settle()
            own(ts_op(acc_t, z2, 1.0 / 15, None, ALU.mult))
            for n in (13, 11, 9, 7, 5, 3):
                settle()
                own(stt(acc_t, acc_t, 1.0 / n, z2, ALU.add, ALU.mult))
            settle()
            own(stt(acc_t, acc_t, 1.0, z, ALU.add, ALU.mult))
            own(ts_op(dtT, dtT, 0.0, None, ALU.max))
            settle()
            own(stt(dtT, acc_t, 2.0, dtT, ALU.mult, ALU.add))
            settle()
            own(ts_op(e, dtT, V("A_log", rows=SH), -1.0, ALU.mult, ALU.mult))
            settle()
            nc.vector.tensor_tensor_scan(cumT, reset[0:SH, :], e, 0.0, ALU.mult, ALU.add).then_inc(dt_ready, 1)
            ve.wait_ge(dt_ready, 1)
            c8 = cumT[:, SEQ:T].rearrange("p (b t) -> p b t", b=BATCHES)
            nc.vector.tensor_copy(lastrow.rearrange("p (b t) -> p b t", b=BATCHES),
                                  c8[:, :, DEC - 1:DEC].broadcast_to([SH, BATCHES, DEC])).then_inc(dt_ready, 1)
            ve.wait_ge(dttr, 1)
            nc.vector.tensor_copy(tok[:, 0:4, 0:32], work[:, 3, 0:128].rearrange("p (t c) -> p t c", t=4))
            nc.vector.tensor_copy(tok[0:SMP, 4, 0:32], work[0:SMP, 3, 128:160]).then_inc(dtt_out, 1)
            for n in range(XBC_TILES):
                q, o = pad[n % 2], conv_t[n % 2][:, 0:CONVW]
                ve.wait_ge(tap0, n + 1)
                for t in range(1, SC):
                    if t > 1:
                        settle()
                    i = stt(o, q[:, t:t + CONVW], V("conv_w", 4 * n + t), o, ALU.mult, ALU.add)
                    if t < SC - 1:
                        own(i)
                i.then_inc(taps, 1)
            ve.wait_ge(dtt_out, 1)
            for tt in range(5):
                n = P if tt < 4 else SMP
                ve.wait_ge(xtr, tt + 1)
                tt_op(xdt[0:n, tt].rearrange("p (h d) -> p h d", h=SH),
                      work[0:n, 0:2, :].rearrange("p a (h d) -> p (a h) d", d=SD),
                      tok[0:n, tt, 0:SH].unsqueeze(2).broadcast_to([n, SH, SD]), ALU.mult).then_inc(xdt_out, 1)
            for j in range(8):
                i = ts_op(XC[:, j], XC[:, j], V("ssd_D", j), None, ALU.mult)
            own(i)
            ve.wait_ge(xdt_out, 5)
            settle()

            def small(c, n, cols, mask):
                ve.wait_ge(small_mm, c + 1)
                nc.vector.copy_predicated(cbm[0:n, :, 0:cols], masks[0:n, mask:mask + 1, 0:cols].broadcast_to([n, SG, cols]),
                                          work[0:n, 2, 0:SG * cols].rearrange("p (g t) -> p g t", g=SG))
                last = work[0:n, 2, 256:256 + SH]
                tt_op(tok[0:n, c, 32:48], last, tok[0:n, c, 16:32], ALU.subtract)
                nc.vector.tensor_copy(tok[0:n, c, 48:64], last).then_inc(small_out, 1)

            def decayed_x(c, n):
                ve.wait_ge(wd_exp, c + 1)
                if c >= 1:
                    ve.wait_ge(h_mm, SG * c)
                tt_op(xw[0:n].rearrange("p (h d) -> p h d", h=SH), xdt[0:n, c].rearrange("p (h d) -> p h d", h=SH),
                      tok[0:n, c, 32:48].unsqueeze(2).broadcast_to([n, SH, SD]), ALU.mult).then_inc(xw_ready, 1)

            def exponents(k, w, cum_s, n):
                ve.wait_ge(bc_mm, k + 1)
                own(tt_op(w, cum_s.unsqueeze(2).broadcast_to(list(w.shape)),
                          work[0:n, 0:2, :].rearrange("p a (h t) -> p (a h) t", t=w.shape[-1]), ALU.subtract))
                settle()
                ts_op(w, w, 0.0, None, ALU.max).then_inc(D_ready, 1)

            for c in range(NC):
                small(c, P, CH, MASK_TRI)
                for g in range(SG):
                    k = SG * c + g
                    w = W[:, 8 * g:8 * g + 8, :]
                    if k >= 2:
                        ve.wait_ge(y_mm, k - 1)
                    exponents(k, w, tok[:, c, 16 + 8 * g:24 + 8 * g], P)
                    if g == 0:
                        decayed_x(c, P)
                    ve.wait_ge(W_exp, k + 1)
                    tt_op(w, w, cbm[:, g:g + 1, :].broadcast_to([P, 8, CH]), ALU.mult).then_inc(W_ready, 1)
                    ve.wait_ge(y_mm, k + 1)
                    ve.wait_ge(e_exp, k + 1)
                    own(tt_op(yt, work[:, 2, :], ecum, ALU.mult))
                    settle()
                    own(tt_op(yt, work[:, 3, :], yt, ALU.add))
                    settle()
                    y = XC[:, 4 * g:4 * g + 4, c * CH:(c + 1) * CH]
                    tt_op(y, y, yt.rearrange("p (j t) -> p j t", j=4), ALU.add).then_inc(y_out, 1)
                    hh = hT[:, g * 512:(g + 1) * 512]
                    own(tt_op(hh.rearrange("p (h d) -> p h d", h=8), hh.rearrange("p (h d) -> p h d", h=8),
                              tok[:, c, 48 + 8 * g:56 + 8 * g].unsqueeze(2).broadcast_to([P, 8, SD]), ALU.mult))
                    settle()
                    ve.wait_ge(h_mm, k + 1)
                    tt_op(hh, work[:, g, :], hh, ALU.add).then_inc(h_ready, 1)
            ve.wait_ge(W_ready, SG * NC)
            own(nc.vector.memset(cbm[0:SMP], 0.0))
            settle()
            small(NC, SMP, SMP, MASK_TRI_S)
            ve.wait_ge(y_mm, SG * NC)
            exponents(SG * NC, W[0:SMP, :, 0:SMP], tok[0:SMP, NC, 16:32], SMP)
            decayed_x(NC, SMP)
            ve.wait_ge(W_exp, SG * NC + 1)
            for g in range(SG):
                w = W[0:SMP, 8 * g:8 * g + 8, 0:SMP]
                i = tt_op(w, w, cbm[0:SMP, g:g + 1, 0:SMP].broadcast_to([SMP, 8, SMP]), ALU.mult)
            i.then_inc(W_ready, 1)
            ve.wait_ge(y_mm, SG * NC + 1)
            ve.wait_ge(b_out, 5)
            for b in range(BATCHES):
                i = ts_op(Bm[:, b].rearrange("p g n -> p (g n)"), B_tok[0:SMP, 4].rearrange("p g n -> p (g n)"),
                          V("batch", b, SMP), None, ALU.mult)
            i.then_inc(sm_ready, 1)
            el2 = decay[:].rearrange("p (j b) -> p j b", j=8)
            for b in range(BATCHES):
                ve.wait_ge(hs_in[b % 2], 32 * (b // 2 + 1))
                ve.wait_ge(wd_exp, NC + 1)
                own(tt_op(hns[:, b % 2], hns[:, b % 2], el2[:, :, b:b + 1].broadcast_to([P, 8, SN]), ALU.mult))
                settle()
                ve.wait_ge(hs_mm, b + 1)
                tt_op(hns[:, b % 2], work[:, 0:2, :].rearrange("p a (j n) -> p (a j) n", j=4), hns[:, b % 2], ALU.add)\
                    .then_inc(hs_ready, 1)
            own(tt_op(yt, work[:, 2, :], ecum, ALU.mult))
            settle()
            own(tt_op(yt, work[:, 3, :], yt, ALU.add))
            settle()
            y = XC[:, 0:8, SEQ:T]
            tt_op(y, y, yt.rearrange("p (j t) -> p j t", j=8), ALU.add).then_inc(y_out, 1)
            ve.wait_ge(y_out, SG * NC + 1)
            ve.wait_ge(zsilu, 1)
            tt_op(XC[:, 0:8], XC[:, 0:8], zT, ALU.mult).then_inc(yz, 1)
            ve.wait_ge(yroot, SG)
            own(nc.vector.reciprocal(zT[:, 0:2], zT[:, 0:2]))
            settle()
            for j in range(8):
                stt(XC[:, j], XC[:, j], V("ssd_norm", j), zT[:, j // 4], ALU.mult, ALU.mult).then_inc(ymix, 1)
            for j in range(8):
                ve.wait_ge(yhi, j + 1)
                tt_op(x_lo[:, 8 + j], XC[:, j], x_hi[:, 8 + j].bitcast(F32), ALU.subtract).then_inc(mix_in, 1)

            nc.vector.memset(sqsum, 0.0).then_inc(sq_free, 2)
            ve.wait_ge(mix_in, 12)
            with ve.Fori(0, OUT_PAIRS) as i:
                for j in range(2):
                    ve.wait_ge(units_done, 4 * i + 2 * j + OUT_UNIT0 + 2)
                    ts_op(mixT[:, bass.ds(2 * i + j, 1), :].rearrange("p o (n t) -> p (o n) t", n=2), proj((1 + j) % 2),
                          1.0, None, ALU.mult).then_inc(taken, 1)
                for j in range(2):
                    ve.wait_ge(msq, 2 * i + j + 1)
                    ve.wait_ge(sq_free, 2 * i + j + 2)
                    tt_op(sqsum, sqsum, sq[j], ALU.add).then_inc(sq_free, 1)
            ve.wait_ge(mroot, 1)
            own(nc.vector.reciprocal(rstd[:], rstd[:]))
            settle()

            def h_lo(kt):
                ve.wait_ge(h_hi, kt + 1)
                stt(x_lo[:, kt], mixT[:, kt], V("ffn_pre", kt), x_hi[:, kt].bitcast(F32), ALU.mult, ALU.subtract)\
                    .then_inc(h_split, 1)

            for kt in range(KT):
                own(stt(mixT[:, kt], mixT[:, kt], V("mix_post", kt), rstd[:], ALU.mult, ALU.mult))
                if kt >= 1:
                    h_lo(kt - 1)
                settle()
                ve.wait_ge(xr_in[kt // 4], 32 if kt >= 12 else 16)
                tt_op(mixT[:, kt], mixT[:, kt], xres(kt), ALU.add).then_inc(h_w, 1)
            h_lo(KT - 1)
            nc.vector.memset(fpad[0][:, 0:FC - 1], 0.0)
            nc.vector.memset(fpad[1][:, 0:FC - 1], 0.0).then_inc(fpad_zero, 1)
            ve.wait_ge(mroot, 2)
            own(nc.vector.reciprocal(rstd[:], rstd[:]))
            settle()

            def take_up(t, j, unit, first=False):
                pd, r = fpad[j % 2], (1 + j) % 2
                ve.wait_ge(units_done, unit + 2 * j + 2)
                if not (first and j < 2):
                    ve.wait_ge(f_padout, t - 1)
                tt_op(pd[:, FC - 1:FC - 1 + SEQ].rearrange("p (n t) -> p n t", n=2), psum_proj[:, 2 * r:2 * r + 2, 0:256],
                      rstd[:, 0:SEQ].rearrange("p (n t) -> p n t", n=2), ALU.mult)
                tt_op(pd[:, FC - 1 + SEQ:].rearrange("p (b t) -> p b t", b=BATCHES)[:, :, FC - 1:],
                      psum_proj[:, 2 * r + 1, 256:320].rearrange("p (b t) -> p b t", b=BATCHES),
                      rstd[:, SEQ:T].rearrange("p (b t) -> p b t", b=BATCHES), ALU.mult).then_inc(taken, 1)

            def taps_of(t, j, q):
                pd, o = fpad[j % 2], ftap[j % 2][:, 0:FCONVW]
                ve.wait_ge(f_tap0, t + 1)
                stt(o, pd[:, 1:1 + FCONVW], fc[q][:, 4 * j + 1:4 * j + 2], o, ALU.mult, ALU.add).then_inc(f_tap1, 1)
                ve.wait_ge(f_tap1, t + 1)
                stt(o, pd[:, 2:2 + FCONVW], fc[q][:, 4 * j + 2:4 * j + 3], o, ALU.mult, ALU.add).then_inc(f_taps, 1)

            def gate_product(pair):
                ve.wait_ge(f_silu, pair + 1)
                ve.wait_ge(f_taps, 2 * pair + 2)
                tt_op(fgate[:, 0:SEQ], fgate[:, 0:SEQ], ftap[1][:, 0:SEQ], ALU.mult)
                g8 = fgate[:, SEQ:T].rearrange("p (b t) -> p b t", b=BATCHES)
                tt_op(g8, g8, ftap[1][:, SEQ + FC - 1:FPADW].rearrange("p (b t) -> p b t", b=BATCHES)[:, :, 0:DEC],
                      ALU.mult).then_inc(f_prod, 1)

            def gate_lo(pair, q, i):
                ve.wait_ge(f_hi, pair + 1)
                tt_op(g_lo[:, q, i], fgate, g_hi[:, q, i].bitcast(F32), ALU.subtract).then_inc(act_ready, 1)

            def take_down(d, unit, count):
                if d % 4 == 3:
                    ve.wait_ge(units_done, unit + d // 4 + 1)
                else:
                    ve.wait_ge(down_mm, count + 3 * (d // 4) + d % 4 + 1)
                a = halves(acc[:, d])
                tt_op(a, proj((1 + d) % 2), a, ALU.add).then_inc(taken, 1)

            def block_up(blk, q, unit, first=False):
                t = 4 * blk
                take_up(t, 0, unit, first)
                taps_of(t, 0, q)
                take_up(t + 1, 1, unit, first)
                taps_of(t + 1, 1, q)
                gate_product(2 * blk)
                gate_lo(2 * blk, q, 0)
                take_up(t + 2, 2, unit)
                taps_of(t + 2, 2, q)
                take_up(t + 3, 3, unit)

            def block_end(blk, q, step):
                if step == 0:
                    taps_of(4 * blk + 3, 3, q)
                elif step == 1:
                    gate_product(2 * blk + 1)
                else:
                    gate_lo(2 * blk + 1, q, 1)

            def block(blk, q, unit, tile):
                block_up(blk, q, unit)
                ve.wait_ge(taken, tile + 4 + 2)
                for d in range(KT):
                    take_down(d, unit + 8, 12 * blk - 12)
                    if d in (1, 4, 7):
                        block_end(blk, q, (1, 4, 7).index(d))

            block_up(0, 0, FFN_UNIT0, first=True)
            for s in range(3):
                block_end(0, 0, s)
            ve.wait_ge(h_st, 16)
            nc.vector.memset(acc.rearrange("p n t -> p (n t)"), 0.0).then_inc(acc_zero, 1)
            ve.wait_ge(acc_zero, 1)
            with ve.Fori(0, (BLOCKS - 2) // 2) as i:
                for q in (1, 0):
                    b = 1 if q else 2
                    block(2 * i + b, q, 24 * i + FFN_UNIT0 - 4 + 12 * b, 40 * i + FFN_TILE0 - 16 + 20 * b)
            b = BLOCKS - 1
            unit, tile = FFN_UNIT0 - 4 + 12 * b, FFN_TILE0 - 16 + 20 * b
            block(b, 1, unit, tile)
            ve.wait_ge(taken, tile + 20 + 2)
            for d in range(KT):
                take_down(d, unit + 12, 12 * b)
            ve.wait_ge(mroot, 3)
            own(nc.vector.reciprocal(rstd[:], rstd[:]))
            settle()
            ve.wait_ge(taken, tile + 36 + 2)
            ve.wait_ge(h_back, 16)
            hb = x_hi[:].bitcast(F32)
            for kt in range(KT):
                own(stt(acc[:, kt], acc[:, kt], V("ffn_post", kt), rstd[:], ALU.mult, ALU.mult))
                settle()
                tt_op(acc[:, kt], acc[:, kt], hb[:, kt], ALU.add).then_inc(y_w, 1)


def _tiles(rows):
    return np.swapaxes(rows.reshape((-1, P) + rows.shape[1:]), 0, 1)


def _weights(w_in, w_out, f_in, f_out):
    cut = np.cumsum([0, GH * GK, GH * GK, GH * GV, GH * GV, RANK, SH * SD, SH * SD + 2 * SG * SN, SH])
    q, k, v, g, lr, z, xbc, dt = (np.arange(cut[i], cut[i + 1]) for i in range(8))
    cols = np.concatenate([dt, q[:16], lr, q[:80], q, k, v, xbc, g, z])

    def by_tile(w):
        return w.reshape(2, 8, P, -1, P).transpose(3, 0, 2, 1, 4).reshape(-1, P, 8, P)

    up = by_tile(f_in).reshape(2, BLOCKS, 4, P, 8, P)
    up = up.reshape(2, BLOCKS, 2, 2, P, 8, P).transpose(1, 2, 0, 3, 4, 5, 6).reshape(BLOCKS, 8, P, 8, P)
    down = f_out.reshape(BLOCKS, 2, P, 4, 4, P).transpose(0, 3, 2, 4, 1, 5).reshape(BLOCKS, 4, P, 8, P)
    ffn = [up[0]]
    for b in range(1, BLOCKS):
        ffn += [up[b], down[b - 1]]
    return np.concatenate([by_tile(w_in[:, cols]), by_tile(w_out)] + ffn + [down[BLOCKS - 1]])


def _masks():
    s, t = np.arange(P)[:, None], np.arange(P)[None, :]
    levels = [(s // (2 * m) == t // (2 * m)) & (s % (2 * m) < m) & (t % (2 * m) >= m) for m in LEVELS]
    return np.stack([s == t] + levels + [s <= t, (s <= t) & (s // DEC == t // DEC)], axis=1).astype(np.float32)


def _ffn_channels(a):
    a = a.reshape((2, BLOCKS, 2, P) + a.shape[1:])
    return np.moveaxis(np.swapaxes(a, 0, 1).swapaxes(1, 2).reshape((BLOCKS, 4, P) + a.shape[4:]), 2, 0)


def _ffn_channels_back(a):
    a = np.moveaxis(a, 0, 2).reshape((BLOCKS, 2, 2, P) + a.shape[3:])
    return np.swapaxes(a, 1, 2).swapaxes(0, 1).reshape((2 * F,) + a.shape[4:])


def kernel(**inputs):
    from concourse import bacc as _bacc
    from concourse.bass_utils import run_bass_kernel_spmd as _run

    a = {k: np.asarray(v) for k, v in inputs.items()}
    x = np.concatenate([a["x_prompt"].reshape(SEQ, D), a["x_sample"].reshape(SMP, D)])
    f32 = x.dtype
    col = {k: a[k][0].reshape(-1, P).T for k in ("norm_mix_pre", "norm_mix_post", "norm_ffn_pre", "norm_ffn_post",
                                                 "gla_norm", "ssd_conv_b", "ssd_norm")}
    pad_rows = lambda v: np.concatenate([v, np.zeros(P - len(v), f32)])[:, None]
    batch_mask = np.zeros((P, BATCHES), f32)
    batch_mask[np.arange(SMP), np.arange(SMP) // DEC] = 1
    vecs = np.concatenate([
        col["norm_mix_pre"], col["norm_mix_post"], col["norm_ffn_pre"], col["norm_ffn_post"],
        a["gla_b_gate"][0].reshape(-1, P).T, col["gla_norm"],
        _tiles(a["ssd_conv_w"][0].T).reshape(P, -1), col["ssd_conv_b"],
        np.repeat(a["ssd_D"][0], SD).reshape(-1, P).T, col["ssd_norm"],
        pad_rows(a["ssd_dt_bias"][0]), pad_rows(a["ssd_A_log"][0]), np.full((P, 1), EPS, f32), batch_mask], axis=1)
    psel = np.repeat(np.eye(SH, dtype=f32), SD, axis=1)
    fvec = np.concatenate([a["ffn_conv_w"][0], a["ffn_conv_b"]]).T
    ssd = a["state_ssd"][0].reshape(BATCHES, SH * SD, SN)
    arrays = [
        ("xT", _tiles(x.T).reshape(P, 4, 4 * T).swapaxes(0, 1)),
        ("weights", _weights(a["w_in"][0], a["w_out"][0], a["ffn_w_in"][0], a["ffn_w_out"][0])),
        ("vecs", vecs),
        ("ident", np.eye(P, dtype=f32)),
        ("masks", _masks()),
        ("psel", psel),
        ("gate2", a["gla_w_gate2"][0]),
        ("sconv_in", _tiles(a["state_ssd_conv"][0].transpose(2, 0, 1))),
        ("fconv_in", _ffn_channels(a["state_ffn_conv"][0].transpose(2, 0, 1)).reshape(P, BLOCKS, -1)),
        ("fvec", _ffn_channels(fvec).reshape(P, BLOCKS, -1)),
        ("gla_in", a["state_gla"][0].transpose(2, 0, 1, 3).reshape(GK, -1, GV)),
        ("ssdT_in", ssd.transpose(2, 0, 1)),
        ("ssd_in", ssd.reshape(BATCHES, 8, P, SN).transpose(2, 0, 1, 3)),
    ]
    outs = [("yT", (4, P, 4, T)), ("gla_p", (P, GH, GV)), ("ssd_p", (SN, SH * SD)), ("sconv_out", (P, XBC_TILES, 27)),
            ("fconv_out", (P, BLOCKS, 72)), ("gla_s", (P, BATCHES * GH, GV)), ("ssd_s", (P, BATCHES, 8, SN))]
    nc = _bacc.Bacc("TRN2", target_bir_lowering=False, num_devices=1)
    fed, args = {}, []
    for name, v in arrays:
        v = np.ascontiguousarray(v)
        fed[f"in_{name}_dram"] = v
        args.append(nc.dram_tensor(f"in_{name}_dram", v.shape, mybir.dt.from_np(v.dtype), kind="ExternalInput").ap())
    for name, shape in outs:
        args.append(nc.dram_tensor(f"out_{name}_dram", shape, F32, kind="ExternalOutput").ap())
    build(nc, *args)
    r = _run(nc, [fed], core_ids=[0])
    o = {name: np.asarray(r.results[0][f"out_{name}_dram"]).reshape(shape) for name, shape in outs}
    y = o["yT"].swapaxes(0, 1).reshape(P, KT, T).transpose(2, 1, 0).reshape(T, D)
    sconv = o["sconv_out"].transpose(2, 1, 0).reshape(27, -1)
    fconv = _ffn_channels_back(o["fconv_out"].reshape(P, BLOCKS, 4, 18)).T
    return (y[:SEQ].reshape(1, SEQ, D), y[SEQ:].reshape(BATCHES, DEC, D),
            o["gla_p"].transpose(1, 0, 2).reshape(1, 1, GH, GK, GV),
            o["ssd_p"].T.reshape(1, 1, SH, SD, SN),
            sconv[:SC - 1].reshape(1, 1, SC - 1, -1),
            fconv[:FC - 1].reshape(1, 1, FC - 1, -1),
            o["gla_s"].reshape(GK, BATCHES, GH, GV).transpose(1, 2, 0, 3)[None],
            o["ssd_s"].transpose(1, 2, 0, 3).reshape(1, BATCHES, SH, SD, SN),
            sconv[SC - 1:].reshape(1, BATCHES, SC - 1, -1),
            fconv[FC - 1:].reshape(1, BATCHES, FC - 1, -1))
```

```python
from contextlib import ExitStack

import numpy as np

import concourse.bass as bass
from concourse import mybir

F32 = mybir.dt.float32
F32R = mybir.dt.float32r
U8 = mybir.dt.uint8
ALU = mybir.AluOpType
ACT = mybir.ActivationFunctionType

P = 128
D = 2048
SEQ, BATCHES, DEC = 512, 8, 8
SMP = BATCHES * DEC
T = SEQ + SMP
KT = D // P
GH, GK, GV = 4, 128, 256
RANK = 16
SH, SD, SN, SG = 16, 64, 128, 2
SC = 4
F = 5632
FT = F // P
FC = 3
EPS = 1e-6
GATE_NORM = 16.0
CH = 128
NC = SEQ // CH
HALF = T // 2
LEVELS = [CH >> (i + 1) for i in range(7)]

PAIR_TILES, PAIR_UNITS = 2, 4
IN_PAIRS = 22
OUT_PAIRS = KT // 2
OUT_UNIT0 = 2 + IN_PAIRS * PAIR_UNITS
OUT_TILE0 = 1 + IN_PAIRS * PAIR_TILES
FFN_UNIT0 = OUT_UNIT0 + OUT_PAIRS * PAIR_UNITS
FFN_TILE0 = OUT_TILE0 + OUT_PAIRS * PAIR_TILES
BLOCKS = FT // 2
UNITS = FFN_UNIT0 + 12 * BLOCKS
RING = 4

XBC_TILES = 12
N_TILE0 = 1 + XBC_TILES
BESIDE = 32
Z_N, Q_N, K_N, G_N, V_N, G2_N = 0, 8, 12, 16, 20, 28
GAP_TR, GAP_STEP, GAP_SMP, GAP_YNORM = 0, 5, 21, 34
GAP_GATE, GAP_ATT, GAP_V, GAP_KD, GAP_CHUNK, GAP_GSMP = 36, 38, 41, 54, 56, 60

COL = {}
_n = 0
for _name, _w in (("mix_pre", 16), ("mix_post", 16), ("ffn_pre", 16), ("ffn_post", 16), ("gate_b", 4),
                  ("gla_norm", 2), ("conv_w", 48), ("conv_b", 12), ("ssd_D", 8), ("ssd_norm", 8),
                  ("dt_bias", 1), ("A_log", 1), ("eps", 1), ("batch", 8)):
    COL[_name] = _n
    _n += _w
NVEC = _n
MASK_TRI, MASK_TRI_S = 8, 9

PADW = SC - 1 + SEQ + BATCHES * (SC - 1 + DEC)
CONVW = PADW - (SC - 1)
FPADW = FC - 1 + SEQ + BATCHES * (FC - 1 + DEC)
FCONVW = FPADW - (FC - 1)


SAMPLE_STEPS = (0, 5, 6, 7)


def att_base(s):
    return GH * s + sum(t < s for t in SAMPLE_STEPS)


def build(nc, xT, weights, vecs, ident_d, masks_d, psel_d, gate2, sconv_in, fconv_in, fvec_d, gla_in,
          ssdT_in, ssd_in, yT, gla_p, ssd_p, sconv_out, fconv_out, gla_s, ssd_s):
    y_spill = nc.dram_tensor("y_spill", [2, 8, P, T], F32, kind="Internal").ap()
    spill = nc.dram_tensor("spill", [BESIDE, P, T], F32, kind="Internal").ap()
    h_spill = nc.dram_tensor("h_spill", [KT, P, T], F32, kind="Internal").ap()
    with ExitStack() as ctx:
        def sb(name, shape, dt=F32):
            return ctx.enter_context(nc.sbuf_tensor(name, shape, dt))

        def sem(name):
            return ctx.enter_context(nc.semaphore(name))

        raw = sb("raw", [P, 2, 8, P])
        w_hi = sb("w_hi", [P, RING, 8, P], F32R)
        w_lo = sb("w_lo", [P, RING, 8, P], F32R)
        x_hi = sb("x_hi", [P, KT, T], F32R)
        x_lo = sb("x_lo", [P, KT, T], F32R)
        vec = sb("vec", [P, NVEC])
        ident = sb("ident", [P, P])
        ones = sb("ones", [P, P])
        masks = sb("masks", [P, 10, P], U8)
        reset = sb("reset", [P, T])
        rstd = sb("rstd", [P, T])
        misc = sb("misc", [P, T])
        decay = sb("decay", [P, 64])
        tok = sb("tok", [P, 5, 64])
        arena = sb("arena", [P, 16768])
        with nc.sbuf_tensor("tail", [P, 4736], F32) as tail:
            pass
        g_hi = sb("g_hi", [P, 2, 2, T], F32R)
        g_lo = sb("g_lo", [P, 2, 2, T], F32R)
        psum_proj = ctx.enter_context(nc.psum_tensor("psum_proj", [P, 4, 512], F32))
        work = ctx.enter_context(nc.psum_tensor("psum_work", [P, 4, 512], F32))

        def V(name, j=0, rows=P):
            return vec[0:rows, COL[name] + j:COL[name] + j + 1]

        def A(off, n, rows=P):
            return arena[0:rows, off:off + n]

        def TL(off, n, rows=P):
            return tail[0:rows, off:off + n]

        gdecay = decay[:, 0:48].rearrange("p (h c) -> p h c", h=GH)
        GQ, GKK, GB, GE = A(0, 2304), A(2304, 2304), A(4608, 2304), A(6912, 2304)
        GE2 = TL(0, 2304)
        xin = [A(6912, 2304), TL(0, 2304)]
        v_tok = A(9216, 5120).rearrange("p (t v) -> p t v", t=5)
        w_gate2 = A(9216, 512)
        masks_f = A(9728, 10 * P).rearrange("p (n t) -> p n t", n=10)
        att = A(14336, 2048).rearrange("p (n t) -> p n t", n=16)
        att_s = A(16384, 256, SMP).rearrange("p (h t) -> p h t", h=GH)
        kd_tok = TL(0, 2560).rearrange("p (t k) -> p t k", t=5)
        stage = TL(2560, 1152).rearrange("p (j t) -> p j t", j=2)
        S = TL(3712, 1024).rearrange("p (h v) -> p h v", h=GH)
        oT = A(2304, 4608).rearrange("p (n t) -> p n t", n=8)
        gsum2 = A(6912 + 2 * T, T)
        s0ring = A(6912, 2048).rearrange("p (r h v) -> p r h v", r=2, h=GH)
        kd_m = A(14336, 1024, SMP).rearrange("p (r h k) -> p r h k", r=2, h=GH)
        gT = A(9216, 4608).rearrange("p (n t) -> p n t", n=8)
        XC = A(0, 6912).rearrange("p (n t) -> p n t", n=12)
        xdt = A(6912, 5120).rearrange("p (t v) -> p t v", t=5)
        dt_tmp = [A(6912 + 576 * i, 576, SH) for i in range(4)]
        B_tok = A(12032, 1280).rearrange("p (t g n) -> p t g n", t=5, g=SG)
        W = A(13312, 2048).rearrange("p (h t) -> p h t", h=SH)
        conv_t = [A(13312 + PADW * i, PADW) for i in range(2)]
        hT = A(15360, 1024)
        cbm = A(16384, 256).rearrange("p (g t) -> p g t", g=SG)
        xw = TL(0, 1024)
        pad = [TL(1024 + PADW * i, PADW) for i in range(2)]
        ecum, yt = TL(1024, 512), TL(1536, 512)
        cumT = TL(3712, 576, SH)
        sconv_o = TL(4288, 324).rearrange("p (n c) -> p n c", n=12)
        lastrow = TL(4612, 64, SH)
        sc_state = A(9216, 288).rearrange("p (n b t) -> p n b t", n=12, b=BATCHES)
        dtT = misc[0:SH, :]
        hTs = A(6912, 2048).rearrange("p (r x) -> p r x", r=2)
        hns = A(8960, 2048).rearrange("p (r j n) -> p r j n", r=2, j=8)
        Bm = A(13312, 2048, SMP).rearrange("p (b g n) -> p b g n", b=BATCHES, g=SG)
        zT = A(6912, 4608).rearrange("p (n t) -> p n t", n=8)
        ysq = A(11520, 4608).rearrange("p (n t) -> p n t", n=8)
        y_hi = ysq.bitcast(F32R)
        mixT = A(0, 9216).rearrange("p (n t) -> p n t", n=KT)
        acc = mixT
        sq = [TL(2560 + 576 * i, 576) for i in range(2)]
        sqsum = TL(3712, 576)

        def xres(kt):
            return A(9216 + 576 * kt, 576) if kt < 13 else TL(576 * (kt - 13), 576)

        fpad = [A(9216 + FPADW * i, FPADW) for i in range(2)]
        ftap = [A(10404 + FPADW * i, FPADW) for i in range(2)]
        fgate = A(11592, 576)
        fstate = A(12168, 1408).rearrange("p (b c) -> p b c", b=BLOCKS)
        fout = A(13576, 1584).rearrange("p (b c) -> p b c", b=BLOCKS)
        fvec = A(15160, 352).rearrange("p (b c) -> p b c", b=BLOCKS)
        fc = [A(15512 + 16 * i, 16) for i in range(2)]
        fsq = [A(15544, 576), A(16120, 576)]

        const_in = sem("const_in")
        gate2_in = sem("gate2_in")
        x_in = [sem("x_in0"), sem("x_in1")]
        raw_in = [sem("raw_in0"), sem("raw_in1")]
        hi_ready, lo_ready = sem("hi_ready"), sem("lo_ready")
        units_done = sem("units_done")
        taken = sem("taken")
        setup = sem("setup")
        own_step = sem("own_step")
        sc_in, pad_st, qk_in, y_kept, yb_in, ylo = (sem(n) for n in ("sc_in", "pad_st", "qk_in", "y_kept", "yb_in", "ylo"))
        small_mm, small_out, e_mm, sq_free, hsq_mm, ysq_mm = (sem(n) for n in (
            "small_mm", "small_out", "e_mm", "sq_free", "hsq_mm", "ysq_mm"))
        f_st, fo_st, f_tap1, down_mm = (sem(n) for n in ("f_st", "fo_st", "f_tap1", "down_mm"))
        x_hi_w, x_split = sem("x_hi_w"), sem("x_split")
        sq_ready, sq_used = sem("sq_ready"), sem("sq_used")
        root_ready = sem("root_ready")
        rstd_ready = sem("rstd_ready")
        gate_mm, gate_out, gate_sub, gate_exp, gate_ln = (sem(n) for n in ("gate_mm", "gate_out", "gate_sub", "gate_exp", "gate_ln"))
        b_ready = sem("b_ready")
        v_tr, v_out = sem("v_tr"), sem("v_out")
        spilled = [sem("spilled0"), sem("spilled1")]
        sub_ready, exp_ready, pq_ready, att_mm, att_out = (sem(n) for n in ("sub_ready", "exp_ready", "pq_ready", "att_mm", "att_out"))
        kdT_ready, kd_tr, kd_out, qd_ready = (sem(n) for n in ("kdT_ready", "kd_tr", "kd_out", "qd_ready"))
        o_mm, o_out, S_mm, S_ready = (sem(n) for n in ("o_mm", "o_out", "S_mm", "S_ready"))
        s0_in = [sem("s0_in0"), sem("s0_in1")]
        s0_out = [sem("s0_out0"), sem("s0_out1")]
        kdm_ready, os_mm, os_out, s1_mm, s1_ready = (sem(n) for n in ("kdm_ready", "os_mm", "os_out", "s1_mm", "s1_ready"))
        gla_p_out = sem("gla_p_out")
        g_in, gsq, gsum, gss, groot, grs, gsilu, gy, ghi, mix_in = (sem(n) for n in (
            "g_in", "gsq", "gsum", "gss", "groot", "grs", "gsilu", "gy", "ghi", "mix_in"))
        pad_in = [sem("pad_in0"), sem("pad_in1")]
        pad_zero, tap0, taps, conv_out, sco = (sem(n) for n in ("pad_zero", "tap0", "taps", "conv_out", "sco"))
        psel_in, dts, dte, dt_ready, dttr, dtt_out = (sem(n) for n in ("psel_in", "dts", "dte", "dt_ready", "dttr", "dtt_out"))
        xtr, xdt_out, b_out = sem("xtr"), sem("xdt_out"), sem("b_out")
        bc_mm, D_ready, W_exp, W_ready, y_mm, e_exp, y_out = (sem(n) for n in (
            "bc_mm", "D_ready", "W_exp", "W_ready", "y_mm", "e_exp", "y_out"))
        wd_exp, xw_ready, h_mm, h_ready = (sem(n) for n in (
            "wd_exp", "xw_ready", "h_mm", "h_ready"))
        ssd_p_out = sem("ssd_p_out")
        hs_in = [sem("hs_in0"), sem("hs_in1")]
        hs_out = [sem("hs_out0"), sem("hs_out1")]
        sm_ready, hs_mm, hs_ready = sem("sm_ready"), sem("hs_mm"), sem("hs_ready")
        z_in, zsilu, yz, ysq_r, ysum, yroot, ymix, yhi = (sem(n) for n in (
            "z_in", "zsilu", "yz", "ysq_r", "ysum", "yroot", "ymix", "yhi"))
        sconv_st = sem("sconv_st")
        xr_in = [sem("xr_in%d" % i) for i in range(4)]
        msq, msum_mm, mroot = (sem(n) for n in ("msq", "msum_mm", "mroot"))
        h_w, hsq, h_hi, h_split, h_st = (sem(n) for n in ("h_w", "hsq", "h_hi", "h_split", "h_st"))
        ffn_in, acc_zero, fpad_zero = sem("ffn_in"), sem("acc_zero"), sem("fpad_zero")
        fc_ready, f_tap0, f_padout, f_taps, f_silu, f_prod, f_hi, act_ready = (sem(n) for n in (
            "fc_ready", "f_tap0", "f_padout", "f_taps", "f_silu", "f_prod", "f_hi", "act_ready"))
        ysq2, h_back, y_w, y_st = (sem(n) for n in (
            "ysq2", "h_back", "y_w", "y_st"))

        block = ctx.enter_context(nc.Block())

        def halves(ap):
            return ap.rearrange("p (n t) -> p n t", n=2)

        def proj(ring):
            return psum_proj[:, 2 * ring:2 * ring + 2, 0:HALF]

        def bcast(ap, shape):
            return ap.broadcast_to(shape)

        @block.sync
        def _(sp):
            def x_chunk(c):
                sp.dma_start(xin[c % 2], xT[c]).then_inc(x_in[c % 2], 16)

            x_chunk(0)
            sp.dma_start(raw[:, 0], weights[0]).then_inc(raw_in[0], 16)
            x_chunk(1)
            sp.dma_start(raw[:, 1], weights[1]).then_inc(raw_in[1], 16)
            for c in (2, 3):
                sp.wait_ge(x_split, 4 * (c - 1))
                sp.wait_ge(sq_ready, 4 * (c - 1))
                x_chunk(c)
            with sp.Fori(1, UNITS // 2) as i:
                for j in range(2):
                    sp.wait_ge(lo_ready, 2 * i + j - 1)
                    sp.dma_start(raw[:, j], weights[bass.ds(2 * i + j, 1)].rearrange("o p a b -> (o p) a b"))\
                        .then_inc(raw_in[j], 16)

        @block.gpsimd
        def _(pool):
            def weight_lo(unit, slot, r):
                pool.wait_ge(hi_ready, unit + 1)
                nc.gpsimd.tensor_tensor(w_lo[:, slot], raw[:, r], w_hi[:, slot].bitcast(F32),
                                        ALU.subtract).then_inc(lo_ready, 1)

            weight_lo(0, 0, 0)
            weight_lo(1, 1, 1)
            with pool.Fori(0, (UNITS - 2) // 4) as i:
                for j in range(4):
                    weight_lo(4 * i + 2 + j, (2 + j) % 4, j % 2)

        @block.scalar
        def _(act):
            def weight_hi(unit, half_unit, slot, r, wait=True):
                act.wait_ge(raw_in[r], 16 * half_unit + 16)
                if wait:
                    act.wait_ge(units_done, unit - 3)
                nc.scalar.activation(w_hi[:, slot], raw[:, r], ACT.Copy).then_inc(hi_ready, 1)

            def two_hi(unit, half_unit, slot):
                weight_hi(unit, half_unit, slot, 0)
                weight_hi(unit + 1, half_unit, slot + 1, 1)

            def hi_for(tile, half):
                weight_hi(2 * tile + 4 + half, tile + 2, 2 * tile % 4 + half, half)

            def root(out, psum, scale, done):
                nc.scalar.activation(halves(out), psum, ACT.Sqrt, bias=V("eps"), scale=scale).then_inc(done, 1)

            act.dma_start(vec[:], vecs).then_inc(const_in, 16)
            act.dma_start(ident[:], ident_d).then_inc(const_in, 16)
            act.dma_start(masks_f, masks_d).then_inc(const_in, 16)
            act.dma_start(sc_state, sconv_in).then_inc(sc_in, 16)
            weight_hi(0, 0, 0, 0, wait=False)
            weight_hi(1, 0, 1, 1, wait=False)
            for kt in range(KT):
                act.wait_ge(x_in[kt // 4 % 2], 16 * (kt // 8 + 1))
                if kt >= 2:
                    act.wait_ge(sq_used, kt - 1)
                nc.scalar.activation(stage[:, kt % 2], xin[kt // 4 % 2][:, kt % 4 * T:(kt % 4 + 1) * T],
                                     ACT.Square).then_inc(sq_ready, 1)
            weight_hi(2, 1, 2, 0, wait=False)
            weight_hi(3, 1, 3, 1, wait=False)
            act.wait_ge(sq_used, KT)
            act.wait_ge(const_in, 48)
            root(rstd[:], work[:, 0:2, 0:HALF], 1.0 / D, root_ready)
            weight_hi(4, 2, 0, 0)
            weight_hi(5, 2, 1, 1)
            act.wait_ge(sc_in, 16)
            act.wait_ge(x_split, KT)
            for n in range(XBC_TILES):
                q, tile = pad[n % 2], n + 1
                smp = q[:, SC - 1 + SEQ:].rearrange("p (b t) -> p b t", b=BATCHES)
                hi_for(tile, 0)
                if n >= 2:
                    act.wait_ge(taps, n - 1)
                nc.scalar.activation(smp[:, :, 0:SC - 1], sc_state[:, n], ACT.Copy).then_inc(pad_st, 1)
                hi_for(tile, 1)
                act.wait_ge(taken, tile + 3)
                act.wait_ge(pad_st, n + 1)
                act.wait_ge(pad_zero, 1)
                nc.scalar.activation(conv_t[n % 2][:, 0:CONVW], q[:, 0:CONVW], ACT.Identity,
                                     bias=V("conv_b", n), scale=V("conv_w", 4 * n)).then_inc(tap0, 1)
                nc.scalar.activation(sconv_o[:, n, 0:SC - 1], q[:, SEQ:SEQ + SC - 1], ACT.Copy)
                nc.scalar.activation(sconv_o[:, n, SC - 1:].rearrange("p (b c) -> p b c", b=BATCHES),
                                     smp[:, :, DEC:], ACT.Copy).then_inc(sco, 1)
                if n == 1:
                    act.wait_ge(dts, 1)
                    nc.scalar.activation(V("A_log", rows=SH), V("A_log", rows=SH), ACT.Exp)
                    nc.scalar.activation(dt_tmp[0], dt_tmp[0], ACT.Exp).then_inc(dte, 1)
                act.wait_ge(taps, n + 1)
                nc.scalar.activation(XC[:, n, 0:SEQ], conv_t[n % 2][:, 0:SEQ], ACT.Silu)
                nc.scalar.activation(
                    XC[:, n, SEQ:].rearrange("p (b t) -> p b t", b=BATCHES),
                    conv_t[n % 2][:, SEQ + SC - 1:].rearrange("p (b t) -> p b t", b=BATCHES)[:, :, 0:DEC], ACT.Silu)\
                    .then_inc(conv_out, 1)
            act.wait_ge(sco, XBC_TILES)
            act.dma_start(sconv_out, sconv_o).then_inc(sconv_st, 16)

            def ssd_step(k):
                c, g = k // SG, k % SG
                if g == 0:
                    act.wait_ge(small_out, c + 1)
                    nc.scalar.activation(tok[:, c, 32:64], tok[:, c, 32:64], ACT.Exp).then_inc(wd_exp, 1)
                act.wait_ge(e_mm, k + 1)
                if k >= 1:
                    act.wait_ge(y_out, k)
                nc.scalar.activation(ecum, work[:, 3, :], ACT.Exp).then_inc(e_exp, 1)
                act.wait_ge(D_ready, k + 1)
                nc.scalar.activation(W[:, 8 * g:8 * g + 8, :], W[:, 8 * g:8 * g + 8, :], ACT.Exp, scale=-1.0)\
                    .then_inc(W_exp, 1)

            def ssd_samples():
                act.wait_ge(small_out, NC + 1)
                nc.scalar.activation(decay[:], work[:, 2, 272:336], ACT.Exp)
                nc.scalar.activation(tok[0:SMP, NC, 32:48], tok[0:SMP, NC, 32:48], ACT.Exp).then_inc(wd_exp, 1)
                act.wait_ge(e_mm, SG * NC + 1)
                act.wait_ge(y_out, SG * NC)
                nc.scalar.activation(ecum, work[:, 3, :], ACT.Exp).then_inc(e_exp, 1)
                act.wait_ge(D_ready, SG * NC + 1)
                nc.scalar.activation(W[0:SMP, :, 0:SMP], W[0:SMP, :, 0:SMP], ACT.Exp, scale=-1.0).then_inc(W_exp, 1)

            def ssd_batch(b):
                act.wait_ge(hs_ready, b + 1)
                act.dma_start(ssd_s[:, b], hns[:, b % 2]).then_inc(hs_out[b % 2], 16)
                if b + 2 < BATCHES:
                    act.wait_ge(hs_mm, b + 1)
                    act.dma_start(hTs[:, b % 2], ssdT_in[:, b + 2]).then_inc(hs_in[b % 2], 16)
                    act.wait_ge(hs_out[b % 2], 16 * (b // 2 + 1))
                    act.dma_start(hns[:, b % 2], ssd_in[:, b + 2]).then_inc(hs_in[b % 2], 16)

            def gates():
                for h in range(GH):
                    act.wait_ge(gate_mm, h + 1)
                    nc.scalar.activation(halves(GE[:, h * T:(h + 1) * T]),
                                         work[:, 2 * (h % 2):2 * (h % 2) + 2, 0:HALF],
                                         ACT.Identity, bias=V("gate_b", h)).then_inc(gate_out, 1)
                act.wait_ge(gate_sub, 1)
                nc.scalar.activation(GE2, GE2, ACT.Exp).then_inc(gate_exp, 1)
                act.wait_ge(gate_exp, 1)
                nc.scalar.activation(GE2, GE2, ACT.Ln, bias=1.0).then_inc(gate_ln, 1)

            def level(s):
                act.wait_ge(sub_ready, s)
                buf = GE if s % 2 else GE2
                view = buf if LEVELS[s - 1] <= 4 else buf.rearrange("p (h t) -> p h t", h=GH)[:, :, 0:SEQ]
                nc.scalar.activation(view, view, ACT.Exp, scale=1.0 / GATE_NORM).then_inc(exp_ready, 1)

            def gla_batch(b):
                act.wait_ge(s1_ready, b + 1)
                act.dma_start(gla_s[:, b * GH:(b + 1) * GH, :], s0ring[:, b % 2]).then_inc(s0_out[b % 2], 16)
                if b + 2 < BATCHES:
                    act.wait_ge(s0_out[b % 2], 16 * (b // 2 + 1))
                    act.dma_start(s0ring[:, b % 2], gla_in[:, (b + 2) * GH:(b + 3) * GH, :])\
                        .then_inc(s0_in[b % 2], 16)

            def gap(m):
                if m < 5:
                    n = P if m < 4 else SMP
                    act.wait_ge(xtr, m + 1)
                    nc.scalar.activation(B_tok[0:n, m].rearrange("p g n -> p (g n)"), work[0:n, 2, 0:SG * SN],
                                         ACT.Copy).then_inc(b_out, 1)
                if GAP_STEP <= m < GAP_SMP and (m - GAP_STEP) % 2 == 0:
                    ssd_step((m - GAP_STEP) // 2)
                if m == GAP_SMP - 1:
                    act.wait_ge(h_ready, SG * NC)
                    act.dma_start(ssd_p, hT).then_inc(ssd_p_out, 16)
                    for b in range(2):
                        act.dma_start(hTs[:, b], ssdT_in[:, b]).then_inc(hs_in[b], 16)
                        act.dma_start(hns[:, b], ssd_in[:, b]).then_inc(hs_in[b], 16)
                if m == GAP_SMP:
                    ssd_samples()
                if GAP_SMP + 2 <= m < GAP_SMP + 2 + BATCHES:
                    ssd_batch(m - GAP_SMP - 2)
                if m == GAP_YNORM - 3:
                    for j in range(2):
                        act.wait_ge(hs_out[j], 16 * BATCHES // 2)
                        act.wait_ge(spilled[j], 16 * 4)
                    act.wait_ge(y_out, SG * NC + 1)
                    act.dma_start(zT, spill[Z_N:Z_N + 8].rearrange("n p t -> p n t")).then_inc(z_in, 16)
                if m == GAP_YNORM - 2:
                    act.wait_ge(z_in, 16)
                    nc.scalar.activation(zT, zT, ACT.Silu).then_inc(zsilu, 1)
                if m == GAP_YNORM - 1:
                    act.wait_ge(yz, 1)
                    act.wait_ge(ssd_p_out, 16)
                    nc.scalar.activation(ysq, XC[:, 0:8, :], ACT.Square).then_inc(ysq_r, 1)
                    act.dma_start(w_gate2[32:32 + RANK, :], gate2).then_inc(gate2_in, 16)
                if m == GAP_YNORM:
                    for g in range(SG):
                        act.wait_ge(ysum, g + 1)
                        root(zT[:, g], work[:, 2 * g:2 * g + 2, 0:HALF], 1.0 / (SH * SD // SG), yroot)
                    for j in range(8):
                        act.wait_ge(ymix, j + 1)
                        nc.scalar.activation(y_hi[:, j], XC[:, j], ACT.Copy).then_inc(yhi, 1)
                if m == GAP_GATE:
                    act.wait_ge(ylo, 8)
                    act.dma_start(y_spill[0].rearrange("n p t -> p n t"), ysq).then_inc(y_kept, 16)
                    act.dma_start(y_spill[1].rearrange("n p t -> p n t"), XC[:, 0:8, :]).then_inc(y_kept, 16)
                    gates()
                    act.wait_ge(y_kept, 32)
                    for j in range(2):
                        act.wait_ge(spilled[j], 16 * 8)
                    for buf, n in ((GQ, Q_N), (GKK, K_N)):
                        act.dma_start(buf.rearrange("p (n t) -> p n t", n=GH),
                                      spill[n:n + GH].rearrange("n p t -> p n t")).then_inc(qk_in, 16)
                if GAP_ATT <= m < GAP_ATT + 14 and (m - GAP_ATT) % 2 == 0:
                    level((m - GAP_ATT) // 2 + 1)
                if m == GAP_ATT + 14:
                    act.wait_ge(sub_ready, 8)
                    nc.scalar.activation(GE, GE, ACT.Exp, scale=1.0 / GATE_NORM).then_inc(exp_ready, 1)
                    nc.scalar.activation(GE2, GB, ACT.Exp, scale=1.0 / GATE_NORM).then_inc(exp_ready, 1)
                if GAP_V <= m <= GAP_V + 14 and (m - GAP_V) % 2 == 0:
                    i = (m - GAP_V) // 2
                    act.wait_ge(v_tr, i + 1)
                    nc.scalar.activation(v_tok[:, 0:4, i * P:(i + 1) * P],
                                         work[:, i % 2, :].rearrange("p (a b) -> p a b", a=4), ACT.Copy)
                    nc.scalar.activation(v_tok[0:SMP, 4, i * P:(i + 1) * P],
                                         work[0:SMP, 2 + i % 2, 0:P], ACT.Copy).then_inc(v_out, 1)
                if m == GAP_KD:
                    act.wait_ge(qd_ready, 1)
                if m in (GAP_KD, GAP_KD + 2):
                    for tt in (range(4) if m == GAP_KD else (4,)):
                        n = P if tt < 4 else SMP
                        act.wait_ge(kd_tr, tt + 1)
                        nc.scalar.activation(kd_tok[0:n, tt, :], work[0:n, tt % 4, :], ACT.Copy).then_inc(kd_out, 1)
                if m == GAP_KD + 2:
                    for b in range(2):
                        act.dma_start(s0ring[:, b], gla_in[:, b * GH:(b + 1) * GH, :]).then_inc(s0_in[b], 16)
                if GAP_CHUNK <= m < GAP_CHUNK + NC:
                    c = m - GAP_CHUNK
                    act.wait_ge(o_mm, c + 1)
                    nc.scalar.activation(oT[:, :, c * CH:(c + 1) * CH],
                                         work[:, 0:2, :].rearrange("p a (b t) -> p (a b) t", b=4), ACT.Copy)\
                        .then_inc(o_out, 1)
                if m == GAP_GSMP:
                    act.wait_ge(S_ready, NC)
                    act.dma_start(gla_p, S).then_inc(gla_p_out, 16)
                if m >= GAP_GSMP:
                    gla_batch(m - GAP_GSMP)

            for n in range(BESIDE):
                hi_for(N_TILE0 + n, 0)
                if n >= 1:
                    gap(2 * n - 1)
                hi_for(N_TILE0 + n, 1)
                if not V_N <= n < V_N + 8:
                    act.wait_ge(taken, N_TILE0 + n + 3)
                    act.dma_start(spill[n], stage[:, n % 2]).then_inc(spilled[n % 2], 16)
                gap(2 * n)
            act.wait_ge(units_done, OUT_UNIT0)
            act.dma_start(x_hi[:, 0:8, :].bitcast(F32), y_spill[0].rearrange("n p t -> p n t")).then_inc(yb_in, 16)
            act.dma_start(x_lo[:, 0:8, :].bitcast(F32), y_spill[1].rearrange("n p t -> p n t")).then_inc(yb_in, 16)
            for b in range(2 * BESIDE - 1 - GAP_GSMP, BATCHES):
                gla_batch(b)
            act.wait_ge(os_mm, 1)
            nc.scalar.activation(oT[:, :, SEQ:T], work[:, 0, :].rearrange("p (n t) -> p n t", n=8), ACT.Copy)\
                .then_inc(os_out, 1)
            for j in range(2):
                act.wait_ge(spilled[j], 16 * 12)
            act.dma_start(gT[:, 0:4, :], spill[G_N:G_N + 4].rearrange("n p t -> p n t")).then_inc(g_in, 16)
            act.dma_start(gT[:, 4:8, :], spill[G2_N:G2_N + 4].rearrange("n p t -> p n t")).then_inc(g_in, 16)
            act.wait_ge(os_out, 1)
            for j in range(2):
                act.wait_ge(s0_out[j], 16 * BATCHES // 2)
            for h in range(GH):
                if h >= 1:
                    act.wait_ge(gss, h)
                nc.scalar.activation(GE[:, 0:2 * T].rearrange("p (n t) -> p n t", n=2), oT[:, 2 * h:2 * h + 2, :],
                                     ACT.Square).then_inc(gsq, 1)
                act.wait_ge(gsum, h + 1)
                root(GQ[:, h * T:(h + 1) * T], work[:, 0:2, 0:HALF], 1.0 / GV, groot)
            act.wait_ge(g_in, 32)
            for h in range(GH):
                nc.scalar.activation(gT[:, 2 * h:2 * h + 2, :], gT[:, 2 * h:2 * h + 2, :], ACT.Silu)\
                    .then_inc(gsilu, 1)
            for h in range(GH):
                act.wait_ge(gy, h + 1)
                nc.scalar.activation(x_hi[:, 8 + 2 * h:10 + 2 * h, :], oT[:, 2 * h:2 * h + 2, :], ACT.Copy)\
                    .then_inc(ghi, 1)
            act.wait_ge(mix_in, 4)
            for c in range(3):
                act.dma_start(A(9216 + 2304 * c, 2304), xT[c]).then_inc(xr_in[c], 16)
            act.dma_start(A(9216 + 3 * 2304, T), xT[3, :, 0:T]).then_inc(xr_in[3], 16)
            act.dma_start(TL(0, 3 * T), xT[3, :, T:4 * T]).then_inc(xr_in[3], 16)
            with act.Fori(0, OUT_PAIRS) as i:
                two_hi(4 * i + OUT_UNIT0 + 4, 2 * i + OUT_UNIT0 // 2 + 2, 2)
                two_hi(4 * i + OUT_UNIT0 + 6, 2 * i + OUT_UNIT0 // 2 + 3, 0)
                for j in range(2):
                    act.wait_ge(taken, 2 * i + j + OUT_TILE0 + 3)
                    act.wait_ge(sq_free, 2 * i + j + 1)
                    nc.scalar.activation(sq[j], mixT[:, bass.ds(2 * i + j, 1), :].rearrange("p o t -> p (o t)"),
                                         ACT.Square).then_inc(msq, 1)
            act.wait_ge(msum_mm, 1)
            root(rstd[:], work[:, 0:2, 0:HALF], 1.0 / D, mroot)
            for kt in range(KT):
                act.wait_ge(h_w, kt + 1)
                if kt >= 2:
                    act.wait_ge(hsq_mm, kt - 1)
                nc.scalar.activation(sq[kt % 2], mixT[:, kt], ACT.Square).then_inc(hsq, 1)
                nc.scalar.activation(x_hi[:, kt], mixT[:, kt], ACT.Copy, scale=V("ffn_pre", kt)).then_inc(h_hi, 1)
            act.dma_start(h_spill.rearrange("n p t -> p n t"), mixT).then_inc(h_st, 16)
            act.wait_ge(h_split, KT)
            act.dma_start(fstate, fconv_in).then_inc(ffn_in, 16)
            act.dma_start(fvec, fvec_d).then_inc(ffn_in, 16)
            act.wait_ge(hsq_mm, KT)
            root(rstd[:], work[:, 0:2, 0:HALF], 1.0 / D, mroot)

            def ffn_up(blk, q, unit, half_unit, first=False):
                act.wait_ge(ffn_in, 32)
                if not first:
                    act.wait_ge(f_taps, 4 * blk - 3)
                nc.scalar.activation(fc[q], fvec[:, bass.ds(blk, 1), :].rearrange("p o c -> p (o c)"), ACT.Copy)\
                    .then_inc(fc_ready, 1)
                for j in range(4):
                    t, pair = 4 * blk + j, 2 * blk + j // 2
                    pd = fpad[j % 2]
                    smp = pd[:, FC - 1 + SEQ:].rearrange("p (b t) -> p b t", b=BATCHES)
                    if not (first and j < 2):
                        act.wait_ge(f_taps, t - 1)
                    nc.scalar.activation(
                        smp[:, :, 0:FC - 1],
                        fstate[:, bass.ds(blk, 1), 16 * j:16 * j + 16].rearrange("p o (b t) -> p (o b) t", b=BATCHES),
                        ACT.Copy).then_inc(f_st, 1)
                    act.wait_ge(taken, 20 * blk + j + (FFN_TILE0 + 3 if first else FFN_TILE0 + 3 - 16))
                    act.wait_ge(fc_ready, blk + 1)
                    act.wait_ge(f_st, t + 1)
                    if j % 2 and not (first and j == 1):
                        act.wait_ge(f_prod, pair)
                    act.wait_ge(fpad_zero, 1)
                    nc.scalar.activation(ftap[j % 2][:, 0:FCONVW], pd[:, 0:FCONVW], ACT.Identity,
                                         bias=fc[q][:, 4 * j + 3:4 * j + 4], scale=fc[q][:, 4 * j:4 * j + 1])\
                        .then_inc(f_tap0, 1)
                    nc.scalar.activation(fout[:, bass.ds(blk, 1), 18 * j:18 * j + 2].rearrange("p o c -> p (o c)"),
                                         pd[:, SEQ:SEQ + FC - 1], ACT.Copy)
                    nc.scalar.activation(
                        fout[:, bass.ds(blk, 1), 18 * j + 2:18 * j + 18].rearrange("p o (b t) -> p (o b) t", b=BATCHES),
                        smp[:, :, DEC:], ACT.Copy).then_inc(f_padout, 1)
                    two_hi(unit + 2 * j, half_unit + j, (2 + 2 * j) % 4)
                    if j % 2:
                        a = ftap[0]
                        act.wait_ge(f_taps, t)
                        if not (first and j == 1):
                            act.wait_ge(act_ready, pair)
                        nc.scalar.activation(fgate[:, 0:SEQ], a[:, 0:SEQ], ACT.Silu)
                        nc.scalar.activation(
                            fgate[:, SEQ:T].rearrange("p (b t) -> p b t", b=BATCHES),
                            a[:, SEQ + FC - 1:].rearrange("p (b t) -> p b t", b=BATCHES)[:, :, 0:DEC], ACT.Silu)\
                            .then_inc(f_silu, 1)
                        act.wait_ge(f_prod, pair + 1)
                        nc.scalar.activation(g_hi[:, q, j // 2], fgate, ACT.Copy).then_inc(f_hi, 1)

            def ffn_down(unit, half_unit):
                two_hi(unit, half_unit, 2)
                two_hi(unit + 2, half_unit + 1, 0)

            act.wait_ge(sconv_st, 16)
            U = FFN_UNIT0 + 4
            ffn_up(0, 0, U, U // 2, first=True)
            with act.Fori(0, (BLOCKS - 2) // 2) as i:
                for q in (1, 0):
                    blk = 2 * i + (1 if q else 2)
                    u = 24 * i + U + 8 + (0 if q else 12)
                    hu = 12 * i + (U + 8) // 2 + (0 if q else 6)
                    ffn_up(blk, q, u, hu)
                    ffn_down(u + 8, hu + 4)
            u = U + 8 + 12 * (BLOCKS - 2)
            ffn_up(BLOCKS - 1, 1, u, u // 2)
            ffn_down(u + 8, u // 2 + 4)
            act.wait_ge(f_padout, 4 * BLOCKS)
            act.dma_start(fconv_out, fout).then_inc(fo_st, 16)
            act.dma_start(x_hi[:].bitcast(F32), h_spill.rearrange("n p t -> p n t")).then_inc(h_back, 16)
            act.wait_ge(taken, FFN_TILE0 + 20 * BLOCKS + 2)
            for kt in range(KT):
                if kt >= 2:
                    act.wait_ge(ysq_mm, kt - 1)
                nc.scalar.activation(fsq[kt % 2], acc[:, kt], ACT.Square).then_inc(ysq2, 1)
            act.wait_ge(ysq_mm, KT)
            root(rstd[:], work[:, 0:2, 0:HALF], 1.0 / D, mroot)
            for n in range(4):
                act.wait_ge(y_w, 4 * (n + 1))
                act.dma_start(yT[n], acc[:, 4 * n:4 * n + 4, :]).then_inc(y_st, 16)
            act.wait_ge(y_st, 64)
            act.wait_ge(fo_st, 16)
            act.wait_ge(sconv_st, 16)
            act.wait_ge(ssd_p_out, 16)
            act.wait_ge(gla_p_out, 16)
            for j in range(2):
                act.wait_ge(s0_out[j], 16 * BATCHES // 2)
                act.wait_ge(hs_out[j], 16 * BATCHES // 2)

        @block.tensor
        def _(pe):
            def products(slot, k, ring, split, first, last, hi, lo):
                cuts = ((0, 0, split), (1, split, T))
                for n, a, b in cuts:
                    for part in (0, 1):
                        nc.tensor.matmul(psum_proj[:, 2 * ring + n, 0:b - a], w_hi[:, slot, k], (hi, lo)[part][:, a:b],
                                         start=first and part == 0, stop=False)
                for n, a, b in cuts:
                    mm = nc.tensor.matmul(psum_proj[:, 2 * ring + n, 0:b - a], w_lo[:, slot, k], hi[:, a:b],
                                          start=False, stop=last)
                return mm

            def project(tile, unit, slot, ring, split=HALF, before=None, middle=None):
                pe.wait_ge(taken, tile + 1)
                for half in range(2):
                    pe.wait_ge(lo_ready, unit + half + 1)
                    if half and middle:
                        middle()
                    for k in range(8):
                        kt = 8 * half + k
                        if before:
                            before(kt)
                        mm = products(slot + half, k, ring, split, kt == 0, kt == KT - 1, x_hi[:, kt], x_lo[:, kt])
                        if k == 7:
                            mm.then_inc(units_done, 1)

            def pair(p, split=HALF, before=None):
                project(2 * p + 1, 4 * p + 2, 2, 1, split, before)
                project(2 * p + 2, 4 * p + 4, 0, 0, split)

            def sum_tokens(sources, bank, done, start=True, stop=True):
                for n in range(2):
                    for i, s in enumerate(sources):
                        mm = nc.tensor.matmul(work[:, bank + n, 0:HALF], ones[:], s[:, n * HALF:(n + 1) * HALF],
                                              start=start and i == 0, stop=stop and i == len(sources) - 1)
                mm.then_inc(done, 1)

            pe.wait_ge(setup, 1)
            for kt in range(KT):
                pe.wait_ge(sq_ready, kt + 1)
                sum_tokens([stage[:, kt % 2]], 0, sq_used, kt == 0, kt == KT - 1)
            project(0, 0, 0, 0, before=lambda kt: pe.wait_ge(x_split, kt + 1))
            with pe.Fori(0, XBC_TILES // 2) as i:
                pair(i, split=256)

            def ssd_before(k):
                c, g = k // SG, k % SG
                a, z = c * CH, (c + 1) * CH
                if k >= 1:
                    pe.wait_ge(y_out, k)
                if g == 0:
                    for gg in range(SG):
                        nc.tensor.matmul(work[:, 2, gg * CH:(gg + 1) * CH], XC[:, 8 + gg, a:z], XC[:, 10 + gg, a:z],
                                         start=True, stop=True)
                    nc.tensor.matmul(work[:, 2, 256:256 + SH], cumT[:, z - 1:z].broadcast_to([SH, P]), ident[0:SH, 0:SH],
                                     start=True, stop=True).then_inc(small_mm, 1)
                if k >= 1:
                    pe.wait_ge(h_ready, k)
                for i in range(8):
                    h = 8 * g + i
                    mm = nc.tensor.matmul(work[:, i // 4, i % 4 * CH:(i % 4 + 1) * CH],
                                          ident[0:SH, h:h + 1].broadcast_to([SH, P]), cumT[:, a:z],
                                          start=True, stop=True)
                mm.then_inc(bc_mm, 1)
                for i in range(8):
                    h = 8 * g + i
                    mm = nc.tensor.matmul(work[i % 2 * SD:(i % 2 + 1) * SD, 3, i // 2 * CH:(i // 2 + 1) * CH],
                                          ident[0:SH, h:h + 1].broadcast_to([SH, SD]), cumT[:, a:z],
                                          start=True, stop=True)
                mm.then_inc(e_mm, 1)

            def ssd_after(k):
                c, g = k // SG, k % SG
                a, z = c * CH, (c + 1) * CH
                pe.wait_ge(small_out, c + 1)
                for i in range(4):
                    j = 4 * g + i
                    nc.tensor.matmul(work[:, 2, i * CH:(i + 1) * CH], hT[:, j * P:(j + 1) * P], XC[:, 10 + g, a:z],
                                     start=True, stop=True)
                pe.wait_ge(e_exp, k + 1)
                pe.wait_ge(W_ready, k + 1)
                for i in range(8):
                    h = 8 * g + i
                    mm = nc.tensor.matmul(work[i % 2 * SD:(i % 2 + 1) * SD, 3, i // 2 * CH:(i // 2 + 1) * CH],
                                          xdt[:, c, h * SD:(h + 1) * SD], W[:, h, :], start=True, stop=True)
                mm.then_inc(y_mm, 1)
                pe.wait_ge(xw_ready, c + 1)
                nc.tensor.matmul(work[:, g, :], B_tok[:, c, g, :], xw[:, g * 512:(g + 1) * 512],
                                 start=True, stop=True).then_inc(h_mm, 1)

            def ssd_samples_before():
                pe.wait_ge(y_out, SG * NC)
                for g in range(SG):
                    nc.tensor.matmul(work[0:SMP, 2, g * SMP:(g + 1) * SMP], XC[:, 8 + g, SEQ:T], XC[:, 10 + g, SEQ:T],
                                     start=True, stop=True)
                nc.tensor.matmul(work[0:SMP, 2, 256:256 + SH], lastrow, ident[0:SH, 0:SH], start=True, stop=True)
                for h in range(SH):
                    at = 272 + h // 2 * BATCHES
                    mm = nc.tensor.matmul(work[h % 2 * SD:(h % 2 + 1) * SD, 2, at:at + BATCHES],
                                          ident[0:SH, h:h + 1].broadcast_to([SH, SD]), cumT[:, SEQ + DEC - 1:T:DEC],
                                          start=True, stop=True)
                mm.then_inc(small_mm, 1)
                pe.wait_ge(h_ready, SG * NC)
                for h in range(SH):
                    mm = nc.tensor.matmul(work[0:SMP, h // 8, h % 8 * SMP:(h % 8 + 1) * SMP],
                                          ident[0:SH, h:h + 1].broadcast_to([SH, SMP]), cumT[:, SEQ:T],
                                          start=True, stop=True)
                mm.then_inc(bc_mm, 1)
                for h in range(SH):
                    mm = nc.tensor.matmul(work[h % 2 * SD:(h % 2 + 1) * SD, 3, h // 2 * SMP:(h // 2 + 1) * SMP],
                                          ident[0:SH, h:h + 1].broadcast_to([SH, SD]), cumT[:, SEQ:T],
                                          start=True, stop=True)
                mm.then_inc(e_mm, 1)

            def ssd_samples_after():
                pe.wait_ge(e_exp, SG * NC + 1)
                pe.wait_ge(W_ready, SG * NC + 1)
                for h in range(SH):
                    mm = nc.tensor.matmul(work[h % 2 * SD:(h % 2 + 1) * SD, 3, h // 2 * SMP:(h // 2 + 1) * SMP],
                                          xdt[0:SMP, 4, h * SD:(h + 1) * SD], W[0:SMP, h, 0:SMP], start=True, stop=True)
                mm.then_inc(y_mm, 1)

            def ssd_batch(b):
                if b == 0:
                    pe.wait_ge(wd_exp, NC + 1)
                    pe.wait_ge(small_out, NC + 1)
                    pe.wait_ge(sm_ready, 1)
                pe.wait_ge(hs_in[b % 2], 32 * (b // 2 + 1))
                for j in range(8):
                    at = j * SMP + b * DEC
                    nc.tensor.matmul(work[:, 2, at:at + DEC], hTs[:, b % 2, j * P:(j + 1) * P],
                                     XC[:, 10 + j // 4, SEQ + b * DEC:SEQ + (b + 1) * DEC], start=True, stop=True)
                if b >= 1:
                    pe.wait_ge(hs_ready, b)
                for j in range(8):
                    mm = nc.tensor.matmul(work[:, j // 4, j % 4 * SN:(j % 4 + 1) * SN], xw[0:SMP, j * P:(j + 1) * P],
                                          Bm[:, b, j // 4, :], start=True, stop=True)
                mm.then_inc(hs_mm, 1)

            def gates():
                pe.wait_ge(gate2_in, 16)
                pe.wait_ge(yroot, SG)
                for h in range(GH):
                    if h >= 2:
                        pe.wait_ge(gate_out, h - 1)
                    for n in range(2):
                        mm = nc.tensor.matmul(work[:, 2 * (h % 2) + n, 0:HALF],
                                              w_gate2[32:32 + RANK, h * GK:(h + 1) * GK],
                                              misc[32:32 + RANK, n * HALF:(n + 1) * HALF], start=True, stop=True)
                    mm.then_inc(gate_mm, 1)

            def att_step(s):
                k, q = (GKK, GQ) if s == 0 else (GE, GE) if s % 2 else (GE2, GE2)
                if s == 0:
                    pe.wait_ge(qk_in, 32)
                    pe.wait_ge(gate_out, GH)
                else:
                    pe.wait_ge(pq_ready, s)
                    if s >= 2:
                        pe.wait_ge(v_out, s - 1)
                for h in range(GH):
                    for c in range(NC):
                        at = h * T + c * CH
                        mm = nc.tensor.matmul(work[:, h, c * CH:(c + 1) * CH], k[:, at:at + CH], q[:, at:at + CH],
                                              start=True, stop=True)
                    mm.then_inc(att_mm, 1)
                if s in SAMPLE_STEPS:
                    pe.wait_ge(att_out, att_base(s) + 1)
                    for h in range(GH):
                        at = h * T + SEQ
                        mm = nc.tensor.matmul(work[0:SMP, 0, h * SMP:(h + 1) * SMP], k[:, at:at + SMP],
                                              q[:, at:at + SMP], start=True, stop=True)
                    mm.then_inc(att_mm, 1)

            def v_by_tokens(i):
                pe.wait_ge(taken, N_TILE0 + V_N + i + 3)
                pe.wait_ge(att_out, att_base(min(i + 2, 8)))
                if i == 7:
                    pe.wait_ge(kd_out, 4)
                for tt in range(4):
                    nc.tensor.transpose(work[:, i % 2, tt * P:(tt + 1) * P], stage[:, i % 2, tt * P:(tt + 1) * P],
                                        ident[:])
                nc.tensor.transpose(work[0:SMP, 2 + i % 2, 0:P], stage[:, i % 2, SEQ:T], ident[:]).then_inc(v_tr, 1)

            def keys_by_tokens(tiles):
                pe.wait_ge(kdT_ready, 1)
                pe.wait_ge(att_out, att_base(8))
                pe.wait_ge(v_out, 7 if tiles[0] == 0 else 8)
                if tiles[0]:
                    pe.wait_ge(kd_out, 4)
                for tt in tiles:
                    n = P if tt < 4 else SMP
                    for h in range(GH):
                        at = h * T + tt * P
                        mm = nc.tensor.transpose(work[0:n, tt % 4, h * GK:(h + 1) * GK], GE[:, at:at + n], ident[:])
                    mm.then_inc(kd_tr, 1)

            def gla_chunk(c):
                if c == 0:
                    pe.wait_ge(v_out, 8)
                    pe.wait_ge(kd_out, 5)
                    pe.wait_ge(qd_ready, 1)
                else:
                    pe.wait_ge(o_out, c)
                    pe.wait_ge(S_ready, c)
                for n in range(8):
                    h, vh = n // 2, n % 2
                    region = work[:, n // 4, n % 4 * CH:(n % 4 + 1) * CH]
                    mm = nc.tensor.matmul(region, v_tok[:, c, n * P:(n + 1) * P], att[:, h * NC + c, :],
                                          start=True, stop=c == 0)
                    if c >= 1:
                        at = h * T + c * CH
                        mm = nc.tensor.matmul(region, S[:, h, vh * P:(vh + 1) * P], GQ[:, at:at + CH],
                                              start=False, stop=True)
                mm.then_inc(o_mm, 1)
                for h in range(GH):
                    mm = nc.tensor.matmul(work[:, 2 + h // 2, h % 2 * GV:(h % 2 + 1) * GV],
                                          kd_tok[:, c, h * GK:(h + 1) * GK], v_tok[:, c, h * GV:(h + 1) * GV],
                                          start=True, stop=True)
                mm.then_inc(S_mm, 1)

            def gla_batch(b):
                if b == 0:
                    pe.wait_ge(o_out, NC)
                    for n in range(8):
                        nc.tensor.matmul(work[:, 0, n * SMP:(n + 1) * SMP], v_tok[0:SMP, 4, n * P:(n + 1) * P],
                                         att_s[:, n // 2, :], start=n == 0, stop=False, skip_group_check=True)
                pe.wait_ge(s0_in[b % 2], 16 * (b // 2 + 1))
                for n in range(8):
                    h, vh = n // 2, n % 2
                    at = h * T + SEQ + b * DEC
                    mm = nc.tensor.matmul(work[:, 0, n * SMP + b * DEC:n * SMP + (b + 1) * DEC],
                                          s0ring[:, b % 2, h, vh * P:(vh + 1) * P], GQ[:, at:at + DEC],
                                          start=False, stop=b == BATCHES - 1 and n == 7, skip_group_check=True)
                if b == BATCHES - 1:
                    mm.then_inc(os_mm, 1)
                pe.wait_ge(kdm_ready, b + 1)
                if b == 0:
                    pe.wait_ge(S_ready, NC)
                else:
                    pe.wait_ge(s1_ready, b)
                for h in range(GH):
                    mm = nc.tensor.matmul(work[:, 2 + h // 2, h % 2 * GV:(h % 2 + 1) * GV],
                                          kd_m[:, b % 2, h, :], v_tok[0:SMP, 4, h * GV:(h + 1) * GV],
                                          start=True, stop=True)
                mm.then_inc(s1_mm, 1)

            def gap(m):
                if m == 0:
                    pe.wait_ge(dt_ready, 2)
                    pe.wait_ge(root_ready, 1)
                    for tt in range(5):
                        n = P if tt < 4 else SMP
                        for i, src in enumerate((dtT, cumT)):
                            mm = nc.tensor.transpose(work[0:n, 3, 32 * tt + SH * i:32 * tt + SH * (i + 1)],
                                                     src[:, tt * P:tt * P + n], ident[0:SH, 0:SH])
                    mm.then_inc(dttr, 1)
                    pe.wait_ge(conv_out, XBC_TILES)
                if m < 5:
                    n = P if m < 4 else SMP
                    if m >= 1:
                        pe.wait_ge(xdt_out, m)
                        pe.wait_ge(b_out, m)
                    for j in range(10):
                        mm = nc.tensor.transpose(work[0:n, j // 4, j % 4 * P:(j % 4 + 1) * P],
                                                 XC[:, j, m * P:m * P + n], ident[:])
                    mm.then_inc(xtr, 1)
                if m == GAP_STEP:
                    pe.wait_ge(xdt_out, 5)
                    pe.wait_ge(b_out, 5)
                    pe.wait_ge(dtt_out, 1)
                if GAP_STEP <= m < GAP_SMP:
                    (ssd_after if (m - GAP_STEP) % 2 else ssd_before)((m - GAP_STEP) // 2)
                if m == GAP_SMP:
                    ssd_samples_before()
                if m == GAP_SMP + 1:
                    ssd_samples_after()
                if GAP_SMP + 2 <= m < GAP_SMP + 2 + BATCHES:
                    ssd_batch(m - GAP_SMP - 2)
                if m == GAP_YNORM:
                    pe.wait_ge(y_out, SG * NC + 1)
                    pe.wait_ge(hs_ready, BATCHES)
                    pe.wait_ge(ysq_r, 1)
                    for g in range(SG):
                        sum_tokens([ysq[:, 4 * g + i] for i in range(4)], 2 * g, ysum)
                if m == GAP_GATE:
                    gates()
                if GAP_ATT <= m < GAP_ATT + 16 and (m - GAP_ATT) % 2 == 0:
                    att_step((m - GAP_ATT) // 2)
                if GAP_V <= m <= GAP_V + 14 and (m - GAP_V) % 2 == 0:
                    v_by_tokens((m - GAP_V) // 2)
                if m == GAP_KD:
                    keys_by_tokens(range(4))
                if m == GAP_KD + 2:
                    keys_by_tokens((4,))
                if GAP_CHUNK <= m < GAP_CHUNK + NC:
                    gla_chunk(m - GAP_CHUNK)
                if m >= GAP_GSMP:
                    gla_batch(m - GAP_GSMP)

            for n in range(BESIDE):
                tile = N_TILE0 + n
                project(tile, 2 * tile, 2 * tile % 4, tile % 2, middle=(lambda: gap(2 * n - 1)) if n else None)
                gap(2 * n)
            for b in range(2 * BESIDE - 1 - GAP_GSMP, BATCHES):
                gla_batch(b)
            pe.wait_ge(os_out, 1)
            for h in range(GH):
                pe.wait_ge(gss, h + 1)
                if h >= 1:
                    pe.wait_ge(groot, h)
                sum_tokens([gsum2], 0, gsum)

            def mix_arrives(kt):
                if kt == 0:
                    pe.wait_ge(yb_in, 32)
                if kt >= 8:
                    pe.wait_ge(mix_in, (kt - 8) // 2 + 1)

            pair(IN_PAIRS, before=mix_arrives)
            with pe.Fori(IN_PAIRS + 1, IN_PAIRS + OUT_PAIRS) as i:
                pair(i)
            pe.wait_ge(sq_free, KT + 2)
            sum_tokens([sqsum], 0, msum_mm)
            pe.wait_ge(mroot, 1)

            def h_arrives(kt):
                pe.wait_ge(hsq, kt + 1)
                sum_tokens([sq[kt % 2]], 0, hsq_mm, kt == 0, kt == KT - 1)
                pe.wait_ge(h_split, kt + 1)

            def up(tile, unit, before=None):
                for j in range(4):
                    project(tile + j, unit + 2 * j, (2 + 2 * j) % 4, (1 + j) % 2, split=256, before=before if j == 0 else None)

            def down(blk, q, tile, unit):
                pe.wait_ge(act_ready, 2 * blk + 2)
                for d in range(KT):
                    if d % 4 == 0:
                        pe.wait_ge(lo_ready, unit + d // 4 + 1)
                    pe.wait_ge(taken, tile + d + 1)
                    for k in range(2):
                        mm = products((2 + d // 4) % 4, d % 4 * 2 + k, (1 + d) % 2, HALF, k == 0, k == 1,
                                      g_hi[:, q, k], g_lo[:, q, k])
                    mm.then_inc(units_done if d % 4 == 3 else down_mm, 1)

            up(FFN_TILE0, FFN_UNIT0, before=h_arrives)
            with pe.Fori(0, (BLOCKS - 2) // 2) as i:
                for q in (1, 0):
                    b = 1 if q else 2
                    tile, unit = FFN_TILE0 - 16 + 20 * b, FFN_UNIT0 - 4 + 12 * b
                    up(40 * i + tile, 24 * i + unit)
                    down(2 * i + b - 1, 1 - q, 40 * i + tile + 4, 24 * i + unit + 8)
            tile, unit = FFN_TILE0 - 16 + 20 * (BLOCKS - 1), FFN_UNIT0 - 4 + 12 * (BLOCKS - 1)
            up(tile, unit)
            down(BLOCKS - 2, 0, tile + 4, unit + 8)
            down(BLOCKS - 1, 1, tile + 20, unit + 12)
            for kt in range(KT):
                pe.wait_ge(ysq2, kt + 1)
                sum_tokens([fsq[kt % 2]], 0, ysq_mm, kt == 0, kt == KT - 1)

        @block.vector
        def _(ve):
            steps = [0]

            def own(instruction):
                instruction.then_inc(own_step, 1)
                steps[0] += 1

            def settle():
                ve.wait_ge(own_step, steps[0])

            tt_op, ts_op, stt = nc.vector.tensor_tensor, nc.vector.tensor_scalar, nc.vector.scalar_tensor_tensor

            nc.vector.memset(ones[:], 1.0).then_inc(setup, 1)
            nc.vector.memset(hT, 0.0).then_inc(taken, 2)
            own(nc.vector.memset(cbm, 0.0))
            own(nc.vector.memset(reset[:], 1.0))
            settle()
            nc.vector.memset(reset[:, 0:SEQ:CH], 0.0)
            own(nc.vector.memset(reset[:, SEQ:T:DEC], 0.0))
            ve.wait_ge(const_in, 48)
            own(nc.vector.tensor_copy(masks[:], masks_f))
            for kt in range(KT):
                x = xin[kt // 4 % 2][:, kt % 4 * T:(kt % 4 + 1) * T]
                ve.wait_ge(x_in[kt // 4 % 2], 16 * (kt // 8 + 1))
                ts_op(x_hi[:, kt], x, V("mix_pre", kt), None, ALU.mult).then_inc(x_hi_w, 1)
                ve.wait_ge(x_hi_w, kt + 1)
                stt(x_lo[:, kt], x, V("mix_pre", kt), x_hi[:, kt].bitcast(F32), ALU.mult, ALU.subtract)\
                    .then_inc(x_split, 1)
            ve.wait_ge(root_ready, 1)
            nc.vector.reciprocal(rstd[:], rstd[:]).then_inc(rstd_ready, 1)
            ve.wait_ge(rstd_ready, 1)
            nc.vector.memset(pad[0][:, 0:SC - 1], 0.0)
            nc.vector.memset(pad[1][:, 0:SC - 1], 0.0).then_inc(pad_zero, 1)

            def take(tile, out):
                ve.wait_ge(units_done, 2 * tile + 2)
                tt_op(halves(out), proj(tile % 2), halves(rstd[:]), ALU.mult).then_inc(taken, 1)

            take(0, misc[:])

            def dt_steps(part):
                e, z, z2, p = dt_tmp
                if part == 0:
                    ve.wait_ge(taken, 3)
                    own(ts_op(dtT, dtT, V("dt_bias", rows=SH), None, ALU.add))
                    settle()
                    own(ts_op(z, dtT, 0.0, None, ALU.min))
                    settle()
                    stt(e, z, 2.0, dtT, ALU.mult, ALU.subtract).then_inc(dts, 1)
                if part == 1:
                    ve.wait_ge(dte, 1)
                    own(ts_op(z, e, 2.0, None, ALU.add))
                    settle()
                    own(nc.vector.reciprocal(z, z))
                    settle()
                    own(tt_op(z, z, e, ALU.mult))
                    settle()
                    own(tt_op(z2, z, z, ALU.mult))
                    settle()
                    own(ts_op(p, z2, 1.0 / 15, None, ALU.mult))
                if part == 2:
                    for n in (13, 11, 9, 7, 5, 3):
                        settle()
                        own(stt(p, p, 1.0 / n, z2, ALU.add, ALU.mult))
                if part == 3:
                    settle()
                    own(stt(p, p, 1.0, z, ALU.add, ALU.mult))
                    own(ts_op(dtT, dtT, 0.0, None, ALU.max))
                    settle()
                    own(stt(dtT, p, 2.0, dtT, ALU.mult, ALU.add))
                    settle()
                    own(ts_op(e, dtT, V("A_log", rows=SH), -1.0, ALU.mult, ALU.mult))
                    settle()
                    nc.vector.tensor_tensor_scan(cumT, reset[0:SH, :], e, 0.0, ALU.mult, ALU.add).then_inc(dt_ready, 1)
                    ve.wait_ge(dt_ready, 1)
                    c8 = cumT[:, SEQ:T].rearrange("p (b t) -> p b t", b=BATCHES)
                    nc.vector.tensor_copy(lastrow.rearrange("p (b t) -> p b t", b=BATCHES),
                                          c8[:, :, DEC - 1:DEC].broadcast_to([SH, BATCHES, DEC])).then_inc(dt_ready, 1)

            for n in range(XBC_TILES):
                q, o, r = pad[n % 2], conv_t[n % 2][:, 0:CONVW], (n + 1) % 2
                ve.wait_ge(units_done, 2 * n + 4)
                if n >= 2:
                    ve.wait_ge(sco, n - 1)
                tt_op(q[:, SC - 1:SC - 1 + SEQ].rearrange("p (n t) -> p n t", n=2), psum_proj[:, 2 * r:2 * r + 2, 0:256],
                      rstd[:, 0:SEQ].rearrange("p (n t) -> p n t", n=2), ALU.mult)
                tt_op(q[:, SC - 1 + SEQ:].rearrange("p (b t) -> p b t", b=BATCHES)[:, :, SC - 1:],
                      psum_proj[:, 2 * r + 1, 256:320].rearrange("p (b t) -> p b t", b=BATCHES),
                      rstd[:, SEQ:T].rearrange("p (b t) -> p b t", b=BATCHES), ALU.mult).then_inc(taken, 1)
                if n == 0:
                    dt_steps(0)
                ve.wait_ge(tap0, n + 1)
                for t in range(1, SC):
                    if t > 1:
                        settle()
                    i = stt(o, q[:, t:t + CONVW], V("conv_w", 4 * n + t), o, ALU.mult, ALU.add)
                    if t < SC - 1:
                        own(i)
                i.then_inc(taps, 1)
                if n in (2, 4, 6):
                    dt_steps(n // 2)

            def small(c, n, cols, mask):
                ve.wait_ge(small_mm, c + 1)
                nc.vector.copy_predicated(cbm[0:n, :, 0:cols], masks[0:n, mask:mask + 1, 0:cols].broadcast_to([n, SG, cols]),
                                          work[0:n, 2, 0:SG * cols].rearrange("p (g t) -> p g t", g=SG))
                last = work[0:n, 2, 256:256 + SH]
                tt_op(tok[0:n, c, 32:48], last, tok[0:n, c, 16:32], ALU.subtract)
                nc.vector.tensor_copy(tok[0:n, c, 48:64], last).then_inc(small_out, 1)

            def decayed_x(c, n):
                ve.wait_ge(wd_exp, c + 1)
                if c >= 1:
                    ve.wait_ge(h_mm, SG * c)
                tt_op(xw[0:n].rearrange("p (h d) -> p h d", h=SH), xdt[0:n, c].rearrange("p (h d) -> p h d", h=SH),
                      tok[0:n, c, 32:48].unsqueeze(2).broadcast_to([n, SH, SD]), ALU.mult).then_inc(xw_ready, 1)

            def exponents(k, w, cum_s, n):
                ve.wait_ge(bc_mm, k + 1)
                own(tt_op(w, cum_s.unsqueeze(2).broadcast_to(list(w.shape)),
                          work[0:n, 0:2, :].rearrange("p a (h t) -> p (a h) t", t=w.shape[-1]), ALU.subtract))
                settle()
                ts_op(w, w, 0.0, None, ALU.max).then_inc(D_ready, 1)

            def ssd_before(k):
                c, g = k // SG, k % SG
                w = W[:, 8 * g:8 * g + 8, :]
                if g == 0:
                    small(c, P, CH, MASK_TRI)
                if k >= 2:
                    ve.wait_ge(y_mm, k - 1)
                exponents(k, w, tok[:, c, 16 + 8 * g:24 + 8 * g], P)
                if g == 0:
                    decayed_x(c, P)
                hh = hT[:, g * 512:(g + 1) * 512].rearrange("p (h d) -> p h d", h=8)
                ve.wait_ge(W_exp, k + 1)
                tt_op(w, w, cbm[:, g:g + 1, :].broadcast_to([P, 8, CH]), ALU.mult).then_inc(W_ready, 1)

            def add_y(y, j):
                own(tt_op(yt, work[:, 2, :], ecum, ALU.mult))
                settle()
                own(tt_op(yt, work[:, 3, :], yt, ALU.add))
                settle()
                tt_op(y, y, yt.rearrange("p (j t) -> p j t", j=j), ALU.add).then_inc(y_out, 1)

            def ssd_after(k):
                c, g = k // SG, k % SG
                ve.wait_ge(y_mm, k + 1)
                ve.wait_ge(e_exp, k + 1)
                add_y(XC[:, 4 * g:4 * g + 4, c * CH:(c + 1) * CH], 4)
                hh = hT[:, g * 512:(g + 1) * 512]
                own(tt_op(hh.rearrange("p (h d) -> p h d", h=8), hh.rearrange("p (h d) -> p h d", h=8),
                          tok[:, c, 48 + 8 * g:56 + 8 * g].unsqueeze(2).broadcast_to([P, 8, SD]), ALU.mult))
                settle()
                ve.wait_ge(h_mm, k + 1)
                tt_op(hh, work[:, g, :], hh, ALU.add).then_inc(h_ready, 1)

            def ssd_samples_before():
                ve.wait_ge(W_ready, SG * NC)
                own(nc.vector.memset(cbm[0:SMP], 0.0))
                settle()
                small(NC, SMP, SMP, MASK_TRI_S)
                exponents(SG * NC, W[0:SMP, :, 0:SMP], tok[0:SMP, NC, 16:32], SMP)
                decayed_x(NC, SMP)
                ve.wait_ge(W_exp, SG * NC + 1)
                for g in range(SG):
                    w = W[0:SMP, 8 * g:8 * g + 8, 0:SMP]
                    i = tt_op(w, w, cbm[0:SMP, g:g + 1, 0:SMP].broadcast_to([SMP, 8, SMP]), ALU.mult)
                i.then_inc(W_ready, 1)

            def ssd_samples_after():
                ve.wait_ge(y_mm, SG * NC + 1)
                ve.wait_ge(b_out, 5)
                for b in range(BATCHES):
                    i = ts_op(Bm[:, b].rearrange("p g n -> p (g n)"), B_tok[0:SMP, 4].rearrange("p g n -> p (g n)"),
                              V("batch", b, SMP), None, ALU.mult)
                i.then_inc(sm_ready, 1)

            el2 = decay[:].rearrange("p (j b) -> p j b", j=8)

            def ssd_batch(b):
                ve.wait_ge(hs_in[b % 2], 32 * (b // 2 + 1))
                ve.wait_ge(wd_exp, NC + 1)
                own(tt_op(hns[:, b % 2], hns[:, b % 2], el2[:, :, b:b + 1].broadcast_to([P, 8, SN]), ALU.mult))
                settle()
                ve.wait_ge(hs_mm, b + 1)
                tt_op(hns[:, b % 2], work[:, 0:2, :].rearrange("p a (j n) -> p (a j) n", j=4), hns[:, b % 2], ALU.add)\
                    .then_inc(hs_ready, 1)

            def gates():
                ve.wait_ge(gate_out, GH)
                own(ts_op(GB, GE, 0.0, None, ALU.min))
                settle()
                stt(GE2, GB, 2.0, GE, ALU.mult, ALU.subtract).then_inc(gate_sub, 1)
                ve.wait_ge(gate_ln, 1)
                own(tt_op(GE, GB, GE2, ALU.subtract))
                settle()
                for h in range(GH):
                    i = nc.vector.tensor_tensor_scan(GB[:, h * T:(h + 1) * T], reset[:], GE[:, h * T:(h + 1) * T],
                                                     0.0, ALU.mult, ALU.add)
                i.then_inc(b_ready, 1)

            def chunk_view(buf, m):
                if m <= DEC // 2:
                    v = buf.rearrange("p (n u m) -> p n u m", u=2, m=m)
                    return v[:, :, 0], v[:, :, 1]
                v = buf.rearrange("p (h t) -> p h t", h=GH)[:, :, 0:SEQ].rearrange("p h (n u m) -> p h n u m", u=2, m=m)
                return v[:, :, :, 0], v[:, :, :, 1]

            def take_att(s):
                for h in range(GH):
                    ve.wait_ge(att_mm, att_base(s) + h + 1)
                    nc.vector.copy_predicated(att[:, h * NC:(h + 1) * NC, :], masks[:, s:s + 1, :].broadcast_to([P, NC, P]),
                                              work[:, h, :].rearrange("p (c t) -> p c t", c=NC)).then_inc(att_out, 1)
                if s in SAMPLE_STEPS:
                    ve.wait_ge(att_mm, att_base(s + 1))
                    nc.vector.copy_predicated(att_s, masks[0:SMP, s:s + 1, 0:SMP].broadcast_to([SMP, GH, SMP]),
                                              work[0:SMP, 0, 0:GH * SMP].rearrange("p (h t) -> p h t", h=GH))\
                        .then_inc(att_out, 1)

            def operands(s):
                m = LEVELS[s - 1]
                buf = GE if s % 2 else GE2
                (k_out, q_out), (k_b, q_b) = chunk_view(buf, m), chunk_view(GB, m)
                ref = k_b[..., m - 1:m].broadcast_to(list(k_b.shape))
                if s >= 3:
                    ve.wait_ge(att_mm, att_base(s - 1))
                tt_op(k_out, ref, k_b, ALU.subtract)
                tt_op(q_out, q_b, ref, ALU.subtract).then_inc(sub_ready, 1)
                ve.wait_ge(exp_ready, s)
                tt_op(k_out, k_out, chunk_view(GKK, m)[0], ALU.mult)
                tt_op(q_out, q_out, chunk_view(GQ, m)[1], ALU.mult).then_inc(pq_ready, 1)

            def decay_to_ends():
                ve.wait_ge(att_mm, att_base(8))
                for lo, hi, n in ((0, SEQ, CH), (SEQ, T, DEC)):
                    def v(buf):
                        return buf.rearrange("p (h t) -> p h t", h=GH)[:, :, lo:hi].rearrange("p h (c t) -> p h c t", t=n)
                    b = v(GB)
                    i = tt_op(v(GE), b[..., n - 1:n].broadcast_to(list(b.shape)), b, ALU.subtract)
                i.then_inc(sub_ready, 1)
                ve.wait_ge(exp_ready, 8)
                tt_op(GE, GE, GKK, ALU.mult).then_inc(kdT_ready, 1)
                ve.wait_ge(exp_ready, 9)
                e = GE2.rearrange("p (h t) -> p h t", h=GH)
                tt_op(GQ, GQ, GE2, ALU.mult)
                nc.vector.tensor_copy(gdecay[:, :, 0:NC], e[:, :, CH - 1:SEQ:CH])
                nc.vector.tensor_copy(gdecay[:, :, NC:NC + BATCHES], e[:, :, SEQ + DEC - 1:T:DEC]).then_inc(qd_ready, 1)
                ve.wait_ge(qd_ready, 1)

            def gla_chunk(c):
                ve.wait_ge(S_mm, c + 1)
                if c == 0:
                    ve.wait_ge(sconv_st, 16)
                else:
                    ve.wait_ge(S_ready, c)
                for h in range(GH):
                    inc = work[:, 2 + h // 2, h % 2 * GV:(h % 2 + 1) * GV]
                    if c == 0:
                        i = nc.vector.tensor_copy(S[:, h, :], inc)
                    else:
                        i = stt(S[:, h, :], S[:, h, :], gdecay[:, h, c:c + 1], inc, ALU.mult, ALU.add)
                i.then_inc(S_ready, 1)

            def masked_keys(b):
                if b >= 2:
                    ve.wait_ge(s1_mm, b - 1)
                ts_op(kd_m[:, b % 2].rearrange("p h k -> p (h k)"), kd_tok[0:SMP, 4, :], V("batch", b, SMP), None, ALU.mult)\
                    .then_inc(kdm_ready, 1)

            def gla_batch(b):
                ve.wait_ge(s1_mm, b + 1)
                ve.wait_ge(s0_in[b % 2], 16 * (b // 2 + 1))
                for h in range(GH):
                    s = s0ring[:, b % 2, h, :]
                    i = stt(s, s, gdecay[:, h, NC + b:NC + b + 1], work[:, 2 + h // 2, h % 2 * GV:(h % 2 + 1) * GV],
                            ALU.mult, ALU.add)
                i.then_inc(s1_ready, 1)
                if b + 2 < BATCHES:
                    masked_keys(b + 2)

            def gap(m):
                if m == 0:
                    ve.wait_ge(dttr, 1)
                    nc.vector.tensor_copy(tok[:, 0:4, 0:32], work[:, 3, 0:128].rearrange("p (t c) -> p t c", t=4))
                    nc.vector.tensor_copy(tok[0:SMP, 4, 0:32], work[0:SMP, 3, 128:160]).then_inc(dtt_out, 1)
                    ve.wait_ge(dtt_out, 1)
                if m < 5:
                    n = P if m < 4 else SMP
                    ve.wait_ge(xtr, m + 1)
                    tt_op(xdt[0:n, m].rearrange("p (h d) -> p h d", h=SH),
                          work[0:n, 0:2, :].rearrange("p a (h d) -> p (a h) d", d=SD),
                          tok[0:n, m, 0:SH].unsqueeze(2).broadcast_to([n, SH, SD]), ALU.mult).then_inc(xdt_out, 1)
                if m == 4:
                    for j in range(8):
                        i = ts_op(XC[:, j], XC[:, j], V("ssd_D", j), None, ALU.mult)
                    own(i)
                    ve.wait_ge(xdt_out, 5)
                    settle()
                if GAP_STEP <= m < GAP_SMP:
                    (ssd_after if (m - GAP_STEP) % 2 else ssd_before)((m - GAP_STEP) // 2)
                if m == GAP_SMP:
                    ssd_samples_before()
                if m == GAP_SMP + 1:
                    ssd_samples_after()
                if GAP_SMP + 2 <= m < GAP_SMP + 2 + BATCHES:
                    ssd_batch(m - GAP_SMP - 2)
                if m == GAP_SMP + 1 + BATCHES:
                    add_y(XC[:, 0:8, SEQ:T], 8)
                    ve.wait_ge(y_out, SG * NC + 1)
                if m == GAP_YNORM - 2:
                    ve.wait_ge(zsilu, 1)
                    tt_op(XC[:, 0:8], XC[:, 0:8], zT, ALU.mult).then_inc(yz, 1)
                if m == GAP_YNORM:
                    ve.wait_ge(yroot, SG)
                    own(nc.vector.reciprocal(zT[:, 0:2], zT[:, 0:2]))
                    settle()
                    for j in range(8):
                        stt(XC[:, j], XC[:, j], V("ssd_norm", j), zT[:, j // 4], ALU.mult, ALU.mult).then_inc(ymix, 1)
                if m == GAP_YNORM + 1:
                    for j in range(8):
                        ve.wait_ge(yhi, j + 1)
                        tt_op(XC[:, j], XC[:, j], ysq[:, j], ALU.subtract).then_inc(ylo, 1)
                if m == GAP_GATE:
                    gates()
                    ve.wait_ge(y_kept, 32)
                    nc.vector.memset(att, 0.0)
                    own(nc.vector.memset(att_s, 0.0))
                    settle()
                    ve.wait_ge(b_ready, 1)
                    ve.wait_ge(qk_in, 32)
                if GAP_ATT <= m < GAP_ATT + 16 and (m - GAP_ATT) % 2 == 0:
                    s = (m - GAP_ATT) // 2
                    take_att(s)
                    if s < 7:
                        operands(s + 1)
                    else:
                        decay_to_ends()
                if GAP_CHUNK <= m < GAP_CHUNK + NC:
                    gla_chunk(m - GAP_CHUNK)
                if m == GAP_GSMP - 1:
                    ve.wait_ge(o_mm, NC)
                    ve.wait_ge(kd_out, 5)
                    masked_keys(0)
                    masked_keys(1)
                if m >= GAP_GSMP:
                    gla_batch(m - GAP_GSMP)

            for n in range(BESIDE):
                ve.wait_ge(units_done, 2 * (N_TILE0 + n) + 2)
                if V_N + 2 <= n < V_N + 10:
                    ve.wait_ge(v_tr, n - V_N - 1)
                elif n >= 2:
                    ve.wait_ge(spilled[n % 2], 16 * (n // 2 if n < V_N + 2 else n // 2 - 4))
                out, p = halves(stage[:, n % 2]), proj((N_TILE0 + n) % 2)
                if Q_N <= n < Q_N + GH:
                    i = stt(out, p, GK ** -0.5, halves(rstd[:]), ALU.mult, ALU.mult)
                else:
                    i = tt_op(out, p, halves(rstd[:]), ALU.mult)
                i.then_inc(taken, 1)
                gap(2 * n)
                if n < BESIDE - 1:
                    gap(2 * n + 1)
            for b in range(2 * BESIDE - 1 - GAP_GSMP, BATCHES):
                gla_batch(b)
            ve.wait_ge(yb_in, 32)
            for h in range(GH):
                ve.wait_ge(gsq, h + 1)
                if h >= 1:
                    ve.wait_ge(gsum, h)
                tt_op(gsum2, GE[:, 0:T], GE[:, T:2 * T], ALU.add).then_inc(gss, 1)
            for h in range(GH):
                ve.wait_ge(groot, h + 1)
                r = GQ[:, h * T:(h + 1) * T]
                nc.vector.reciprocal(r, r).then_inc(grs, 1)
                ve.wait_ge(grs, h + 1)
                for vh in range(2):
                    o = oT[:, 2 * h + vh]
                    i = stt(o, o, V("gla_norm", vh), r, ALU.mult, ALU.mult)
                own(i)
                settle()
                ve.wait_ge(gsilu, h + 1)
                o = oT[:, 2 * h:2 * h + 2]
                tt_op(o, o, gT[:, 2 * h:2 * h + 2], ALU.mult).then_inc(gy, 1)
            for h in range(GH):
                ve.wait_ge(ghi, h + 1)
                tt_op(x_lo[:, 8 + 2 * h:10 + 2 * h], oT[:, 2 * h:2 * h + 2], x_hi[:, 8 + 2 * h:10 + 2 * h].bitcast(F32),
                      ALU.subtract).then_inc(mix_in, 1)

            nc.vector.memset(sqsum, 0.0).then_inc(sq_free, 2)
            ve.wait_ge(mix_in, 4)
            with ve.Fori(0, OUT_PAIRS) as i:
                for j in range(2):
                    ve.wait_ge(units_done, 4 * i + 2 * j + OUT_UNIT0 + 2)
                    ts_op(mixT[:, bass.ds(2 * i + j, 1), :].rearrange("p o (n t) -> p (o n) t", n=2), proj((1 + j) % 2),
                          1.0, None, ALU.mult).then_inc(taken, 1)
                for j in range(2):
                    ve.wait_ge(msq, 2 * i + j + 1)
                    ve.wait_ge(sq_free, 2 * i + j + 2)
                    tt_op(sqsum, sqsum, sq[j], ALU.add).then_inc(sq_free, 1)
            ve.wait_ge(mroot, 1)
            own(nc.vector.reciprocal(rstd[:], rstd[:]))
            settle()

            def h_lo(kt):
                ve.wait_ge(h_hi, kt + 1)
                stt(x_lo[:, kt], mixT[:, kt], V("ffn_pre", kt), x_hi[:, kt].bitcast(F32), ALU.mult, ALU.subtract)\
                    .then_inc(h_split, 1)

            for kt in range(KT):
                own(stt(mixT[:, kt], mixT[:, kt], V("mix_post", kt), rstd[:], ALU.mult, ALU.mult))
                if kt >= 1:
                    h_lo(kt - 1)
                settle()
                ve.wait_ge(xr_in[kt // 4], 32 if kt >= 12 else 16)
                tt_op(mixT[:, kt], mixT[:, kt], xres(kt), ALU.add).then_inc(h_w, 1)
            h_lo(KT - 1)
            nc.vector.memset(fpad[0][:, 0:FC - 1], 0.0)
            nc.vector.memset(fpad[1][:, 0:FC - 1], 0.0).then_inc(fpad_zero, 1)
            ve.wait_ge(mroot, 2)
            own(nc.vector.reciprocal(rstd[:], rstd[:]))
            settle()

            def take_up(t, j, unit, first=False):
                pd, r = fpad[j % 2], (1 + j) % 2
                ve.wait_ge(units_done, unit + 2 * j + 2)
                if not (first and j < 2):
                    ve.wait_ge(f_padout, t - 1)
                tt_op(pd[:, FC - 1:FC - 1 + SEQ].rearrange("p (n t) -> p n t", n=2), psum_proj[:, 2 * r:2 * r + 2, 0:256],
                      rstd[:, 0:SEQ].rearrange("p (n t) -> p n t", n=2), ALU.mult)
                tt_op(pd[:, FC - 1 + SEQ:].rearrange("p (b t) -> p b t", b=BATCHES)[:, :, FC - 1:],
                      psum_proj[:, 2 * r + 1, 256:320].rearrange("p (b t) -> p b t", b=BATCHES),
                      rstd[:, SEQ:T].rearrange("p (b t) -> p b t", b=BATCHES), ALU.mult).then_inc(taken, 1)

            def taps_of(t, j, q):
                pd, o = fpad[j % 2], ftap[j % 2][:, 0:FCONVW]
                ve.wait_ge(f_tap0, t + 1)
                stt(o, pd[:, 1:1 + FCONVW], fc[q][:, 4 * j + 1:4 * j + 2], o, ALU.mult, ALU.add).then_inc(f_tap1, 1)
                ve.wait_ge(f_tap1, t + 1)
                stt(o, pd[:, 2:2 + FCONVW], fc[q][:, 4 * j + 2:4 * j + 3], o, ALU.mult, ALU.add).then_inc(f_taps, 1)

            def gate_product(pair):
                ve.wait_ge(f_silu, pair + 1)
                ve.wait_ge(f_taps, 2 * pair + 2)
                tt_op(fgate[:, 0:SEQ], fgate[:, 0:SEQ], ftap[1][:, 0:SEQ], ALU.mult)
                g8 = fgate[:, SEQ:T].rearrange("p (b t) -> p b t", b=BATCHES)
                tt_op(g8, g8, ftap[1][:, SEQ + FC - 1:FPADW].rearrange("p (b t) -> p b t", b=BATCHES)[:, :, 0:DEC],
                      ALU.mult).then_inc(f_prod, 1)

            def gate_lo(pair, q, i):
                ve.wait_ge(f_hi, pair + 1)
                tt_op(g_lo[:, q, i], fgate, g_hi[:, q, i].bitcast(F32), ALU.subtract).then_inc(act_ready, 1)

            def take_down(d, unit, count):
                if d % 4 == 3:
                    ve.wait_ge(units_done, unit + d // 4 + 1)
                else:
                    ve.wait_ge(down_mm, count + 3 * (d // 4) + d % 4 + 1)
                a = halves(acc[:, d])
                tt_op(a, proj((1 + d) % 2), a, ALU.add).then_inc(taken, 1)

            def block_up(blk, q, unit, first=False):
                t = 4 * blk
                take_up(t, 0, unit, first)
                taps_of(t, 0, q)
                take_up(t + 1, 1, unit, first)
                taps_of(t + 1, 1, q)
                gate_product(2 * blk)
                gate_lo(2 * blk, q, 0)
                take_up(t + 2, 2, unit)
                taps_of(t + 2, 2, q)
                take_up(t + 3, 3, unit)

            def block_end(blk, q, step):
                if step == 0:
                    taps_of(4 * blk + 3, 3, q)
                elif step == 1:
                    gate_product(2 * blk + 1)
                else:
                    gate_lo(2 * blk + 1, q, 1)

            def block(blk, q, unit, tile):
                block_up(blk, q, unit)
                ve.wait_ge(taken, tile + 4 + 2)
                for d in range(KT):
                    take_down(d, unit + 8, 12 * blk - 12)
                    if d in (1, 4, 7):
                        block_end(blk, q, (1, 4, 7).index(d))

            block_up(0, 0, FFN_UNIT0, first=True)
            for s in range(3):
                block_end(0, 0, s)
            ve.wait_ge(h_st, 16)
            nc.vector.memset(acc.rearrange("p n t -> p (n t)"), 0.0).then_inc(acc_zero, 1)
            ve.wait_ge(acc_zero, 1)
            with ve.Fori(0, (BLOCKS - 2) // 2) as i:
                for q in (1, 0):
                    b = 1 if q else 2
                    block(2 * i + b, q, 24 * i + FFN_UNIT0 - 4 + 12 * b, 40 * i + FFN_TILE0 - 16 + 20 * b)
            b = BLOCKS - 1
            unit, tile = FFN_UNIT0 - 4 + 12 * b, FFN_TILE0 - 16 + 20 * b
            block(b, 1, unit, tile)
            ve.wait_ge(taken, tile + 20 + 2)
            for d in range(KT):
                take_down(d, unit + 12, 12 * b)
            ve.wait_ge(mroot, 3)
            own(nc.vector.reciprocal(rstd[:], rstd[:]))
            settle()
            ve.wait_ge(taken, tile + 36 + 2)
            ve.wait_ge(h_back, 16)
            hb = x_hi[:].bitcast(F32)
            for kt in range(KT):
                own(stt(acc[:, kt], acc[:, kt], V("ffn_post", kt), rstd[:], ALU.mult, ALU.mult))
                settle()
                tt_op(acc[:, kt], acc[:, kt], hb[:, kt], ALU.add).then_inc(y_w, 1)


def _tiles(rows):
    return np.swapaxes(rows.reshape((-1, P) + rows.shape[1:]), 0, 1)


def _weights(w_in, w_out, f_in, f_out):
    cut = np.cumsum([0, GH * GK, GH * GK, GH * GV, GH * GV, RANK, SH * SD, SH * SD + 2 * SG * SN, SH])
    q, k, v, g, lr, z, xbc, dt = (np.arange(cut[i], cut[i + 1]) for i in range(8))
    cols = np.concatenate([dt, q[:16], lr, q[:80], xbc, z, q, k, g[:4 * P], v, g[4 * P:]])

    def by_tile(w):
        return w.reshape(2, 8, P, -1, P).transpose(3, 0, 2, 1, 4).reshape(-1, P, 8, P)

    up = by_tile(f_in).reshape(2, BLOCKS, 4, P, 8, P)
    up = up.reshape(2, BLOCKS, 2, 2, P, 8, P).transpose(1, 2, 0, 3, 4, 5, 6).reshape(BLOCKS, 8, P, 8, P)
    down = f_out.reshape(BLOCKS, 2, P, 4, 4, P).transpose(0, 3, 2, 4, 1, 5).reshape(BLOCKS, 4, P, 8, P)
    ffn = [up[0]]
    for b in range(1, BLOCKS):
        ffn += [up[b], down[b - 1]]
    w_out = np.concatenate([w_out[GH * GV:], w_out[:GH * GV]])
    return np.concatenate([by_tile(w_in[:, cols]), by_tile(w_out)] + ffn + [down[BLOCKS - 1]])


def _masks():
    s, t = np.arange(P)[:, None], np.arange(P)[None, :]
    levels = [(s // (2 * m) == t // (2 * m)) & (s % (2 * m) < m) & (t % (2 * m) >= m) for m in LEVELS]
    return np.stack([s == t] + levels + [s <= t, (s <= t) & (s // DEC == t // DEC)], axis=1).astype(np.float32)


def _ffn_channels(a):
    a = a.reshape((2, BLOCKS, 2, P) + a.shape[1:])
    return np.moveaxis(np.swapaxes(a, 0, 1).swapaxes(1, 2).reshape((BLOCKS, 4, P) + a.shape[4:]), 2, 0)


def _ffn_channels_back(a):
    a = np.moveaxis(a, 0, 2).reshape((BLOCKS, 2, 2, P) + a.shape[3:])
    return np.swapaxes(a, 1, 2).swapaxes(0, 1).reshape((2 * F,) + a.shape[4:])


def kernel(**inputs):
    from concourse import bacc as _bacc
    from concourse.bass_utils import run_bass_kernel_spmd as _run

    a = {k: np.asarray(v) for k, v in inputs.items()}
    x = np.concatenate([a["x_prompt"].reshape(SEQ, D), a["x_sample"].reshape(SMP, D)])
    f32 = x.dtype
    col = {k: a[k][0].reshape(-1, P).T for k in ("norm_mix_pre", "norm_mix_post", "norm_ffn_pre", "norm_ffn_post",
                                                 "gla_norm", "ssd_conv_b", "ssd_norm")}
    pad_rows = lambda v: np.concatenate([v, np.zeros(P - len(v), f32)])[:, None]
    batch_mask = np.zeros((P, BATCHES), f32)
    batch_mask[np.arange(SMP), np.arange(SMP) // DEC] = 1
    vecs = np.concatenate([
        col["norm_mix_pre"], col["norm_mix_post"], col["norm_ffn_pre"], col["norm_ffn_post"],
        a["gla_b_gate"][0].reshape(-1, P).T, col["gla_norm"],
        _tiles(a["ssd_conv_w"][0].T).reshape(P, -1), col["ssd_conv_b"],
        np.repeat(a["ssd_D"][0], SD).reshape(-1, P).T, col["ssd_norm"],
        pad_rows(a["ssd_dt_bias"][0]), pad_rows(a["ssd_A_log"][0]), np.full((P, 1), EPS, f32), batch_mask], axis=1)
    psel = np.repeat(np.eye(SH, dtype=f32), SD, axis=1)
    fvec = np.concatenate([a["ffn_conv_w"][0], a["ffn_conv_b"]]).T
    ssd = a["state_ssd"][0].reshape(BATCHES, SH * SD, SN)
    arrays = [
        ("xT", _tiles(x.T).reshape(P, 4, 4 * T).swapaxes(0, 1)),
        ("weights", _weights(a["w_in"][0], a["w_out"][0], a["ffn_w_in"][0], a["ffn_w_out"][0])),
        ("vecs", vecs),
        ("ident", np.eye(P, dtype=f32)),
        ("masks", _masks()),
        ("psel", psel),
        ("gate2", a["gla_w_gate2"][0]),
        ("sconv_in", _tiles(a["state_ssd_conv"][0].transpose(2, 0, 1))),
        ("fconv_in", _ffn_channels(a["state_ffn_conv"][0].transpose(2, 0, 1)).reshape(P, BLOCKS, -1)),
        ("fvec", _ffn_channels(fvec).reshape(P, BLOCKS, -1)),
        ("gla_in", a["state_gla"][0].transpose(2, 0, 1, 3).reshape(GK, -1, GV)),
        ("ssdT_in", ssd.transpose(2, 0, 1)),
        ("ssd_in", ssd.reshape(BATCHES, 8, P, SN).transpose(2, 0, 1, 3)),
    ]
    outs = [("yT", (4, P, 4, T)), ("gla_p", (P, GH, GV)), ("ssd_p", (SN, SH * SD)), ("sconv_out", (P, XBC_TILES, 27)),
            ("fconv_out", (P, BLOCKS, 72)), ("gla_s", (P, BATCHES * GH, GV)), ("ssd_s", (P, BATCHES, 8, SN))]
    nc = _bacc.Bacc("TRN2", target_bir_lowering=False, num_devices=1)
    fed, args = {}, []
    for name, v in arrays:
        v = np.ascontiguousarray(v)
        fed[f"in_{name}_dram"] = v
        args.append(nc.dram_tensor(f"in_{name}_dram", v.shape, mybir.dt.from_np(v.dtype), kind="ExternalInput").ap())
    for name, shape in outs:
        args.append(nc.dram_tensor(f"out_{name}_dram", shape, F32, kind="ExternalOutput").ap())
    build(nc, *args)
    r = _run(nc, [fed], core_ids=[0])
    o = {name: np.asarray(r.results[0][f"out_{name}_dram"]).reshape(shape) for name, shape in outs}
    y = o["yT"].swapaxes(0, 1).reshape(P, KT, T).transpose(2, 1, 0).reshape(T, D)
    sconv = o["sconv_out"].transpose(2, 1, 0).reshape(27, -1)
    fconv = _ffn_channels_back(o["fconv_out"].reshape(P, BLOCKS, 4, 18)).T
    return (y[:SEQ].reshape(1, SEQ, D), y[SEQ:].reshape(BATCHES, DEC, D),
            o["gla_p"].transpose(1, 0, 2).reshape(1, 1, GH, GK, GV),
            o["ssd_p"].T.reshape(1, 1, SH, SD, SN),
            sconv[:SC - 1].reshape(1, 1, SC - 1, -1),
            fconv[:FC - 1].reshape(1, 1, FC - 1, -1),
            o["gla_s"].reshape(GK, BATCHES, GH, GV).transpose(1, 2, 0, 3)[None],
            o["ssd_s"].transpose(1, 2, 0, 3).reshape(1, BATCHES, SH, SD, SN),
            sconv[SC - 1:].reshape(1, BATCHES, SC - 1, -1),
            fconv[FC - 1:].reshape(1, BATCHES, FC - 1, -1))
```

```python
from contextlib import ExitStack

import numpy as np

import concourse.bass as bass
from concourse import mybir

F32 = mybir.dt.float32
F32R = mybir.dt.float32r
U8 = mybir.dt.uint8
ALU = mybir.AluOpType
ACT = mybir.ActivationFunctionType

P = 128
D = 2048
SEQ, BATCHES, DEC = 512, 8, 8
SMP = BATCHES * DEC
T = SEQ + SMP
KT = D // P
GH, GK, GV = 4, 128, 256
RANK = 16
SH, SD, SN, SG = 16, 64, 128, 2
SC = 4
F = 5632
FT = F // P
FC = 3
EPS = 1e-6
GATE_NORM = 16.0
CH = 128
NC = SEQ // CH
HALF = T // 2
LEVELS = [CH >> (i + 1) for i in range(7)]

PAIR_TILES, PAIR_UNITS = 2, 4
IN_PAIRS = 22
OUT_PAIRS = KT // 2
OUT_UNIT0 = 2 + IN_PAIRS * PAIR_UNITS
OUT_TILE0 = 1 + IN_PAIRS * PAIR_TILES
FFN_UNIT0 = OUT_UNIT0 + OUT_PAIRS * PAIR_UNITS
FFN_TILE0 = OUT_TILE0 + 2 * KT
BLOCKS = FT // 2
UNITS = FFN_UNIT0 + 12 * BLOCKS
RING = 4

XBC_TILES = 12
N_TILE0 = 1 + XBC_TILES
BESIDE = 32
Z_N, Q_N, K_N, G_N, V_N, G2_N = 0, 8, 12, 16, 20, 28
GAP_TR, GAP_STEP, GAP_SMP, GAP_YNORM = 0, 5, 21, 34
GAP_GATE, GAP_ATT, GAP_V, GAP_KD, GAP_CHUNK, GAP_GSMP = 38, 40, 43, 56, 58, 62

COL = {}
_n = 0
for _name, _w in (("mix_pre", 16), ("mix_post", 16), ("ffn_pre", 16), ("ffn_post", 16), ("gate_b", 4),
                  ("gla_norm", 2), ("conv_w", 48), ("conv_b", 12), ("ssd_D", 8), ("ssd_norm", 8),
                  ("dt_bias", 1), ("A_log", 1), ("eps", 1), ("batch", 8)):
    COL[_name] = _n
    _n += _w
NVEC = _n
MASK_TRI, MASK_TRI_S = 8, 9
VE_ADDS = (3, 7, 10, 11, 14, 15)

PADW = SC - 1 + SEQ + BATCHES * (SC - 1 + DEC)
CONVW = PADW - (SC - 1)
FPADW = FC - 1 + SEQ + BATCHES * (FC - 1 + DEC)
FCONVW = FPADW - (FC - 1)


SAMPLE_STEPS = (0, 5, 6, 7)


def att_base(s):
    return GH * s + sum(t < s for t in SAMPLE_STEPS)


def build(nc, xT, weights, vecs, ident_d, masks_d, gate2, sconv_in, fconv_in, fvec_d, gla_in,
          ssdT_in, ssd_in, yT, gla_p, ssd_p, sconv_out, fconv_out, gla_s, ssd_s):
    y_spill = nc.dram_tensor("y_spill", [2, 8, P, T], F32, kind="Internal").ap()
    spill = nc.dram_tensor("spill", [BESIDE, P, T], F32, kind="Internal").ap()
    h_spill = nc.dram_tensor("h_spill", [KT, P, T], F32, kind="Internal").ap()
    with ExitStack() as ctx:
        def sb(name, shape, dt=F32):
            return ctx.enter_context(nc.sbuf_tensor(name, shape, dt))

        def sem(name):
            return ctx.enter_context(nc.semaphore(name))

        raw = sb("raw", [P, 2, 8, P])
        w_hi = sb("w_hi", [P, RING, 8, P], F32R)
        w_lo = sb("w_lo", [P, RING, 8, P], F32R)
        with nc.sbuf_tensor("x_flat", [P, 2 * KT, T], F32) as x_flat:
            pass
        x_hi = sb("x_hi", [P, KT, T], F32R)
        x_lo = sb("x_lo", [P, KT, T], F32R)
        vec = sb("vec", [P, NVEC])
        ident = sb("ident", [P, P])
        ones = sb("ones", [P, P])
        masks = sb("masks", [P, 10, P], U8)
        reset = sb("reset", [P, T])
        rstd = sb("rstd", [P, T])
        misc = sb("misc", [P, T])
        decay = sb("decay", [P, 64])
        tok = sb("tok", [P, 5, 64])
        with nc.sbuf_tensor("arena", [P, 16768], F32) as arena:
            pass
        gla_ops = sb("gla_ops", [P, KT, T], F32R)
        sb("arena_rest", [P, 16768 - KT * T])
        with nc.sbuf_tensor("tail", [P, 4736], F32) as tail:
            pass
        g_hi = sb("g_hi", [P, 2, 2, T], F32R)
        g_lo = sb("g_lo", [P, 2, 2, T], F32R)
        psum_proj = ctx.enter_context(nc.psum_tensor("psum_proj", [P, 4, 512], F32))
        work = ctx.enter_context(nc.psum_tensor("psum_work", [P, 4, 512], F32))

        def V(name, j=0, rows=P):
            return vec[0:rows, COL[name] + j:COL[name] + j + 1]

        def A(off, n, rows=P):
            return arena[0:rows, off:off + n]

        def TL(off, n, rows=P):
            return tail[0:rows, off:off + n]

        gdecay = decay[:, 0:48].rearrange("p (h c) -> p h c", h=GH)
        GQ, GKK, GB, GE = A(0, 2304), A(2304, 2304), A(4608, 2304), A(6912, 2304)
        GE2 = TL(0, 2304)
        xin = [A(2304 * c, 2304) for c in range(4)]
        v_tok = A(9216, 5120).rearrange("p (t v) -> p t v", t=5)
        w_gate2 = A(9216, 512)
        masks_f = A(9728, 10 * P).rearrange("p (n t) -> p n t", n=10)
        att = A(14336, 2048).rearrange("p (n t) -> p n t", n=16)
        att_s = A(16384, 256, SMP).rearrange("p (h t) -> p h t", h=GH)
        kd_tok = TL(0, 2560).rearrange("p (t k) -> p t k", t=5)
        stage = TL(2560, 1152).rearrange("p (j t) -> p j t", j=2)
        S = TL(3712, 1024).rearrange("p (h v) -> p h v", h=GH)
        oT = A(2304, 4608).rearrange("p (n t) -> p n t", n=8)
        xsum = A(14336, T)
        gsum2 = A(6912 + 2 * T, T)
        s0ring = A(6912, 2048).rearrange("p (r h v) -> p r h v", r=2, h=GH)
        kd_m = A(14336, 1024, SMP).rearrange("p (r h k) -> p r h k", r=2, h=GH)
        gT = A(9216, 4608).rearrange("p (n t) -> p n t", n=8)
        XC = A(0, 6912).rearrange("p (n t) -> p n t", n=12)
        xdt = A(6912, 5120).rearrange("p (t v) -> p t v", t=5)
        dt_tmp = [A(6912 + 576 * i, 576, SH) for i in range(4)]
        B_tok = A(12032, 1280).rearrange("p (t g n) -> p t g n", t=5, g=SG)
        W = A(13312, 2048).rearrange("p (h t) -> p h t", h=SH)
        conv_t = [A(13312 + PADW * i, PADW) for i in range(2)]
        hT = A(15360, 1024)
        cbm = A(16384, 256).rearrange("p (g t) -> p g t", g=SG)
        xw = TL(0, 1024)
        pad = [TL(1024 + PADW * i, PADW) for i in range(2)]
        ecum, yt = TL(1024, 512), TL(1536, 512)
        cumT = TL(3712, 576, SH)
        sconv_o = TL(4288, 324).rearrange("p (n c) -> p n c", n=12)
        lastrow = TL(4612, 64, SH)
        sc_state = A(9216, 288).rearrange("p (n b t) -> p n b t", n=12, b=BATCHES)
        dtT = misc[0:SH, :]
        hTs = A(6912, 2048).rearrange("p (r x) -> p r x", r=2)
        hns = A(8960, 2048).rearrange("p (r j n) -> p r j n", r=2, j=8)
        Bm = A(13312, 2048, SMP).rearrange("p (b g n) -> p b g n", b=BATCHES, g=SG)
        zT = A(6912, 4608).rearrange("p (n t) -> p n t", n=8)
        ysq = A(11520, 4608).rearrange("p (n t) -> p n t", n=8)
        y_hi = ysq.bitcast(F32R)
        mix = x_flat[:, 8:8 + KT, :]
        mixT = A(0, 9216).rearrange("p (n t) -> p n t", n=KT)
        acc = mixT
        sq = [TL(2560 + 576 * i, 576) for i in range(2)]
        sqsum = TL(3712, 576)

        def xres(kt):
            return A(9216 + 576 * kt, 576) if kt < 13 else TL(576 * (kt - 13), 576)

        fpad = [A(9216 + FPADW * i, FPADW) for i in range(2)]
        ftap = [A(10404 + FPADW * i, FPADW) for i in range(2)]
        fgate = A(11592, 576)
        fstate = A(12168, 1408).rearrange("p (b c) -> p b c", b=BLOCKS)
        fout = A(13576, 1584).rearrange("p (b c) -> p b c", b=BLOCKS)
        fvec = A(15160, 352).rearrange("p (b c) -> p b c", b=BLOCKS)
        fc = [A(15512 + 16 * i, 16) for i in range(2)]
        fsq = [A(15544, 576), A(16120, 576)]
        fsum = A(9216, 576)

        const_in = sem("const_in")
        gate2_in = sem("gate2_in")
        x_in = [sem("x_in%d" % i) for i in range(3)]
        raw_in = [sem("raw_in0"), sem("raw_in1")]
        hi_ready, lo_ready = sem("hi_ready"), sem("lo_ready")
        units_done = sem("units_done")
        taken = sem("taken")
        setup = sem("setup")
        own_step = sem("own_step")
        sc_in, pad_st, qk_in, y_kept, ylo = (sem(n) for n in ("sc_in", "pad_st", "qk_in", "y_kept", "ylo"))
        h_m, y_m, y_wp, ysq_sum = (sem(n) for n in ("h_m", "y_m", "y_wp", "ysq_sum"))
        yb_in = [sem("yb_in%d" % i) for i in range(4)]
        vec_in, masks_in = sem("vec_in"), sem("masks_in")
        ylo_kept, sq_sum = sem("ylo_kept"), sem("sq_sum")
        small_mm, small_out, e_mm, sq_free, hsq_mm, ysq_mm = (sem(n) for n in (
            "small_mm", "small_out", "e_mm", "sq_free", "hsq_mm", "ysq_mm"))
        f_st, fo_st, f_tap1, down_mm = (sem(n) for n in ("f_st", "fo_st", "f_tap1", "down_mm"))
        x_hi_w, x_split = sem("x_hi_w"), sem("x_split")
        sq_ready, sq_used = sem("sq_ready"), sem("sq_used")
        root_ready = sem("root_ready")
        rstd_ready = sem("rstd_ready")
        gate_mm, gate_out, gate_sub, gate_exp, gate_ln = (sem(n) for n in ("gate_mm", "gate_out", "gate_sub", "gate_exp", "gate_ln"))
        b_ready = sem("b_ready")
        v_tr, v_out = sem("v_tr"), sem("v_out")
        spilled = [sem("spilled0"), sem("spilled1")]
        sub_ready, exp_ready, pq_ready, att_mm, att_out = (sem(n) for n in ("sub_ready", "exp_ready", "pq_ready", "att_mm", "att_out"))
        kdT_ready, kd_tr, kd_out, qd_ready = (sem(n) for n in ("kdT_ready", "kd_tr", "kd_out", "qd_ready"))
        o_mm, o_out, S_mm, S_ready = (sem(n) for n in ("o_mm", "o_out", "S_mm", "S_ready"))
        s0_in = [sem("s0_in0"), sem("s0_in1")]
        s0_out = [sem("s0_out0"), sem("s0_out1")]
        kdm_ready, os_mm, os_out, s1_mm, s1_ready = (sem(n) for n in ("kdm_ready", "os_mm", "os_out", "s1_mm", "s1_ready"))
        gla_p_out = sem("gla_p_out")
        g_in, gsq, gsum, gss, groot, grs, gsilu, gy, ghi, mix_in = (sem(n) for n in (
            "g_in", "gsq", "gsum", "gss", "groot", "grs", "gsilu", "gy", "ghi", "mix_in"))
        pad_zero, tap0, taps, conv_out, sco = (sem(n) for n in ("pad_zero", "tap0", "taps", "conv_out", "sco"))
        dts, dte, dt_ready, dttr, dtt_out = (sem(n) for n in ("dts", "dte", "dt_ready", "dttr", "dtt_out"))
        xtr, xdt_out, b_out = sem("xtr"), sem("xdt_out"), sem("b_out")
        bc_mm, D_ready, W_exp, W_ready, y_mm, e_exp, y_out = (sem(n) for n in (
            "bc_mm", "D_ready", "W_exp", "W_ready", "y_mm", "e_exp", "y_out"))
        wd_exp, xw_ready, h_mm, h_ready = (sem(n) for n in (
            "wd_exp", "xw_ready", "h_mm", "h_ready"))
        ssd_p_out = sem("ssd_p_out")
        hs_in = [sem("hs_in0"), sem("hs_in1")]
        hs_out = [sem("hs_out0"), sem("hs_out1")]
        sm_ready, hs_mm, hs_ready = sem("sm_ready"), sem("hs_mm"), sem("hs_ready")
        z_in, zsilu, yz, ysq_r, ysum, yroot, ymix, yhi = (sem(n) for n in (
            "z_in", "zsilu", "yz", "ysq_r", "ysum", "yroot", "ymix", "yhi"))
        sconv_st = sem("sconv_st")
        xr_in = [sem("xr_in%d" % i) for i in range(4)]
        msq, msum_mm, mroot = (sem(n) for n in ("msq", "msum_mm", "mroot"))
        h_w, hsq, h_hi, h_split, h_st = (sem(n) for n in ("h_w", "hsq", "h_hi", "h_split", "h_st"))
        ffn_in, acc_zero, fpad_zero = sem("ffn_in"), sem("acc_zero"), sem("fpad_zero")
        fc_ready, f_tap0, f_padout, f_taps, f_silu, f_prod, f_hi, act_ready = (sem(n) for n in (
            "fc_ready", "f_tap0", "f_padout", "f_taps", "f_silu", "f_prod", "f_hi", "act_ready"))
        ysq2, h_back, y_w, y_st = (sem(n) for n in (
            "ysq2", "h_back", "y_w", "y_st"))

        block = ctx.enter_context(nc.Block())

        def gla_hi(kt, n=1):
            return gla_ops[:, 12 + kt:12 + kt + n] if kt < 4 else gla_ops[:, kt - 4:kt - 4 + n]

        def gla_lo(kt, n=1):
            return gla_ops[:, 4 + kt:4 + kt + n]

        def halves(ap):
            return ap.rearrange("p (n t) -> p n t", n=2)

        def proj(ring):
            return psum_proj[:, 2 * ring:2 * ring + 2, 0:HALF]

        def bcast(ap, shape):
            return ap.broadcast_to(shape)

        @block.sync
        def _(sp):
            sp.dma_start(xin[0], xT[0]).then_inc(x_in[0], 16)
            sp.dma_start(raw[:, 0], weights[0]).then_inc(raw_in[0], 16)
            sp.dma_start(xin[1], xT[1]).then_inc(x_in[1], 16)
            sp.dma_start(raw[:, 1], weights[1]).then_inc(raw_in[1], 16)
            for c in (2, 3):
                sp.dma_start(xin[c], xT[c]).then_inc(x_in[2], 16)
            with sp.Fori(1, UNITS // 2) as i:
                for j in range(2):
                    sp.wait_ge(lo_ready, 2 * i + j - 1)
                    sp.dma_start(raw[:, j], weights[bass.ds(2 * i + j, 1)].rearrange("o p a b -> (o p) a b"))\
                        .then_inc(raw_in[j], 16)

        @block.gpsimd
        def _(pool):
            def weight_lo(unit, slot, r):
                pool.wait_ge(hi_ready, unit + 1)
                nc.gpsimd.tensor_tensor(w_lo[:, slot], raw[:, r], w_hi[:, slot].bitcast(F32),
                                        ALU.subtract).then_inc(lo_ready, 1)

            weight_lo(0, 0, 0)
            pool.wait_ge(setup, 2)
            for kt in range(0, KT, 2):
                pool.wait_ge(sq_ready, kt + 1)
                if kt:
                    pool.wait_ge(sq_sum, kt // 2)
                nc.gpsimd.tensor_tensor(xsum, xsum, stage[:, 0], ALU.add).then_inc(sq_sum, 1)
                if kt == 4:
                    weight_lo(1, 1, 1)

            def weights_lo(start, stop):
                with pool.Fori(start, stop) as i:
                    for j in range(4):
                        weight_lo(4 * i + 2 + j, (2 + j) % 4, j % 2)

            at_ynorm, at_h = (GAP_YNORM // 2 + N_TILE0 + 2) // 2, (FFN_UNIT0 + 4 - 2) // 4
            weights_lo(0, at_ynorm)
            for j in range(4):
                pool.wait_ge(yhi, j + 1)
                nc.gpsimd.tensor_tensor(XC[:, j], XC[:, j], ysq[:, j], ALU.subtract).then_inc(ylo, 1)
            weights_lo(at_ynorm, at_h)
            for kt in range(KT):
                pool.wait_ge(h_m, kt + 1)
                pool.wait_ge(xr_in[kt // 4], 32 if kt >= 12 else 16)
                nc.gpsimd.tensor_tensor(mixT[:, kt], mixT[:, kt], xres(kt), ALU.add).then_inc(h_w, 1)
            weights_lo(at_h, (UNITS - 2) // 4)
            for kt in range(1, KT):
                pool.wait_ge(ysq2, kt + 1)
                if kt > 1:
                    pool.wait_ge(ysq_sum, kt - 1)
                nc.gpsimd.tensor_tensor(fsum, fsq[0] if kt == 1 else fsum, fsq[kt % 2], ALU.add).then_inc(ysq_sum, 1)
            pool.wait_ge(h_back, 16)
            for kt in range(KT):
                if kt not in VE_ADDS:
                    pool.wait_ge(y_m, kt + 1)
                    nc.gpsimd.tensor_tensor(acc[:, kt], acc[:, kt], x_hi[:, kt].bitcast(F32), ALU.add).then_inc(y_wp, 1)

        @block.scalar
        def _(act):
            def weight_hi(unit, half_unit, slot, r, wait=True):
                act.wait_ge(raw_in[r], 16 * half_unit + 16)
                if wait:
                    act.wait_ge(units_done, unit - 3)
                nc.scalar.activation(w_hi[:, slot], raw[:, r], ACT.Copy).then_inc(hi_ready, 1)

            def two_hi(unit, half_unit, slot):
                weight_hi(unit, half_unit, slot, 0)
                weight_hi(unit + 1, half_unit, slot + 1, 1)

            def hi_for(tile, half):
                weight_hi(2 * tile + 4 + half, tile + 2, 2 * tile % 4 + half, half)

            def root(out, psum, scale, done):
                nc.scalar.activation(halves(out), psum, ACT.Sqrt, bias=V("eps"), scale=scale).then_inc(done, 1)

            act.dma_start(vec[:], vecs).then_inc(vec_in, 16)
            act.dma_start(ident[:], ident_d).then_inc(const_in, 16)
            act.dma_start(sc_state, sconv_in).then_inc(sc_in, 16)
            weight_hi(0, 0, 0, 0, wait=False)
            act.dma_start(masks_f, masks_d).then_inc(masks_in, 16)
            for kt in range(KT):
                act.wait_ge(x_in[min(kt // 4, 2)], 32 if kt >= 8 else 16)
                if kt >= 2:
                    act.wait_ge(sq_used if kt % 2 else sq_sum, kt // 2)
                nc.scalar.activation(stage[:, kt % 2], xin[kt // 4][:, kt % 4 * T:(kt % 4 + 1) * T],
                                     ACT.Square).then_inc(sq_ready, 1)
                if kt == 3:
                    weight_hi(1, 0, 1, 1, wait=False)
            weight_hi(2, 1, 2, 0, wait=False)
            weight_hi(3, 1, 3, 1, wait=False)
            act.wait_ge(sq_used, KT // 2 + 1)
            act.wait_ge(vec_in, 16)
            root(rstd[:], work[:, 0:2, 0:HALF], 1.0 / D, root_ready)
            weight_hi(4, 2, 0, 0)
            weight_hi(5, 2, 1, 1)
            act.wait_ge(sc_in, 16)
            act.wait_ge(x_split, KT)
            for n in range(XBC_TILES):
                q, tile = pad[n % 2], n + 1
                smp = q[:, SC - 1 + SEQ:].rearrange("p (b t) -> p b t", b=BATCHES)
                hi_for(tile, 0)
                if n >= 2:
                    act.wait_ge(taps, n - 1)
                nc.scalar.activation(smp[:, :, 0:SC - 1], sc_state[:, n], ACT.Copy).then_inc(pad_st, 1)
                hi_for(tile, 1)
                act.wait_ge(taken, tile + 3)
                act.wait_ge(pad_st, n + 1)
                act.wait_ge(pad_zero, 1)
                nc.scalar.activation(conv_t[n % 2][:, 0:CONVW], q[:, 0:CONVW], ACT.Identity,
                                     bias=V("conv_b", n), scale=V("conv_w", 4 * n)).then_inc(tap0, 1)
                nc.scalar.activation(sconv_o[:, n, 0:SC - 1], q[:, SEQ:SEQ + SC - 1], ACT.Copy)
                nc.scalar.activation(sconv_o[:, n, SC - 1:].rearrange("p (b c) -> p b c", b=BATCHES),
                                     smp[:, :, DEC:], ACT.Copy).then_inc(sco, 1)
                if n == 1:
                    act.wait_ge(dts, 1)
                    nc.scalar.activation(V("A_log", rows=SH), V("A_log", rows=SH), ACT.Exp)
                    nc.scalar.activation(dt_tmp[0], dt_tmp[0], ACT.Exp).then_inc(dte, 1)
                act.wait_ge(taps, n + 1)
                nc.scalar.activation(XC[:, n, 0:SEQ], conv_t[n % 2][:, 0:SEQ], ACT.Silu)
                nc.scalar.activation(
                    XC[:, n, SEQ:].rearrange("p (b t) -> p b t", b=BATCHES),
                    conv_t[n % 2][:, SEQ + SC - 1:].rearrange("p (b t) -> p b t", b=BATCHES)[:, :, 0:DEC], ACT.Silu)\
                    .then_inc(conv_out, 1)
            act.wait_ge(sco, XBC_TILES)
            act.dma_start(sconv_out, sconv_o).then_inc(sconv_st, 16)

            def ssd_step(k):
                c, g = k // SG, k % SG
                if g == 0:
                    act.wait_ge(small_out, c + 1)
                    nc.scalar.activation(tok[:, c, 32:64], tok[:, c, 32:64], ACT.Exp).then_inc(wd_exp, 1)
                act.wait_ge(e_mm, k + 1)
                if k >= 1:
                    act.wait_ge(y_out, k)
                nc.scalar.activation(ecum, work[:, 3, :], ACT.Exp).then_inc(e_exp, 1)
                act.wait_ge(D_ready, k + 1)
                nc.scalar.activation(W[:, 8 * g:8 * g + 8, :], W[:, 8 * g:8 * g + 8, :], ACT.Exp, scale=-1.0)\
                    .then_inc(W_exp, 1)

            def ssd_samples():
                act.wait_ge(small_out, NC + 1)
                nc.scalar.activation(decay[:], work[:, 2, 272:336], ACT.Exp)
                nc.scalar.activation(tok[0:SMP, NC, 32:48], tok[0:SMP, NC, 32:48], ACT.Exp).then_inc(wd_exp, 1)
                act.wait_ge(e_mm, SG * NC + 1)
                act.wait_ge(y_out, SG * NC)
                nc.scalar.activation(ecum, work[:, 3, :], ACT.Exp).then_inc(e_exp, 1)
                act.wait_ge(D_ready, SG * NC + 1)
                nc.scalar.activation(W[0:SMP, :, 0:SMP], W[0:SMP, :, 0:SMP], ACT.Exp, scale=-1.0).then_inc(W_exp, 1)

            def ssd_batch(b):
                act.wait_ge(hs_ready, b + 1)
                act.dma_start(ssd_s[:, b], hns[:, b % 2]).then_inc(hs_out[b % 2], 16)
                if b + 2 < BATCHES:
                    act.wait_ge(hs_mm, b + 1)
                    act.dma_start(hTs[:, b % 2], ssdT_in[:, b + 2]).then_inc(hs_in[b % 2], 16)
                    act.wait_ge(hs_out[b % 2], 16 * (b // 2 + 1))
                    act.dma_start(hns[:, b % 2], ssd_in[:, b + 2]).then_inc(hs_in[b % 2], 16)

            def gates():
                for h in range(GH):
                    act.wait_ge(gate_mm, h + 1)
                    nc.scalar.activation(halves(GE[:, h * T:(h + 1) * T]),
                                         work[:, 2 * (h % 2):2 * (h % 2) + 2, 0:HALF],
                                         ACT.Identity, bias=V("gate_b", h)).then_inc(gate_out, 1)
                act.wait_ge(ylo_kept, 16)
                for j in range(2):
                    act.wait_ge(spilled[j], 16 * 8)
                for buf, n in ((GQ, Q_N), (GKK, K_N)):
                    act.dma_start(buf.rearrange("p (n t) -> p n t", n=GH),
                                  spill[n:n + GH].rearrange("n p t -> p n t")).then_inc(qk_in, 16)
                act.wait_ge(gate_sub, 1)
                nc.scalar.activation(GE2, GE2, ACT.Exp).then_inc(gate_exp, 1)
                act.wait_ge(gate_exp, 1)
                nc.scalar.activation(GE2, GE2, ACT.Ln, bias=1.0).then_inc(gate_ln, 1)

            def level(s):
                act.wait_ge(sub_ready, s)
                buf = GE if s % 2 else GE2
                view = buf if LEVELS[s - 1] <= 4 else buf.rearrange("p (h t) -> p h t", h=GH)[:, :, 0:SEQ]
                nc.scalar.activation(view, view, ACT.Exp, scale=1.0 / GATE_NORM).then_inc(exp_ready, 1)

            def gla_batch(b):
                act.wait_ge(s1_ready, b + 1)
                act.dma_start(gla_s[:, b * GH:(b + 1) * GH, :], s0ring[:, b % 2]).then_inc(s0_out[b % 2], 16)
                if b + 2 < BATCHES:
                    act.wait_ge(s0_out[b % 2], 16 * (b // 2 + 1))
                    act.dma_start(s0ring[:, b % 2], gla_in[:, (b + 2) * GH:(b + 3) * GH, :])\
                        .then_inc(s0_in[b % 2], 16)

            def gap(m):
                if m < 5:
                    n = P if m < 4 else SMP
                    act.wait_ge(xtr, m + 1)
                    nc.scalar.activation(B_tok[0:n, m].rearrange("p g n -> p (g n)"), work[0:n, 2, 0:SG * SN],
                                         ACT.Copy).then_inc(b_out, 1)
                if GAP_STEP <= m < GAP_SMP and (m - GAP_STEP) % 2 == 0:
                    ssd_step((m - GAP_STEP) // 2)
                if m == GAP_SMP - 1:
                    act.wait_ge(h_ready, SG * NC)
                    act.dma_start(ssd_p, hT).then_inc(ssd_p_out, 16)
                    for b in range(2):
                        act.dma_start(hTs[:, b], ssdT_in[:, b]).then_inc(hs_in[b], 16)
                        act.dma_start(hns[:, b], ssd_in[:, b]).then_inc(hs_in[b], 16)
                if m == GAP_SMP:
                    ssd_samples()
                if GAP_SMP + 2 <= m < GAP_SMP + 2 + BATCHES:
                    ssd_batch(m - GAP_SMP - 2)
                if m == GAP_YNORM - 3:
                    for j in range(2):
                        act.wait_ge(hs_out[j], 16 * BATCHES // 2)
                        act.wait_ge(spilled[j], 16 * 4)
                    act.wait_ge(y_out, SG * NC + 1)
                    act.dma_start(zT, spill[Z_N:Z_N + 8].rearrange("n p t -> p n t")).then_inc(z_in, 16)
                if m == GAP_YNORM - 2:
                    act.wait_ge(z_in, 16)
                    nc.scalar.activation(zT, zT, ACT.Silu).then_inc(zsilu, 1)
                if m == GAP_YNORM - 1:
                    act.wait_ge(yz, 1)
                    act.wait_ge(ssd_p_out, 16)
                    nc.scalar.activation(ysq, XC[:, 0:8, :], ACT.Square).then_inc(ysq_r, 1)
                    act.dma_start(w_gate2[32:32 + RANK, :], gate2).then_inc(gate2_in, 16)
                if m == GAP_YNORM:
                    for g in range(SG):
                        act.wait_ge(ysum, g + 1)
                        root(zT[:, g], work[:, 2 * g:2 * g + 2, 0:HALF], 1.0 / (SH * SD // SG), yroot)
                if m in (GAP_YNORM, GAP_YNORM + 2):
                    g = (m - GAP_YNORM) // 2
                    for j in range(4 * g, 4 * g + 4):
                        act.wait_ge(ymix, j + 1)
                        nc.scalar.activation(y_hi[:, j], XC[:, j], ACT.Copy).then_inc(yhi, 1)
                if m == GAP_YNORM + 3:
                    act.wait_ge(ylo, 8)
                    act.dma_start(y_spill[1].rearrange("n p t -> p n t"), XC[:, 0:8, :]).then_inc(ylo_kept, 16)
                    act.dma_start(y_spill[0].rearrange("n p t -> p n t"), ysq).then_inc(y_kept, 16)
                if m == GAP_GATE:
                    gates()
                if GAP_ATT <= m < GAP_ATT + 14 and (m - GAP_ATT) % 2 == 0:
                    level((m - GAP_ATT) // 2 + 1)
                if m == GAP_ATT + 14:
                    act.wait_ge(sub_ready, 8)
                    nc.scalar.activation(GE, GE, ACT.Exp, scale=1.0 / GATE_NORM).then_inc(exp_ready, 1)
                    nc.scalar.activation(GE2, GB, ACT.Exp, scale=1.0 / GATE_NORM).then_inc(exp_ready, 1)
                if GAP_V <= m <= GAP_V + 14 and (m - GAP_V) % 2 == 0:
                    i = (m - GAP_V) // 2
                    act.wait_ge(v_tr, i + 1)
                    nc.scalar.activation(v_tok[:, 0:4, i * P:(i + 1) * P],
                                         work[:, i % 2, :].rearrange("p (a b) -> p a b", a=4), ACT.Copy)
                    nc.scalar.activation(v_tok[0:SMP, 4, i * P:(i + 1) * P],
                                         work[0:SMP, 2 + i % 2, 0:P], ACT.Copy).then_inc(v_out, 1)
                if m == GAP_KD:
                    act.wait_ge(qd_ready, 1)
                if m in (GAP_KD, GAP_KD + 2):
                    for tt in (range(4) if m == GAP_KD else (4,)):
                        n = P if tt < 4 else SMP
                        act.wait_ge(kd_tr, tt + 1)
                        nc.scalar.activation(kd_tok[0:n, tt, :], work[0:n, tt % 4, :], ACT.Copy).then_inc(kd_out, 1)
                if m == GAP_KD + 2:
                    for b in range(2):
                        act.dma_start(s0ring[:, b], gla_in[:, b * GH:(b + 1) * GH, :]).then_inc(s0_in[b], 16)
                if GAP_CHUNK <= m < GAP_CHUNK + NC:
                    c = m - GAP_CHUNK
                    act.wait_ge(o_mm, c + 1)
                    nc.scalar.activation(oT[:, :, c * CH:(c + 1) * CH],
                                         work[:, 0:2, :].rearrange("p a (b t) -> p (a b) t", b=4), ACT.Copy)\
                        .then_inc(o_out, 1)
                if m == GAP_GSMP:
                    act.wait_ge(S_ready, NC)
                    act.dma_start(gla_p, S).then_inc(gla_p_out, 16)
                if m >= GAP_GSMP:
                    gla_batch(m - GAP_GSMP)

            for n in range(BESIDE):
                hi_for(N_TILE0 + n, 0)
                if n >= 1:
                    gap(2 * n - 1)
                hi_for(N_TILE0 + n, 1)
                if not V_N <= n < V_N + 8:
                    act.wait_ge(taken, N_TILE0 + n + 3)
                    act.dma_start(spill[n], stage[:, n % 2]).then_inc(spilled[n % 2], 16)
                if n == BESIDE - 1:
                    act.wait_ge(units_done, OUT_UNIT0)
                    act.wait_ge(y_kept, 16)
                    for i in range(4):
                        a, z = 2 * i, 2 * i + 2
                        act.dma_start(x_hi[:, a:z, :].bitcast(F32), y_spill[0, a:z].rearrange("n p t -> p n t"))\
                            .then_inc(yb_in[i], 16)
                        act.dma_start(x_lo[:, 8 + a:8 + z, :].bitcast(F32), y_spill[1, a:z].rearrange("n p t -> p n t"))\
                            .then_inc(yb_in[i], 16)
                gap(2 * n)
            def squares(h):
                if h >= 1:
                    act.wait_ge(gss, h)
                nc.scalar.activation(GE[:, 0:2 * T].rearrange("p (n t) -> p n t", n=2), oT[:, 2 * h:2 * h + 2, :],
                                     ACT.Square).then_inc(gsq, 1)

            def late(d):
                if d < 6:
                    gla_batch(d + 2)
                if d == 6:
                    act.wait_ge(os_mm, 1)
                    nc.scalar.activation(oT[:, :, SEQ:T], work[:, 0, :].rearrange("p (n t) -> p n t", n=8), ACT.Copy)\
                        .then_inc(os_out, 1)
                    for j in range(2):
                        act.wait_ge(spilled[j], 16 * 12)
                    act.dma_start(gT[:, 0:4, :], spill[G_N:G_N + 4].rearrange("n p t -> p n t")).then_inc(g_in, 16)
                    act.dma_start(gT[:, 4:8, :], spill[G2_N:G2_N + 4].rearrange("n p t -> p n t")).then_inc(g_in, 16)
                    act.wait_ge(os_out, 1)
                    for j in range(2):
                        act.wait_ge(s0_out[j], 16 * BATCHES // 2)
                    squares(0)
                if d == 7:
                    act.wait_ge(g_in, 32)
                    nc.scalar.activation(gT, gT, ACT.Silu).then_inc(gsilu, 1)
                if 8 <= d < 8 + GH:
                    h = d - 8
                    act.wait_ge(gsum, h + 1)
                    root(GQ[:, h * T:(h + 1) * T], work[:, 0:2, 0:HALF], 1.0 / GV, groot)
                    if h + 1 < GH:
                        squares(h + 1)
                if d == 12:
                    for h in range(GH):
                        act.wait_ge(gy, h + 1)
                        nc.scalar.activation(gla_hi(2 * h, 2), oT[:, 2 * h:2 * h + 2, :], ACT.Copy).then_inc(ghi, 1)

            late(-1)
            for d in range(KT):
                weight_hi(OUT_UNIT0 + 4 + d, OUT_UNIT0 // 2 + 2 + d // 2, (2 + d) % 4, d % 2)
                late(d)

            act.wait_ge(mix_in, 4)
            for c in range(3):
                act.dma_start(A(9216 + 2304 * c, 2304), xT[c]).then_inc(xr_in[c], 16)
            act.dma_start(A(9216 + 3 * 2304, T), xT[3, :, 0:T]).then_inc(xr_in[3], 16)
            act.dma_start(TL(0, 3 * T), xT[3, :, T:4 * T]).then_inc(xr_in[3], 16)
            with act.Fori(0, KT // 4) as i:
                two_hi(4 * i + OUT_UNIT0 + 4 + KT, 2 * i + OUT_UNIT0 // 2 + 2 + KT // 2, 2)
                for j in range(4):
                    act.wait_ge(taken, 4 * i + j + OUT_TILE0 + KT + 3)
                    act.wait_ge(sq_free, 4 * i + j + 1)
                    nc.scalar.activation(sq[j % 2], mix[:, bass.ds(4 * i + j, 1), :].rearrange("p o t -> p (o t)"),
                                         ACT.Square).then_inc(msq, 1)
                    if j == 1:
                        two_hi(4 * i + OUT_UNIT0 + 6 + KT, 2 * i + OUT_UNIT0 // 2 + 3 + KT // 2, 0)
            act.wait_ge(msum_mm, 1)
            root(rstd[:], work[:, 0:2, 0:HALF], 1.0 / D, mroot)
            for kt in range(KT):
                act.wait_ge(h_w, kt + 1)
                if kt >= 2:
                    act.wait_ge(hsq_mm, kt - 1)
                nc.scalar.activation(sq[kt % 2], mixT[:, kt], ACT.Square).then_inc(hsq, 1)
                nc.scalar.activation(x_hi[:, kt], mixT[:, kt], ACT.Copy, scale=V("ffn_pre", kt)).then_inc(h_hi, 1)
            act.dma_start(h_spill.rearrange("n p t -> p n t"), mixT).then_inc(h_st, 16)
            act.wait_ge(h_split, KT)
            act.dma_start(fstate, fconv_in).then_inc(ffn_in, 16)
            act.dma_start(fvec, fvec_d).then_inc(ffn_in, 16)
            weight_hi(FFN_UNIT0 + 4, FFN_UNIT0 // 2 + 2, 2, 0)
            act.wait_ge(hsq_mm, KT)
            root(rstd[:], work[:, 0:2, 0:HALF], 1.0 / D, mroot)

            def ffn_up(blk, q, unit, half_unit, first=False):
                act.wait_ge(ffn_in, 32)
                if not first:
                    act.wait_ge(f_taps, 4 * blk - 3)
                nc.scalar.activation(fc[q], fvec[:, bass.ds(blk, 1), :].rearrange("p o c -> p (o c)"), ACT.Copy)\
                    .then_inc(fc_ready, 1)
                for j in range(4):
                    t, pair = 4 * blk + j, 2 * blk + j // 2
                    pd = fpad[j % 2]
                    smp = pd[:, FC - 1 + SEQ:].rearrange("p (b t) -> p b t", b=BATCHES)
                    if not (first and j < 2):
                        act.wait_ge(f_taps, t - 1)
                    nc.scalar.activation(
                        smp[:, :, 0:FC - 1],
                        fstate[:, bass.ds(blk, 1), 16 * j:16 * j + 16].rearrange("p o (b t) -> p (o b) t", b=BATCHES),
                        ACT.Copy).then_inc(f_st, 1)
                    act.wait_ge(taken, 20 * blk + j + (FFN_TILE0 + 3 if first else FFN_TILE0 + 3 - 16))
                    act.wait_ge(fc_ready, blk + 1)
                    act.wait_ge(f_st, t + 1)
                    if j % 2 and not (first and j == 1):
                        act.wait_ge(f_prod, pair)
                    act.wait_ge(fpad_zero, 1)
                    nc.scalar.activation(ftap[j % 2][:, 0:FCONVW], pd[:, 0:FCONVW], ACT.Identity,
                                         bias=fc[q][:, 4 * j + 3:4 * j + 4], scale=fc[q][:, 4 * j:4 * j + 1])\
                        .then_inc(f_tap0, 1)
                    nc.scalar.activation(fout[:, bass.ds(blk, 1), 18 * j:18 * j + 2].rearrange("p o c -> p (o c)"),
                                         pd[:, SEQ:SEQ + FC - 1], ACT.Copy)
                    nc.scalar.activation(
                        fout[:, bass.ds(blk, 1), 18 * j + 2:18 * j + 18].rearrange("p o (b t) -> p (o b) t", b=BATCHES),
                        smp[:, :, DEC:], ACT.Copy).then_inc(f_padout, 1)
                    if not (first and j == 0):
                        two_hi(unit + 2 * j, half_unit + j, (2 + 2 * j) % 4)
                    if j % 2:
                        a = ftap[0]
                        act.wait_ge(f_taps, t)
                        if not (first and j == 1):
                            act.wait_ge(act_ready, pair)
                        nc.scalar.activation(fgate[:, 0:SEQ], a[:, 0:SEQ], ACT.Silu)
                        nc.scalar.activation(
                            fgate[:, SEQ:T].rearrange("p (b t) -> p b t", b=BATCHES),
                            a[:, SEQ + FC - 1:].rearrange("p (b t) -> p b t", b=BATCHES)[:, :, 0:DEC], ACT.Silu)\
                            .then_inc(f_silu, 1)
                        act.wait_ge(f_prod, pair + 1)
                        nc.scalar.activation(g_hi[:, q, j // 2], fgate, ACT.Copy).then_inc(f_hi, 1)

            def ffn_down(unit, half_unit):
                two_hi(unit, half_unit, 2)
                two_hi(unit + 2, half_unit + 1, 0)

            weight_hi(FFN_UNIT0 + 5, FFN_UNIT0 // 2 + 2, 3, 1)
            act.wait_ge(sconv_st, 16)
            U = FFN_UNIT0 + 4
            ffn_up(0, 0, U, U // 2, first=True)
            with act.Fori(0, (BLOCKS - 2) // 2) as i:
                for q in (1, 0):
                    blk = 2 * i + (1 if q else 2)
                    u = 24 * i + U + 8 + (0 if q else 12)
                    hu = 12 * i + (U + 8) // 2 + (0 if q else 6)
                    ffn_up(blk, q, u, hu)
                    ffn_down(u + 8, hu + 4)
            u = U + 8 + 12 * (BLOCKS - 2)
            ffn_up(BLOCKS - 1, 1, u, u // 2)
            ffn_down(u + 8, u // 2 + 4)
            act.wait_ge(f_padout, 4 * BLOCKS)
            act.dma_start(fconv_out, fout).then_inc(fo_st, 16)
            act.dma_start(x_hi[:].bitcast(F32), h_spill.rearrange("n p t -> p n t")).then_inc(h_back, 16)
            act.wait_ge(f_taps, 4 * BLOCKS)
            for kt in range(KT):
                act.wait_ge(taken, FFN_TILE0 + 20 * BLOCKS - KT + kt + 3)
                if kt >= 2:
                    act.wait_ge(ysq_sum, max(kt - 2, 1))
                nc.scalar.activation(fsq[kt % 2], acc[:, kt], ACT.Square).then_inc(ysq2, 1)
            act.wait_ge(ysq_mm, 1)
            root(rstd[:], work[:, 0:2, 0:HALF], 1.0 / D, mroot)
            for n in range(4):
                by_ve = sum(kt < 4 * (n + 1) for kt in VE_ADDS)
                act.wait_ge(y_w, by_ve)
                act.wait_ge(y_wp, 4 * (n + 1) - by_ve)
                act.dma_start(yT[n], acc[:, 4 * n:4 * n + 4, :]).then_inc(y_st, 16)
            act.wait_ge(y_st, 64)
            act.wait_ge(fo_st, 16)
            act.wait_ge(sconv_st, 16)
            act.wait_ge(ssd_p_out, 16)
            act.wait_ge(gla_p_out, 16)
            for j in range(2):
                act.wait_ge(s0_out[j], 16 * BATCHES // 2)
                act.wait_ge(hs_out[j], 16 * BATCHES // 2)

        @block.tensor
        def _(pe):
            def products(slot, k, ring, split, first, last, hi, lo):
                cuts = ((0, 0, split), (1, split, T))
                for n, a, b in cuts:
                    for part in (0, 1):
                        nc.tensor.matmul(psum_proj[:, 2 * ring + n, 0:b - a], w_hi[:, slot, k], (hi, lo)[part][:, a:b],
                                         start=first and part == 0, stop=False)
                for n, a, b in cuts:
                    mm = nc.tensor.matmul(psum_proj[:, 2 * ring + n, 0:b - a], w_lo[:, slot, k], hi[:, a:b],
                                          start=False, stop=last)
                return mm

            def project(tile, unit, slot, ring, split=HALF, before=None, middle=None):
                pe.wait_ge(taken, tile + 1)
                for half in range(2):
                    pe.wait_ge(lo_ready, unit + half + 1)
                    if half and middle:
                        middle()
                    for k in range(8):
                        kt = 8 * half + k
                        if before:
                            before(kt)
                        mm = products(slot + half, k, ring, split, kt == 0, kt == KT - 1, x_hi[:, kt], x_lo[:, kt])
                        if k == 7:
                            mm.then_inc(units_done, 1)

            def pair(p, split):
                project(2 * p + 1, 4 * p + 2, 2, 1, split)
                project(2 * p + 2, 4 * p + 4, 0, 0, split)

            def sum_tokens(sources, bank, done, start=True, stop=True):
                for n in range(2):
                    for i, s in enumerate(sources):
                        mm = nc.tensor.matmul(work[:, bank + n, 0:HALF], ones[:], s[:, n * HALF:(n + 1) * HALF],
                                              start=start and i == 0, stop=stop and i == len(sources) - 1)
                mm.then_inc(done, 1)

            def x_arrives(kt):
                if kt % 2:
                    pe.wait_ge(sq_ready, kt + 1)
                    sum_tokens([stage[:, 1]], 0, sq_used, kt == 1, False)
                pe.wait_ge(x_split, kt + 1)

            pe.wait_ge(setup, 2)
            project(0, 0, 0, 0, before=x_arrives)
            pe.wait_ge(sq_sum, KT // 2)
            sum_tokens([xsum], 0, sq_used, False, True)
            with pe.Fori(0, XBC_TILES // 2) as i:
                pair(i, split=256)

            def ssd_before(k):
                c, g = k // SG, k % SG
                a, z = c * CH, (c + 1) * CH
                if k >= 1:
                    pe.wait_ge(y_out, k)
                if g == 0:
                    for gg in range(SG):
                        nc.tensor.matmul(work[:, 2, gg * CH:(gg + 1) * CH], XC[:, 8 + gg, a:z], XC[:, 10 + gg, a:z],
                                         start=True, stop=True)
                    nc.tensor.matmul(work[:, 2, 256:256 + SH], cumT[:, z - 1:z].broadcast_to([SH, P]), ident[0:SH, 0:SH],
                                     start=True, stop=True).then_inc(small_mm, 1)
                if k >= 1:
                    pe.wait_ge(h_ready, k)
                for i in range(8):
                    h = 8 * g + i
                    mm = nc.tensor.matmul(work[:, i // 4, i % 4 * CH:(i % 4 + 1) * CH],
                                          ident[0:SH, h:h + 1].broadcast_to([SH, P]), cumT[:, a:z],
                                          start=True, stop=True)
                mm.then_inc(bc_mm, 1)
                for i in range(8):
                    h = 8 * g + i
                    mm = nc.tensor.matmul(work[i % 2 * SD:(i % 2 + 1) * SD, 3, i // 2 * CH:(i // 2 + 1) * CH],
                                          ident[0:SH, h:h + 1].broadcast_to([SH, SD]), cumT[:, a:z],
                                          start=True, stop=True)
                mm.then_inc(e_mm, 1)

            def ssd_after(k):
                c, g = k // SG, k % SG
                a, z = c * CH, (c + 1) * CH
                pe.wait_ge(small_out, c + 1)
                for i in range(4):
                    j = 4 * g + i
                    nc.tensor.matmul(work[:, 2, i * CH:(i + 1) * CH], hT[:, j * P:(j + 1) * P], XC[:, 10 + g, a:z],
                                     start=True, stop=True)
                pe.wait_ge(e_exp, k + 1)
                pe.wait_ge(W_ready, k + 1)
                for i in range(8):
                    h = 8 * g + i
                    mm = nc.tensor.matmul(work[i % 2 * SD:(i % 2 + 1) * SD, 3, i // 2 * CH:(i // 2 + 1) * CH],
                                          xdt[:, c, h * SD:(h + 1) * SD], W[:, h, :], start=True, stop=True)
                mm.then_inc(y_mm, 1)
                pe.wait_ge(xw_ready, c + 1)
                nc.tensor.matmul(work[:, g, :], B_tok[:, c, g, :], xw[:, g * 512:(g + 1) * 512],
                                 start=True, stop=True).then_inc(h_mm, 1)

            def ssd_samples_before():
                pe.wait_ge(y_out, SG * NC)
                for g in range(SG):
                    nc.tensor.matmul(work[0:SMP, 2, g * SMP:(g + 1) * SMP], XC[:, 8 + g, SEQ:T], XC[:, 10 + g, SEQ:T],
                                     start=True, stop=True)
                nc.tensor.matmul(work[0:SMP, 2, 256:256 + SH], lastrow, ident[0:SH, 0:SH], start=True, stop=True)
                for h in range(SH):
                    at = 272 + h // 2 * BATCHES
                    mm = nc.tensor.matmul(work[h % 2 * SD:(h % 2 + 1) * SD, 2, at:at + BATCHES],
                                          ident[0:SH, h:h + 1].broadcast_to([SH, SD]), cumT[:, SEQ + DEC - 1:T:DEC],
                                          start=True, stop=True)
                mm.then_inc(small_mm, 1)
                pe.wait_ge(h_ready, SG * NC)
                for h in range(SH):
                    mm = nc.tensor.matmul(work[0:SMP, h // 8, h % 8 * SMP:(h % 8 + 1) * SMP],
                                          ident[0:SH, h:h + 1].broadcast_to([SH, SMP]), cumT[:, SEQ:T],
                                          start=True, stop=True)
                mm.then_inc(bc_mm, 1)
                for h in range(SH):
                    mm = nc.tensor.matmul(work[h % 2 * SD:(h % 2 + 1) * SD, 3, h // 2 * SMP:(h // 2 + 1) * SMP],
                                          ident[0:SH, h:h + 1].broadcast_to([SH, SD]), cumT[:, SEQ:T],
                                          start=True, stop=True)
                mm.then_inc(e_mm, 1)

            def ssd_samples_after():
                pe.wait_ge(e_exp, SG * NC + 1)
                pe.wait_ge(W_ready, SG * NC + 1)
                for h in range(SH):
                    mm = nc.tensor.matmul(work[h % 2 * SD:(h % 2 + 1) * SD, 3, h // 2 * SMP:(h // 2 + 1) * SMP],
                                          xdt[0:SMP, 4, h * SD:(h + 1) * SD], W[0:SMP, h, 0:SMP], start=True, stop=True)
                mm.then_inc(y_mm, 1)

            def ssd_batch(b):
                if b == 0:
                    pe.wait_ge(wd_exp, NC + 1)
                    pe.wait_ge(small_out, NC + 1)
                    pe.wait_ge(sm_ready, 1)
                pe.wait_ge(hs_in[b % 2], 32 * (b // 2 + 1))
                for j in range(8):
                    at = j * SMP + b * DEC
                    nc.tensor.matmul(work[:, 2, at:at + DEC], hTs[:, b % 2, j * P:(j + 1) * P],
                                     XC[:, 10 + j // 4, SEQ + b * DEC:SEQ + (b + 1) * DEC], start=True, stop=True)
                if b >= 1:
                    pe.wait_ge(hs_ready, b)
                for j in range(8):
                    mm = nc.tensor.matmul(work[:, j // 4, j % 4 * SN:(j % 4 + 1) * SN], xw[0:SMP, j * P:(j + 1) * P],
                                          Bm[:, b, j // 4, :], start=True, stop=True)
                mm.then_inc(hs_mm, 1)

            def gates():
                pe.wait_ge(gate2_in, 16)
                pe.wait_ge(yroot, SG)
                for h in range(GH):
                    if h >= 2:
                        pe.wait_ge(gate_out, h - 1)
                    for n in range(2):
                        mm = nc.tensor.matmul(work[:, 2 * (h % 2) + n, 0:HALF],
                                              w_gate2[32:32 + RANK, h * GK:(h + 1) * GK],
                                              misc[32:32 + RANK, n * HALF:(n + 1) * HALF], start=True, stop=True)
                    mm.then_inc(gate_mm, 1)

            def att_step(s):
                k, q = (GKK, GQ) if s == 0 else (GE, GE) if s % 2 else (GE2, GE2)
                if s == 0:
                    pe.wait_ge(qk_in, 32)
                    pe.wait_ge(gate_out, GH)
                else:
                    pe.wait_ge(pq_ready, s)
                    if s >= 2:
                        pe.wait_ge(v_out, s - 1)
                for h in range(GH):
                    for c in range(NC):
                        at = h * T + c * CH
                        mm = nc.tensor.matmul(work[:, h, c * CH:(c + 1) * CH], k[:, at:at + CH], q[:, at:at + CH],
                                              start=True, stop=True)
                    mm.then_inc(att_mm, 1)
                if s in SAMPLE_STEPS:
                    pe.wait_ge(att_out, att_base(s) + 1)
                    for h in range(GH):
                        at = h * T + SEQ
                        mm = nc.tensor.matmul(work[0:SMP, 0, h * SMP:(h + 1) * SMP], k[:, at:at + SMP],
                                              q[:, at:at + SMP], start=True, stop=True)
                    mm.then_inc(att_mm, 1)

            def v_by_tokens(i):
                pe.wait_ge(taken, N_TILE0 + V_N + i + 3)
                pe.wait_ge(att_out, att_base(min(i + 2, 8)))
                if i == 7:
                    pe.wait_ge(kd_out, 4)
                for tt in range(4):
                    nc.tensor.transpose(work[:, i % 2, tt * P:(tt + 1) * P], stage[:, i % 2, tt * P:(tt + 1) * P],
                                        ident[:])
                nc.tensor.transpose(work[0:SMP, 2 + i % 2, 0:P], stage[:, i % 2, SEQ:T], ident[:]).then_inc(v_tr, 1)

            def keys_by_tokens(tiles):
                pe.wait_ge(kdT_ready, 1)
                pe.wait_ge(att_out, att_base(8))
                pe.wait_ge(v_out, 7 if tiles[0] == 0 else 8)
                if tiles[0]:
                    pe.wait_ge(kd_out, 4)
                for tt in tiles:
                    n = P if tt < 4 else SMP
                    for h in range(GH):
                        at = h * T + tt * P
                        mm = nc.tensor.transpose(work[0:n, tt % 4, h * GK:(h + 1) * GK], GE[:, at:at + n], ident[:])
                    mm.then_inc(kd_tr, 1)

            def gla_chunk(c):
                if c == 0:
                    pe.wait_ge(v_out, 8)
                    pe.wait_ge(kd_out, 5)
                    pe.wait_ge(qd_ready, 1)
                else:
                    pe.wait_ge(o_out, c)
                    pe.wait_ge(S_ready, c)
                for n in range(8):
                    h, vh = n // 2, n % 2
                    region = work[:, n // 4, n % 4 * CH:(n % 4 + 1) * CH]
                    mm = nc.tensor.matmul(region, v_tok[:, c, n * P:(n + 1) * P], att[:, h * NC + c, :],
                                          start=True, stop=c == 0)
                    if c >= 1:
                        at = h * T + c * CH
                        mm = nc.tensor.matmul(region, S[:, h, vh * P:(vh + 1) * P], GQ[:, at:at + CH],
                                              start=False, stop=True)
                mm.then_inc(o_mm, 1)
                for h in range(GH):
                    mm = nc.tensor.matmul(work[:, 2 + h // 2, h % 2 * GV:(h % 2 + 1) * GV],
                                          kd_tok[:, c, h * GK:(h + 1) * GK], v_tok[:, c, h * GV:(h + 1) * GV],
                                          start=True, stop=True)
                mm.then_inc(S_mm, 1)

            def gla_batch(b):
                if b == 0:
                    pe.wait_ge(o_out, NC)
                    for n in range(8):
                        nc.tensor.matmul(work[:, 0, n * SMP:(n + 1) * SMP], v_tok[0:SMP, 4, n * P:(n + 1) * P],
                                         att_s[:, n // 2, :], start=n == 0, stop=False, skip_group_check=True)
                pe.wait_ge(s0_in[b % 2], 16 * (b // 2 + 1))
                for n in range(8):
                    h, vh = n // 2, n % 2
                    at = h * T + SEQ + b * DEC
                    mm = nc.tensor.matmul(work[:, 0, n * SMP + b * DEC:n * SMP + (b + 1) * DEC],
                                          s0ring[:, b % 2, h, vh * P:(vh + 1) * P], GQ[:, at:at + DEC],
                                          start=False, stop=b == BATCHES - 1 and n == 7, skip_group_check=True)
                if b == BATCHES - 1:
                    mm.then_inc(os_mm, 1)
                pe.wait_ge(kdm_ready, b + 1)
                if b == 0:
                    pe.wait_ge(S_ready, NC)
                else:
                    pe.wait_ge(s1_ready, b)
                for h in range(GH):
                    mm = nc.tensor.matmul(work[:, 2 + h // 2, h % 2 * GV:(h % 2 + 1) * GV],
                                          kd_m[:, b % 2, h, :], v_tok[0:SMP, 4, h * GV:(h + 1) * GV],
                                          start=True, stop=True)
                mm.then_inc(s1_mm, 1)

            def gap(m):
                if m == 0:
                    pe.wait_ge(dt_ready, 2)
                    pe.wait_ge(root_ready, 1)
                    pe.wait_ge(const_in, 16)
                    for tt in range(5):
                        n = P if tt < 4 else SMP
                        for i, src in enumerate((dtT, cumT)):
                            mm = nc.tensor.transpose(work[0:n, 3, 32 * tt + SH * i:32 * tt + SH * (i + 1)],
                                                     src[:, tt * P:tt * P + n], ident[0:SH, 0:SH])
                    mm.then_inc(dttr, 1)
                    pe.wait_ge(conv_out, XBC_TILES)
                if m < 5:
                    n = P if m < 4 else SMP
                    if m >= 1:
                        pe.wait_ge(xdt_out, m)
                        pe.wait_ge(b_out, m)
                    for j in range(10):
                        mm = nc.tensor.transpose(work[0:n, j // 4, j % 4 * P:(j % 4 + 1) * P],
                                                 XC[:, j, m * P:m * P + n], ident[:])
                    mm.then_inc(xtr, 1)
                if m == GAP_STEP:
                    pe.wait_ge(xdt_out, 5)
                    pe.wait_ge(b_out, 5)
                    pe.wait_ge(dtt_out, 1)
                if GAP_STEP <= m < GAP_SMP:
                    (ssd_after if (m - GAP_STEP) % 2 else ssd_before)((m - GAP_STEP) // 2)
                if m == GAP_SMP:
                    ssd_samples_before()
                if m == GAP_SMP + 1:
                    ssd_samples_after()
                if GAP_SMP + 2 <= m < GAP_SMP + 2 + BATCHES:
                    ssd_batch(m - GAP_SMP - 2)
                if m == GAP_YNORM:
                    pe.wait_ge(y_out, SG * NC + 1)
                    pe.wait_ge(hs_ready, BATCHES)
                    pe.wait_ge(ysq_r, 1)
                    for g in range(SG):
                        sum_tokens([ysq[:, 4 * g + i] for i in range(4)], 2 * g, ysum)
                if m == GAP_GATE:
                    gates()
                if GAP_ATT <= m < GAP_ATT + 16 and (m - GAP_ATT) % 2 == 0:
                    att_step((m - GAP_ATT) // 2)
                if GAP_V <= m <= GAP_V + 14 and (m - GAP_V) % 2 == 0:
                    v_by_tokens((m - GAP_V) // 2)
                if m == GAP_KD:
                    keys_by_tokens(range(4))
                if m == GAP_KD + 2:
                    keys_by_tokens((4,))
                if GAP_CHUNK <= m < GAP_CHUNK + NC:
                    gla_chunk(m - GAP_CHUNK)
                if m >= GAP_GSMP:
                    gla_batch(m - GAP_GSMP)

            for n in range(BESIDE):
                tile = N_TILE0 + n
                project(tile, 2 * tile, 2 * tile % 4, tile % 2, middle=(lambda: gap(2 * n - 1)) if n else None)
                gap(2 * n)

            def half_tile(tile, unit, slot, ring, ops, first=False):
                pe.wait_ge(taken, tile + 1)
                pe.wait_ge(lo_ready, unit + 1)
                for k in range(8):
                    if first and k % 2 == 0:
                        pe.wait_ge(yb_in[k // 2], 32)
                    mm = products(slot, k, ring, HALF, k == 0, k == 7, *ops(k))
                mm.then_inc(units_done, 1)

            def late(d):
                if d < 6:
                    gla_batch(d + 2)
                if 8 <= d < 8 + GH:
                    h = d - 8
                    pe.wait_ge(os_out, 1)
                    pe.wait_ge(gss, h + 1)
                    if h >= 1:
                        pe.wait_ge(groot, h)
                    sum_tokens([gsum2], 0, gsum)

            late(-1)
            for d in range(KT):
                half_tile(OUT_TILE0 + d, OUT_UNIT0 + d, (2 + d) % 4, (1 + d) % 2,
                          lambda k: (x_hi[:, k], x_lo[:, 8 + k]), first=d == 0)
                late(d)
            pe.wait_ge(mix_in, GH)
            with pe.Fori(0, KT // 4) as i:
                for j in range(4):
                    half_tile(4 * i + j + OUT_TILE0 + KT, 4 * i + j + OUT_UNIT0 + KT, (2 + j) % 4, (1 + j) % 2,
                              lambda k: (gla_hi(k)[:, 0], gla_lo(k)[:, 0]))
            pe.wait_ge(sq_free, KT + 2)
            sum_tokens([sqsum], 0, msum_mm)
            pe.wait_ge(mroot, 1)

            def h_arrives(kt):
                pe.wait_ge(hsq, kt + 1)
                sum_tokens([sq[kt % 2]], 0, hsq_mm, kt == 0, kt == KT - 1)
                pe.wait_ge(h_split, kt + 1)

            def up(tile, unit, before=None):
                for j in range(4):
                    project(tile + j, unit + 2 * j, (2 + 2 * j) % 4, (1 + j) % 2, split=256, before=before if j == 0 else None)

            def down(blk, q, tile, unit):
                pe.wait_ge(act_ready, 2 * blk + 2)
                for d in range(KT):
                    if d % 4 == 0:
                        pe.wait_ge(lo_ready, unit + d // 4 + 1)
                    pe.wait_ge(taken, tile + d + 1)
                    for k in range(2):
                        mm = products((2 + d // 4) % 4, d % 4 * 2 + k, (1 + d) % 2, HALF, k == 0, k == 1,
                                      g_hi[:, q, k], g_lo[:, q, k])
                    mm.then_inc(units_done if d % 4 == 3 else down_mm, 1)

            up(FFN_TILE0, FFN_UNIT0, before=h_arrives)
            with pe.Fori(0, (BLOCKS - 2) // 2) as i:
                for q in (1, 0):
                    b = 1 if q else 2
                    tile, unit = FFN_TILE0 - 16 + 20 * b, FFN_UNIT0 - 4 + 12 * b
                    up(40 * i + tile, 24 * i + unit)
                    down(2 * i + b - 1, 1 - q, 40 * i + tile + 4, 24 * i + unit + 8)
            tile, unit = FFN_TILE0 - 16 + 20 * (BLOCKS - 1), FFN_UNIT0 - 4 + 12 * (BLOCKS - 1)
            up(tile, unit)
            down(BLOCKS - 2, 0, tile + 4, unit + 8)
            down(BLOCKS - 1, 1, tile + 20, unit + 12)
            pe.wait_ge(ysq_sum, KT - 1)
            sum_tokens([fsum], 0, ysq_mm)

        @block.vector
        def _(ve):
            steps = [0]

            def own(instruction):
                instruction.then_inc(own_step, 1)
                steps[0] += 1

            def settle():
                ve.wait_ge(own_step, steps[0])

            tt_op, ts_op, stt = nc.vector.tensor_tensor, nc.vector.tensor_scalar, nc.vector.scalar_tensor_tensor

            nc.vector.memset(ones[:], 1.0).then_inc(setup, 1)
            nc.vector.memset(xsum, 0.0).then_inc(setup, 1)
            nc.vector.memset(hT, 0.0).then_inc(taken, 2)
            own(nc.vector.memset(cbm, 0.0))
            own(nc.vector.memset(reset[:], 1.0))
            settle()
            nc.vector.memset(reset[:, 0:SEQ:CH], 0.0)
            own(nc.vector.memset(reset[:, SEQ:T:DEC], 0.0))
            ve.wait_ge(vec_in, 16)
            for kt in range(KT):
                x = xin[kt // 4][:, kt % 4 * T:(kt % 4 + 1) * T]
                ve.wait_ge(x_in[min(kt // 4, 2)], 32 if kt >= 8 else 16)
                ts_op(x_hi[:, kt], x, V("mix_pre", kt), None, ALU.mult).then_inc(x_hi_w, 1)
                ve.wait_ge(x_hi_w, kt + 1)
                stt(x_lo[:, kt], x, V("mix_pre", kt), x_hi[:, kt].bitcast(F32), ALU.mult, ALU.subtract)\
                    .then_inc(x_split, 1)
            ve.wait_ge(masks_in, 16)
            own(nc.vector.tensor_copy(masks[:], masks_f))
            ve.wait_ge(root_ready, 1)
            nc.vector.reciprocal(rstd[:], rstd[:]).then_inc(rstd_ready, 1)
            ve.wait_ge(rstd_ready, 1)
            nc.vector.memset(pad[0][:, 0:SC - 1], 0.0)
            nc.vector.memset(pad[1][:, 0:SC - 1], 0.0).then_inc(pad_zero, 1)

            def take(tile, out):
                ve.wait_ge(units_done, 2 * tile + 2)
                tt_op(halves(out), proj(tile % 2), halves(rstd[:]), ALU.mult).then_inc(taken, 1)

            take(0, misc[:])

            def dt_steps(part):
                e, z, z2, p = dt_tmp
                if part == 0:
                    ve.wait_ge(taken, 3)
                    own(ts_op(dtT, dtT, V("dt_bias", rows=SH), None, ALU.add))
                    settle()
                    own(ts_op(z, dtT, 0.0, None, ALU.min))
                    settle()
                    stt(e, z, 2.0, dtT, ALU.mult, ALU.subtract).then_inc(dts, 1)
                if part == 1:
                    ve.wait_ge(dte, 1)
                    own(ts_op(z, e, 2.0, None, ALU.add))
                    settle()
                    own(nc.vector.reciprocal(z, z))
                    settle()
                    own(tt_op(z, z, e, ALU.mult))
                    settle()
                    own(tt_op(z2, z, z, ALU.mult))
                    settle()
                    own(ts_op(p, z2, 1.0 / 15, None, ALU.mult))
                if part == 2:
                    for n in (13, 11, 9, 7, 5, 3):
                        settle()
                        own(stt(p, p, 1.0 / n, z2, ALU.add, ALU.mult))
                if part == 3:
                    settle()
                    own(stt(p, p, 1.0, z, ALU.add, ALU.mult))
                    own(ts_op(dtT, dtT, 0.0, None, ALU.max))
                    settle()
                    own(stt(dtT, p, 2.0, dtT, ALU.mult, ALU.add))
                    settle()
                    own(ts_op(e, dtT, V("A_log", rows=SH), -1.0, ALU.mult, ALU.mult))
                    settle()
                    nc.vector.tensor_tensor_scan(cumT, reset[0:SH, :], e, 0.0, ALU.mult, ALU.add).then_inc(dt_ready, 1)
                    ve.wait_ge(dt_ready, 1)
                    c8 = cumT[:, SEQ:T].rearrange("p (b t) -> p b t", b=BATCHES)
                    nc.vector.tensor_copy(lastrow.rearrange("p (b t) -> p b t", b=BATCHES),
                                          c8[:, :, DEC - 1:DEC].broadcast_to([SH, BATCHES, DEC])).then_inc(dt_ready, 1)

            for n in range(XBC_TILES):
                q, o, r = pad[n % 2], conv_t[n % 2][:, 0:CONVW], (n + 1) % 2
                ve.wait_ge(units_done, 2 * n + 4)
                if n >= 2:
                    ve.wait_ge(sco, n - 1)
                tt_op(q[:, SC - 1:SC - 1 + SEQ].rearrange("p (n t) -> p n t", n=2), psum_proj[:, 2 * r:2 * r + 2, 0:256],
                      rstd[:, 0:SEQ].rearrange("p (n t) -> p n t", n=2), ALU.mult)
                tt_op(q[:, SC - 1 + SEQ:].rearrange("p (b t) -> p b t", b=BATCHES)[:, :, SC - 1:],
                      psum_proj[:, 2 * r + 1, 256:320].rearrange("p (b t) -> p b t", b=BATCHES),
                      rstd[:, SEQ:T].rearrange("p (b t) -> p b t", b=BATCHES), ALU.mult).then_inc(taken, 1)
                if n == 0:
                    dt_steps(0)
                ve.wait_ge(tap0, n + 1)
                for t in range(1, SC):
                    if t > 1:
                        settle()
                    i = stt(o, q[:, t:t + CONVW], V("conv_w", 4 * n + t), o, ALU.mult, ALU.add)
                    if t < SC - 1:
                        own(i)
                i.then_inc(taps, 1)
                if n in (2, 4, 6):
                    dt_steps(n // 2)

            def small(c, n, cols, mask):
                ve.wait_ge(small_mm, c + 1)
                nc.vector.copy_predicated(cbm[0:n, :, 0:cols], masks[0:n, mask:mask + 1, 0:cols].broadcast_to([n, SG, cols]),
                                          work[0:n, 2, 0:SG * cols].rearrange("p (g t) -> p g t", g=SG))
                last = work[0:n, 2, 256:256 + SH]
                tt_op(tok[0:n, c, 32:48], last, tok[0:n, c, 16:32], ALU.subtract)
                nc.vector.tensor_copy(tok[0:n, c, 48:64], last).then_inc(small_out, 1)

            def decayed_x(c, n):
                ve.wait_ge(wd_exp, c + 1)
                if c >= 1:
                    ve.wait_ge(h_mm, SG * c)
                tt_op(xw[0:n].rearrange("p (h d) -> p h d", h=SH), xdt[0:n, c].rearrange("p (h d) -> p h d", h=SH),
                      tok[0:n, c, 32:48].unsqueeze(2).broadcast_to([n, SH, SD]), ALU.mult).then_inc(xw_ready, 1)

            def exponents(k, w, cum_s, n):
                ve.wait_ge(bc_mm, k + 1)
                own(tt_op(w, cum_s.unsqueeze(2).broadcast_to(list(w.shape)),
                          work[0:n, 0:2, :].rearrange("p a (h t) -> p (a h) t", t=w.shape[-1]), ALU.subtract))
                settle()
                ts_op(w, w, 0.0, None, ALU.max).then_inc(D_ready, 1)

            def ssd_before(k):
                c, g = k // SG, k % SG
                w = W[:, 8 * g:8 * g + 8, :]
                if g == 0:
                    small(c, P, CH, MASK_TRI)
                if k >= 2:
                    ve.wait_ge(y_mm, k - 1)
                exponents(k, w, tok[:, c, 16 + 8 * g:24 + 8 * g], P)
                if g == 0:
                    decayed_x(c, P)
                ve.wait_ge(W_exp, k + 1)
                tt_op(w, w, cbm[:, g:g + 1, :].broadcast_to([P, 8, CH]), ALU.mult).then_inc(W_ready, 1)

            def add_y(y, j):
                own(tt_op(yt, work[:, 2, :], ecum, ALU.mult))
                settle()
                own(tt_op(yt, work[:, 3, :], yt, ALU.add))
                settle()
                tt_op(y, y, yt.rearrange("p (j t) -> p j t", j=j), ALU.add).then_inc(y_out, 1)

            def ssd_after(k):
                c, g = k // SG, k % SG
                ve.wait_ge(y_mm, k + 1)
                ve.wait_ge(e_exp, k + 1)
                add_y(XC[:, 4 * g:4 * g + 4, c * CH:(c + 1) * CH], 4)
                hh = hT[:, g * 512:(g + 1) * 512]
                own(tt_op(hh.rearrange("p (h d) -> p h d", h=8), hh.rearrange("p (h d) -> p h d", h=8),
                          tok[:, c, 48 + 8 * g:56 + 8 * g].unsqueeze(2).broadcast_to([P, 8, SD]), ALU.mult))
                settle()
                ve.wait_ge(h_mm, k + 1)
                tt_op(hh, work[:, g, :], hh, ALU.add).then_inc(h_ready, 1)

            def ssd_samples_before():
                ve.wait_ge(W_ready, SG * NC)
                own(nc.vector.memset(cbm[0:SMP], 0.0))
                settle()
                small(NC, SMP, SMP, MASK_TRI_S)
                exponents(SG * NC, W[0:SMP, :, 0:SMP], tok[0:SMP, NC, 16:32], SMP)
                decayed_x(NC, SMP)
                ve.wait_ge(W_exp, SG * NC + 1)
                for g in range(SG):
                    w = W[0:SMP, 8 * g:8 * g + 8, 0:SMP]
                    i = tt_op(w, w, cbm[0:SMP, g:g + 1, 0:SMP].broadcast_to([SMP, 8, SMP]), ALU.mult)
                i.then_inc(W_ready, 1)

            def ssd_samples_after():
                ve.wait_ge(y_mm, SG * NC + 1)
                ve.wait_ge(b_out, 5)
                for b in range(BATCHES):
                    i = ts_op(Bm[:, b].rearrange("p g n -> p (g n)"), B_tok[0:SMP, 4].rearrange("p g n -> p (g n)"),
                              V("batch", b, SMP), None, ALU.mult)
                i.then_inc(sm_ready, 1)

            el2 = decay[:].rearrange("p (j b) -> p j b", j=8)

            def ssd_batch(b):
                ve.wait_ge(hs_in[b % 2], 32 * (b // 2 + 1))
                ve.wait_ge(wd_exp, NC + 1)
                own(tt_op(hns[:, b % 2], hns[:, b % 2], el2[:, :, b:b + 1].broadcast_to([P, 8, SN]), ALU.mult))
                settle()
                ve.wait_ge(hs_mm, b + 1)
                tt_op(hns[:, b % 2], work[:, 0:2, :].rearrange("p a (j n) -> p (a j) n", j=4), hns[:, b % 2], ALU.add)\
                    .then_inc(hs_ready, 1)

            def gates():
                ve.wait_ge(gate_out, GH)
                own(ts_op(GB, GE, 0.0, None, ALU.min))
                settle()
                stt(GE2, GB, 2.0, GE, ALU.mult, ALU.subtract).then_inc(gate_sub, 1)
                ve.wait_ge(gate_ln, 1)
                own(tt_op(GE, GB, GE2, ALU.subtract))
                settle()
                for h in range(GH):
                    i = nc.vector.tensor_tensor_scan(GB[:, h * T:(h + 1) * T], reset[:], GE[:, h * T:(h + 1) * T],
                                                     0.0, ALU.mult, ALU.add)
                i.then_inc(b_ready, 1)

            def chunk_view(buf, m):
                if m <= DEC // 2:
                    v = buf.rearrange("p (n u m) -> p n u m", u=2, m=m)
                    return v[:, :, 0], v[:, :, 1]
                v = buf.rearrange("p (h t) -> p h t", h=GH)[:, :, 0:SEQ].rearrange("p h (n u m) -> p h n u m", u=2, m=m)
                return v[:, :, :, 0], v[:, :, :, 1]

            def take_att(s):
                for h in range(GH):
                    ve.wait_ge(att_mm, att_base(s) + h + 1)
                    nc.vector.copy_predicated(att[:, h * NC:(h + 1) * NC, :], masks[:, s:s + 1, :].broadcast_to([P, NC, P]),
                                              work[:, h, :].rearrange("p (c t) -> p c t", c=NC)).then_inc(att_out, 1)
                if s in SAMPLE_STEPS:
                    ve.wait_ge(att_mm, att_base(s + 1))
                    nc.vector.copy_predicated(att_s, masks[0:SMP, s:s + 1, 0:SMP].broadcast_to([SMP, GH, SMP]),
                                              work[0:SMP, 0, 0:GH * SMP].rearrange("p (h t) -> p h t", h=GH))\
                        .then_inc(att_out, 1)

            def operands(s):
                m = LEVELS[s - 1]
                buf = GE if s % 2 else GE2
                (k_out, q_out), (k_b, q_b) = chunk_view(buf, m), chunk_view(GB, m)
                ref = k_b[..., m - 1:m].broadcast_to(list(k_b.shape))
                if s >= 3:
                    ve.wait_ge(att_mm, att_base(s - 1))
                tt_op(k_out, ref, k_b, ALU.subtract)
                tt_op(q_out, q_b, ref, ALU.subtract).then_inc(sub_ready, 1)
                ve.wait_ge(exp_ready, s)
                tt_op(k_out, k_out, chunk_view(GKK, m)[0], ALU.mult)
                tt_op(q_out, q_out, chunk_view(GQ, m)[1], ALU.mult).then_inc(pq_ready, 1)

            def decay_to_ends():
                ve.wait_ge(att_mm, att_base(8))
                for lo, hi, n in ((0, SEQ, CH), (SEQ, T, DEC)):
                    def v(buf):
                        return buf.rearrange("p (h t) -> p h t", h=GH)[:, :, lo:hi].rearrange("p h (c t) -> p h c t", t=n)
                    b = v(GB)
                    i = tt_op(v(GE), b[..., n - 1:n].broadcast_to(list(b.shape)), b, ALU.subtract)
                i.then_inc(sub_ready, 1)
                ve.wait_ge(exp_ready, 8)
                tt_op(GE, GE, GKK, ALU.mult).then_inc(kdT_ready, 1)
                ve.wait_ge(exp_ready, 9)
                e = GE2.rearrange("p (h t) -> p h t", h=GH)
                tt_op(GQ, GQ, GE2, ALU.mult)
                nc.vector.tensor_copy(gdecay[:, :, 0:NC], e[:, :, CH - 1:SEQ:CH])
                nc.vector.tensor_copy(gdecay[:, :, NC:NC + BATCHES], e[:, :, SEQ + DEC - 1:T:DEC]).then_inc(qd_ready, 1)
                ve.wait_ge(qd_ready, 1)

            def gla_chunk(c):
                ve.wait_ge(S_mm, c + 1)
                if c == 0:
                    ve.wait_ge(sconv_st, 16)
                else:
                    ve.wait_ge(S_ready, c)
                for h in range(GH):
                    inc = work[:, 2 + h // 2, h % 2 * GV:(h % 2 + 1) * GV]
                    if c == 0:
                        i = nc.vector.tensor_copy(S[:, h, :], inc)
                    else:
                        i = stt(S[:, h, :], S[:, h, :], gdecay[:, h, c:c + 1], inc, ALU.mult, ALU.add)
                i.then_inc(S_ready, 1)

            def masked_keys(b):
                if b >= 2:
                    ve.wait_ge(s1_mm, b - 1)
                ts_op(kd_m[:, b % 2].rearrange("p h k -> p (h k)"), kd_tok[0:SMP, 4, :], V("batch", b, SMP), None, ALU.mult)\
                    .then_inc(kdm_ready, 1)

            def gla_batch(b):
                ve.wait_ge(s1_mm, b + 1)
                ve.wait_ge(s0_in[b % 2], 16 * (b // 2 + 1))
                for h in range(GH):
                    s = s0ring[:, b % 2, h, :]
                    i = stt(s, s, gdecay[:, h, NC + b:NC + b + 1], work[:, 2 + h // 2, h % 2 * GV:(h % 2 + 1) * GV],
                            ALU.mult, ALU.add)
                i.then_inc(s1_ready, 1)
                if b + 2 < BATCHES:
                    masked_keys(b + 2)

            def gap(m):
                if m == 0:
                    ve.wait_ge(dttr, 1)
                    nc.vector.tensor_copy(tok[:, 0:4, 0:32], work[:, 3, 0:128].rearrange("p (t c) -> p t c", t=4))
                    nc.vector.tensor_copy(tok[0:SMP, 4, 0:32], work[0:SMP, 3, 128:160]).then_inc(dtt_out, 1)
                    ve.wait_ge(dtt_out, 1)
                if m < 5:
                    n = P if m < 4 else SMP
                    ve.wait_ge(xtr, m + 1)
                    tt_op(xdt[0:n, m].rearrange("p (h d) -> p h d", h=SH),
                          work[0:n, 0:2, :].rearrange("p a (h d) -> p (a h) d", d=SD),
                          tok[0:n, m, 0:SH].unsqueeze(2).broadcast_to([n, SH, SD]), ALU.mult).then_inc(xdt_out, 1)
                if m == 4:
                    for j in range(8):
                        i = ts_op(XC[:, j], XC[:, j], V("ssd_D", j), None, ALU.mult)
                    own(i)
                    ve.wait_ge(xdt_out, 5)
                    settle()
                if GAP_STEP <= m < GAP_SMP:
                    (ssd_after if (m - GAP_STEP) % 2 else ssd_before)((m - GAP_STEP) // 2)
                if m == GAP_SMP:
                    ssd_samples_before()
                if m == GAP_SMP + 1:
                    ssd_samples_after()
                if GAP_SMP + 2 <= m < GAP_SMP + 2 + BATCHES:
                    ssd_batch(m - GAP_SMP - 2)
                if m == GAP_SMP + 1 + BATCHES:
                    add_y(XC[:, 0:8, SEQ:T], 8)
                    ve.wait_ge(y_out, SG * NC + 1)
                if m == GAP_YNORM - 2:
                    ve.wait_ge(zsilu, 1)
                    tt_op(XC[:, 0:8], XC[:, 0:8], zT, ALU.mult).then_inc(yz, 1)
                if m in (GAP_YNORM, GAP_YNORM + 2):
                    g = (m - GAP_YNORM) // 2
                    ve.wait_ge(yroot, g + 1)
                    own(nc.vector.reciprocal(zT[:, g], zT[:, g]))
                    settle()
                    for j in range(4 * g, 4 * g + 4):
                        stt(XC[:, j], XC[:, j], V("ssd_norm", j), zT[:, j // 4], ALU.mult, ALU.mult).then_inc(ymix, 1)
                if m == GAP_YNORM + 3:
                    for j in range(4, 8):
                        ve.wait_ge(yhi, j + 1)
                        tt_op(XC[:, j], XC[:, j], ysq[:, j], ALU.subtract).then_inc(ylo, 1)
                if m == GAP_GATE:
                    gates()
                    ve.wait_ge(y_kept, 16)
                    nc.vector.memset(att, 0.0)
                    own(nc.vector.memset(att_s, 0.0))
                    settle()
                if GAP_ATT <= m < GAP_ATT + 16 and (m - GAP_ATT) % 2 == 0:
                    s = (m - GAP_ATT) // 2
                    if s == 0:
                        ve.wait_ge(b_ready, 1)
                        ve.wait_ge(qk_in, 32)
                    take_att(s)
                    if s < 7:
                        operands(s + 1)
                    else:
                        decay_to_ends()
                if GAP_CHUNK <= m < GAP_CHUNK + NC:
                    gla_chunk(m - GAP_CHUNK)
                if m == GAP_GSMP - 1:
                    ve.wait_ge(o_mm, NC)
                    ve.wait_ge(kd_out, 5)
                    masked_keys(0)
                    masked_keys(1)
                if m >= GAP_GSMP:
                    gla_batch(m - GAP_GSMP)

            for n in range(BESIDE):
                ve.wait_ge(units_done, 2 * (N_TILE0 + n) + 2)
                if V_N + 2 <= n < V_N + 10:
                    ve.wait_ge(v_tr, n - V_N - 1)
                elif n >= 2:
                    ve.wait_ge(spilled[n % 2], 16 * (n // 2 if n < V_N + 2 else n // 2 - 4))
                out, p = halves(stage[:, n % 2]), proj((N_TILE0 + n) % 2)
                if Q_N <= n < Q_N + GH:
                    i = stt(out, p, GK ** -0.5, halves(rstd[:]), ALU.mult, ALU.mult)
                else:
                    i = tt_op(out, p, halves(rstd[:]), ALU.mult)
                i.then_inc(taken, 1)
                gap(2 * n)
                if n < BESIDE - 1:
                    gap(2 * n + 1)
            def late(d):
                if d < 6:
                    gla_batch(d + 2)
                if 7 <= d < 7 + GH:
                    h = d - 7
                    ve.wait_ge(gsq, h + 1)
                    if h >= 1:
                        ve.wait_ge(gsum, h)
                    tt_op(gsum2, GE[:, 0:T], GE[:, T:2 * T], ALU.add).then_inc(gss, 1)
                if 8 <= d < 8 + GH:
                    h = d - 8
                    ve.wait_ge(groot, h + 1)
                    r = GQ[:, h * T:(h + 1) * T]
                    nc.vector.reciprocal(r, r).then_inc(grs, 1)
                    ve.wait_ge(grs, h + 1)
                    for vh in range(2):
                        o = oT[:, 2 * h + vh]
                        i = stt(o, o, V("gla_norm", vh), r, ALU.mult, ALU.mult)
                    own(i)
                    settle()
                    ve.wait_ge(gsilu, 1)
                    o = oT[:, 2 * h:2 * h + 2]
                    tt_op(o, o, gT[:, 2 * h:2 * h + 2], ALU.mult).then_inc(gy, 1)
                if d == 12:
                    for h in range(GH):
                        ve.wait_ge(ghi, h + 1)
                        tt_op(gla_lo(2 * h, 2), oT[:, 2 * h:2 * h + 2], gla_hi(2 * h, 2).bitcast(F32), ALU.subtract)\
                            .then_inc(mix_in, 1)

            late(-1)
            for d in range(KT):
                ve.wait_ge(units_done, OUT_UNIT0 + d + 1)
                nc.vector.tensor_copy(halves(mix[:, d]), proj((1 + d) % 2)).then_inc(taken, 1)
                late(d)
            ve.wait_ge(gla_p_out, 16)
            nc.vector.memset(sqsum, 0.0).then_inc(sq_free, 2)
            ve.wait_ge(taken, OUT_TILE0 + KT + 2)

            def add_square(i, j):
                ve.wait_ge(msq, 4 * i + j + 1)
                ve.wait_ge(sq_free, 4 * i + j + 2)
                tt_op(sqsum, sqsum, sq[j % 2], ALU.add).then_inc(sq_free, 1)

            with ve.Fori(0, KT // 4) as i:
                for j in range(4):
                    ve.wait_ge(units_done, 4 * i + j + OUT_UNIT0 + KT + 1)
                    o = mix[:, bass.ds(4 * i + j, 1), :].rearrange("p o (n t) -> p (o n) t", n=2)
                    tt_op(o, proj((1 + j) % 2), o, ALU.add).then_inc(taken, 1)
                    if j:
                        add_square(i, j - 1)
                add_square(i, 3)
            ve.wait_ge(mroot, 1)
            own(nc.vector.reciprocal(rstd[:], rstd[:]))
            settle()

            def h_lo(kt):
                ve.wait_ge(h_hi, kt + 1)
                stt(x_lo[:, kt], mixT[:, kt], V("ffn_pre", kt), x_hi[:, kt].bitcast(F32), ALU.mult, ALU.subtract)\
                    .then_inc(h_split, 1)

            for kt in range(KT):
                stt(mixT[:, kt], mix[:, (kt + 8) % KT], V("mix_post", kt), rstd[:], ALU.mult, ALU.mult).then_inc(h_m, 1)
                if kt >= 2:
                    h_lo(kt - 2)
            h_lo(KT - 2)
            h_lo(KT - 1)
            nc.vector.memset(fpad[0][:, 0:FC - 1], 0.0)
            nc.vector.memset(fpad[1][:, 0:FC - 1], 0.0).then_inc(fpad_zero, 1)
            ve.wait_ge(mroot, 2)
            own(nc.vector.reciprocal(rstd[:], rstd[:]))
            settle()

            def take_up(t, j, unit, first=False):
                pd, r = fpad[j % 2], (1 + j) % 2
                ve.wait_ge(units_done, unit + 2 * j + 2)
                if not (first and j < 2):
                    ve.wait_ge(f_padout, t - 1)
                tt_op(pd[:, FC - 1:FC - 1 + SEQ].rearrange("p (n t) -> p n t", n=2), psum_proj[:, 2 * r:2 * r + 2, 0:256],
                      rstd[:, 0:SEQ].rearrange("p (n t) -> p n t", n=2), ALU.mult)
                tt_op(pd[:, FC - 1 + SEQ:].rearrange("p (b t) -> p b t", b=BATCHES)[:, :, FC - 1:],
                      psum_proj[:, 2 * r + 1, 256:320].rearrange("p (b t) -> p b t", b=BATCHES),
                      rstd[:, SEQ:T].rearrange("p (b t) -> p b t", b=BATCHES), ALU.mult).then_inc(taken, 1)

            def taps_of(t, j, q):
                pd, o = fpad[j % 2], ftap[j % 2][:, 0:FCONVW]
                ve.wait_ge(f_tap0, t + 1)
                stt(o, pd[:, 1:1 + FCONVW], fc[q][:, 4 * j + 1:4 * j + 2], o, ALU.mult, ALU.add).then_inc(f_tap1, 1)
                ve.wait_ge(f_tap1, t + 1)
                stt(o, pd[:, 2:2 + FCONVW], fc[q][:, 4 * j + 2:4 * j + 3], o, ALU.mult, ALU.add).then_inc(f_taps, 1)

            def gate_product(pair):
                ve.wait_ge(f_silu, pair + 1)
                ve.wait_ge(f_taps, 2 * pair + 2)
                tt_op(fgate[:, 0:SEQ], fgate[:, 0:SEQ], ftap[1][:, 0:SEQ], ALU.mult)
                g8 = fgate[:, SEQ:T].rearrange("p (b t) -> p b t", b=BATCHES)
                tt_op(g8, g8, ftap[1][:, SEQ + FC - 1:FPADW].rearrange("p (b t) -> p b t", b=BATCHES)[:, :, 0:DEC],
                      ALU.mult).then_inc(f_prod, 1)

            def gate_lo(pair, q, i):
                ve.wait_ge(f_hi, pair + 1)
                tt_op(g_lo[:, q, i], fgate, g_hi[:, q, i].bitcast(F32), ALU.subtract).then_inc(act_ready, 1)

            def take_down(d, unit, count):
                if d % 4 == 3:
                    ve.wait_ge(units_done, unit + d // 4 + 1)
                else:
                    ve.wait_ge(down_mm, count + 3 * (d // 4) + d % 4 + 1)
                a = halves(acc[:, d])
                tt_op(a, proj((1 + d) % 2), a, ALU.add).then_inc(taken, 1)

            def block_up(blk, q, unit, first=False):
                t = 4 * blk
                take_up(t, 0, unit, first)
                taps_of(t, 0, q)
                take_up(t + 1, 1, unit, first)
                taps_of(t + 1, 1, q)
                gate_product(2 * blk)
                gate_lo(2 * blk, q, 0)
                take_up(t + 2, 2, unit)
                taps_of(t + 2, 2, q)
                take_up(t + 3, 3, unit)

            def block_end(blk, q, step):
                if step == 0:
                    taps_of(4 * blk + 3, 3, q)
                elif step == 1:
                    gate_product(2 * blk + 1)
                else:
                    gate_lo(2 * blk + 1, q, 1)

            def block(blk, q, unit, tile):
                block_up(blk, q, unit)
                ve.wait_ge(taken, tile + 4 + 2)
                for d in range(KT):
                    take_down(d, unit + 8, 12 * blk - 12)
                    if d in (1, 4, 7):
                        block_end(blk, q, (1, 4, 7).index(d))

            block_up(0, 0, FFN_UNIT0, first=True)
            for s in range(3):
                block_end(0, 0, s)
            ve.wait_ge(h_st, 16)
            nc.vector.memset(acc.rearrange("p n t -> p (n t)"), 0.0).then_inc(acc_zero, 1)
            ve.wait_ge(acc_zero, 1)
            with ve.Fori(0, (BLOCKS - 2) // 2) as i:
                for q in (1, 0):
                    b = 1 if q else 2
                    block(2 * i + b, q, 24 * i + FFN_UNIT0 - 4 + 12 * b, 40 * i + FFN_TILE0 - 16 + 20 * b)
            b = BLOCKS - 1
            unit, tile = FFN_UNIT0 - 4 + 12 * b, FFN_TILE0 - 16 + 20 * b
            block(b, 1, unit, tile)
            ve.wait_ge(taken, tile + 20 + 2)
            for d in range(KT):
                take_down(d, unit + 12, 12 * b)
            ve.wait_ge(mroot, 3)
            own(nc.vector.reciprocal(rstd[:], rstd[:]))
            settle()
            ve.wait_ge(taken, tile + 36 + 2)
            ve.wait_ge(h_back, 16)
            for kt in range(KT):
                stt(acc[:, kt], acc[:, kt], V("ffn_post", kt), rstd[:], ALU.mult, ALU.mult).then_inc(y_m, 1)
                if kt in VE_ADDS:
                    ve.wait_ge(y_m, kt + 1)
                    tt_op(acc[:, kt], acc[:, kt], x_hi[:, kt].bitcast(F32), ALU.add).then_inc(y_w, 1)


def _tiles(rows):
    return np.swapaxes(rows.reshape((-1, P) + rows.shape[1:]), 0, 1)


def _weights(w_in, w_out, f_in, f_out):
    cut = np.cumsum([0, GH * GK, GH * GK, GH * GV, GH * GV, RANK, SH * SD, SH * SD + 2 * SG * SN, SH])
    q, k, v, g, lr, z, xbc, dt = (np.arange(cut[i], cut[i + 1]) for i in range(8))
    cols = np.concatenate([dt, q[:16], lr, q[:80], xbc, z, q, k, g[:4 * P], v, g[4 * P:]])

    def by_tile(w):
        return w.reshape(2, 8, P, -1, P).transpose(3, 0, 2, 1, 4).reshape(-1, P, 8, P)

    up = by_tile(f_in).reshape(2, BLOCKS, 4, P, 8, P)
    up = up.reshape(2, BLOCKS, 2, 2, P, 8, P).transpose(1, 2, 0, 3, 4, 5, 6).reshape(BLOCKS, 8, P, 8, P)
    down = f_out.reshape(BLOCKS, 2, P, 4, 4, P).transpose(0, 3, 2, 4, 1, 5).reshape(BLOCKS, 4, P, 8, P)
    ffn = [up[0]]
    for b in range(1, BLOCKS):
        ffn += [up[b], down[b - 1]]
    out = w_out.reshape(2, 8, P, KT, P).transpose(0, 3, 2, 1, 4)[::-1]
    out = np.concatenate([out[:, 8:], out[:, :8]], axis=1).reshape(-1, P, 8, P)
    return np.concatenate([by_tile(w_in[:, cols]), out] + ffn + [down[BLOCKS - 1]])


def _masks():
    s, t = np.arange(P)[:, None], np.arange(P)[None, :]
    levels = [(s // (2 * m) == t // (2 * m)) & (s % (2 * m) < m) & (t % (2 * m) >= m) for m in LEVELS]
    return np.stack([s == t] + levels + [s <= t, (s <= t) & (s // DEC == t // DEC)], axis=1).astype(np.float32)


def _ffn_channels(a):
    a = a.reshape((2, BLOCKS, 2, P) + a.shape[1:])
    return np.moveaxis(np.swapaxes(a, 0, 1).swapaxes(1, 2).reshape((BLOCKS, 4, P) + a.shape[4:]), 2, 0)


def _ffn_channels_back(a):
    a = np.moveaxis(a, 0, 2).reshape((BLOCKS, 2, 2, P) + a.shape[3:])
    return np.swapaxes(a, 1, 2).swapaxes(0, 1).reshape((2 * F,) + a.shape[4:])


def kernel(**inputs):
    from concourse import bacc as _bacc
    from concourse.bass_utils import run_bass_kernel_spmd as _run

    a = {k: np.asarray(v) for k, v in inputs.items()}
    x = np.concatenate([a["x_prompt"].reshape(SEQ, D), a["x_sample"].reshape(SMP, D)])
    f32 = x.dtype
    col = {k: a[k][0].reshape(-1, P).T for k in ("norm_mix_pre", "norm_mix_post", "norm_ffn_pre", "norm_ffn_post",
                                                 "gla_norm", "ssd_conv_b", "ssd_norm")}
    pad_rows = lambda v: np.concatenate([v, np.zeros(P - len(v), f32)])[:, None]
    batch_mask = np.zeros((P, BATCHES), f32)
    batch_mask[np.arange(SMP), np.arange(SMP) // DEC] = 1
    vecs = np.concatenate([
        col["norm_mix_pre"], col["norm_mix_post"], col["norm_ffn_pre"], col["norm_ffn_post"],
        a["gla_b_gate"][0].reshape(-1, P).T, col["gla_norm"],
        _tiles(a["ssd_conv_w"][0].T).reshape(P, -1), col["ssd_conv_b"],
        np.repeat(a["ssd_D"][0], SD).reshape(-1, P).T, col["ssd_norm"],
        pad_rows(a["ssd_dt_bias"][0]), pad_rows(a["ssd_A_log"][0]), np.full((P, 1), EPS, f32), batch_mask], axis=1)
    fvec = np.concatenate([a["ffn_conv_w"][0], a["ffn_conv_b"]]).T
    ssd = a["state_ssd"][0].reshape(BATCHES, SH * SD, SN)
    arrays = [
        ("xT", _tiles(x.T).reshape(P, 4, 4 * T).swapaxes(0, 1)),
        ("weights", _weights(a["w_in"][0], a["w_out"][0], a["ffn_w_in"][0], a["ffn_w_out"][0])),
        ("vecs", vecs),
        ("ident", np.eye(P, dtype=f32)),
        ("masks", _masks()),
        ("gate2", a["gla_w_gate2"][0]),
        ("sconv_in", _tiles(a["state_ssd_conv"][0].transpose(2, 0, 1))),
        ("fconv_in", _ffn_channels(a["state_ffn_conv"][0].transpose(2, 0, 1)).reshape(P, BLOCKS, -1)),
        ("fvec", _ffn_channels(fvec).reshape(P, BLOCKS, -1)),
        ("gla_in", a["state_gla"][0].transpose(2, 0, 1, 3).reshape(GK, -1, GV)),
        ("ssdT_in", ssd.transpose(2, 0, 1)),
        ("ssd_in", ssd.reshape(BATCHES, 8, P, SN).transpose(2, 0, 1, 3)),
    ]
    outs = [("yT", (4, P, 4, T)), ("gla_p", (P, GH, GV)), ("ssd_p", (SN, SH * SD)), ("sconv_out", (P, XBC_TILES, 27)),
            ("fconv_out", (P, BLOCKS, 72)), ("gla_s", (P, BATCHES * GH, GV)), ("ssd_s", (P, BATCHES, 8, SN))]
    nc = _bacc.Bacc("TRN2", target_bir_lowering=False, num_devices=1)
    fed, args = {}, []
    for name, v in arrays:
        v = np.ascontiguousarray(v)
        fed[f"in_{name}_dram"] = v
        args.append(nc.dram_tensor(f"in_{name}_dram", v.shape, mybir.dt.from_np(v.dtype), kind="ExternalInput").ap())
    for name, shape in outs:
        args.append(nc.dram_tensor(f"out_{name}_dram", shape, F32, kind="ExternalOutput").ap())
    build(nc, *args)
    r = _run(nc, [fed], core_ids=[0])
    o = {name: np.asarray(r.results[0][f"out_{name}_dram"]).reshape(shape) for name, shape in outs}
    y = o["yT"].swapaxes(0, 1).reshape(P, KT, T).transpose(2, 1, 0).reshape(T, D)
    sconv = o["sconv_out"].transpose(2, 1, 0).reshape(27, -1)
    fconv = _ffn_channels_back(o["fconv_out"].reshape(P, BLOCKS, 4, 18)).T
    return (y[:SEQ].reshape(1, SEQ, D), y[SEQ:].reshape(BATCHES, DEC, D),
            o["gla_p"].transpose(1, 0, 2).reshape(1, 1, GH, GK, GV),
            o["ssd_p"].T.reshape(1, 1, SH, SD, SN),
            sconv[:SC - 1].reshape(1, 1, SC - 1, -1),
            fconv[:FC - 1].reshape(1, 1, FC - 1, -1),
            o["gla_s"].reshape(GK, BATCHES, GH, GV).transpose(1, 2, 0, 3)[None],
            o["ssd_s"].transpose(1, 2, 0, 3).reshape(1, BATCHES, SH, SD, SN),
            sconv[SC - 1:].reshape(1, BATCHES, SC - 1, -1),
            fconv[FC - 1:].reshape(1, BATCHES, FC - 1, -1))
```
